# Optimizing a Trainium2 kernel written in Bass

```python
import jax, jax.numpy as jnp
from jax import lax
import numpy as np

'''Hybrid diffusion / flow-matching backbone layer stack.

Each layer: adaLN-modulated input -> ONE combined input projection whose columns are
partitioned into two parallel head groups (multi-scale pooling mixer, 4 channel groups;
grouped-query attention with per-head q/k RMSNorm and 2-D axial rotary over the latent grid)
-> concatenation over head groups -> ONE output projection -> gated DeepNorm post-LayerNorm;
then adaLN-modulated DeepSeek-V3 style MoE (sigmoid, group-limited top-k routing + shared
expert) -> gated DeepNorm post-LayerNorm. Context tokens form an un-noised prefix through the
SAME weights, modulated by c_ctx, reading only context tokens; latent queries attend in one
softmax to all latent keys plus all context keys.

Inputs: x (BATCH, SEQ, D_MODEL), c (BATCH, D_MODEL), ctx (BATCH, CTX_LEN, D_MODEL),
c_ctx (D_MODEL,), per-layer weights stacked on a leading DEPTH axis.
Output: latent stream (BATCH, SEQ, D_MODEL).
'''

D_MODEL = 1024
BATCH = 1
SEQ = 512
DEPTH = 1

CTX_LEN = 256
GRID_W = 64
D_MIX = D_MODEL
POOL_WIDTH = D_MIX // 4
POOL_WINDOWS = (2, 4, 8, 16)
POOL_GROUP = POOL_WIDTH // len(POOL_WINDOWS)
ATTN_WIDTH = D_MIX - POOL_WIDTH
HEAD_DIM = 64
N_HEADS = ATTN_WIDTH // HEAD_DIM
N_KV_HEADS = 4
GQA_GROUP = N_HEADS // N_KV_HEADS
KV_WIDTH = N_KV_HEADS * HEAD_DIM
PROJ_WIDTH = POOL_WIDTH + ATTN_WIDTH + 2 * KV_WIDTH
Q_BLOCK = 128
ROPE_THETA = 10000.0
AXIS_DIM = HEAD_DIM // 2
N_EXPERTS = 64
TOP_K = 8
N_GROUPS = 8
TOPK_GROUPS = 4
EXPERT_FF = 256
SHARED_FF = 256
ROUTED_SCALE = 2.5
EXPERT_BLOCK = 256
ALPHA = (2.0 * DEPTH) ** 0.25
BETA = (8.0 * DEPTH) ** -0.25
LN_EPS = 1e-5
RMS_EPS = 1e-6

kernel_name = 'hybrid_pool_gqa_moe_dit_layer'

def layer_norm(x, g, b):
    xf = x.astype(jnp.float32)
    mu = jnp.mean(xf, axis=-1, keepdims=True)
    var = jnp.mean(jnp.square(xf - mu), axis=-1, keepdims=True)
    return ((xf - mu) * lax.rsqrt(var + LN_EPS) * g + b).astype(x.dtype)

def head_rms_norm(x, g):
    xf = x.astype(jnp.float32)
    return (xf * lax.rsqrt(jnp.mean(jnp.square(xf), axis=-1, keepdims=True) + RMS_EPS) * g).astype(x.dtype)

def axial_rope_tables(rows):
    inv_freq = ROPE_THETA ** (-jnp.arange(0, AXIS_DIM, 2, dtype=jnp.float32) / AXIS_DIM)
    row = jnp.repeat(jnp.arange(rows, dtype=jnp.float32), GRID_W)
    col = jnp.tile(jnp.arange(GRID_W, dtype=jnp.float32), rows)
    ang = jnp.concatenate([row[:, None] * inv_freq, col[:, None] * inv_freq], axis=-1)
    return jnp.cos(ang), jnp.sin(ang)

def apply_rope(x, cos, sin):
    shape = x.shape
    xf = x.astype(jnp.float32).reshape(shape[:-1] + (HEAD_DIM // 2, 2))
    bshape = (1, shape[1]) + (1,) * (x.ndim - 3) + (HEAD_DIM // 2,)
    c = cos.reshape(bshape)
    s = sin.reshape(bshape)
    x0, x1 = xf[..., 0], xf[..., 1]
    out = jnp.stack([x0 * c - x1 * s, x0 * s + x1 * c], axis=-1)
    return out.reshape(shape).astype(x.dtype)

def split_projection(p):
    B_, L, _ = p.shape
    o1 = POOL_WIDTH
    o2 = o1 + ATTN_WIDTH
    o3 = o2 + KV_WIDTH
    u = p[..., :o1]
    q = p[..., o1:o2].reshape(B_, L, N_KV_HEADS, GQA_GROUP, HEAD_DIM)
    k = p[..., o2:o3].reshape(B_, L, N_KV_HEADS, HEAD_DIM)
    v = p[..., o3:].reshape(B_, L, N_KV_HEADS, HEAD_DIM)
    return u, q, k, v

def pool_mixer(u, pool_w, pool_scale):
    B_, L, _ = u.shape
    uf = u.astype(jnp.float32)
    cs = jnp.concatenate([jnp.zeros((B_, 1, POOL_WIDTH), jnp.float32), jnp.cumsum(uf, axis=1)], axis=1)
    t = jnp.arange(L)
    parts = []
    for gi, win in enumerate(POOL_WINDOWS):
        lo = jnp.clip(t - win // 2, 0, L)
        hi = jnp.clip(t + win - win // 2, 0, L)
        sl = slice(gi * POOL_GROUP, (gi + 1) * POOL_GROUP)
        window_mean = (cs[:, hi, sl] - cs[:, lo, sl]) / (hi - lo).astype(jnp.float32)[None, :, None]
        parts.append(window_mean - uf[:, :, sl])
    d = jnp.stack(parts, axis=2).astype(u.dtype)
    y = jnp.einsum('blgc,gcd->blgd', d, pool_w).reshape(B_, L, POOL_WIDTH)
    return y * pool_scale

def attend(q, k, v):
    s = jnp.einsum('bqhgd,bkhd->bhgqk', q, k, preferred_element_type=jnp.float32) * (HEAD_DIM ** -0.5)
    p = jax.nn.softmax(s, axis=-1).astype(v.dtype)
    return jnp.einsum('bhgqk,bkhd->bqhgd', p, v)

def attend_latent_blocks(q, k_all, v_all):
    B_, L = q.shape[:2]
    nb = L // Q_BLOCK
    qb = jnp.moveaxis(q.reshape((B_, nb, Q_BLOCK) + q.shape[2:]), 1, 0)
    o = lax.map(lambda qblk: attend(qblk, k_all, v_all), qb)
    return jnp.moveaxis(o, 0, 1).reshape(B_, L, ATTN_WIDTH)

def moe_ffn(h, w_router, router_bias, w_gate, w_up, w_down, ws_gate, ws_up, ws_down):
    B_, L, D = h.shape
    xt = h.reshape(-1, D)
    T = xt.shape[0]
    scores = jax.nn.sigmoid(jnp.dot(xt.astype(jnp.float32), w_router.astype(jnp.float32)))
    sel = scores + router_bias.astype(jnp.float32)
    grp = sel.reshape(T, N_GROUPS, N_EXPERTS // N_GROUPS)
    grp_score = lax.top_k(grp, 2)[0].sum(-1)
    _, top_groups = lax.top_k(grp_score, TOPK_GROUPS)
    group_mask = jnp.any(top_groups[:, :, None] == jnp.arange(N_GROUPS)[None, None, :], axis=1)
    expert_mask = jnp.repeat(group_mask, N_EXPERTS // N_GROUPS, axis=1)
    sel = jnp.where(expert_mask, sel, -jnp.inf)
    _, idx = lax.top_k(sel, TOP_K)
    wts = jnp.take_along_axis(scores, idx, axis=1)
    wts = wts / jnp.sum(wts, axis=-1, keepdims=True) * ROUTED_SCALE
    A = T * TOP_K
    e_flat = idx.reshape(-1)
    order = jnp.argsort(e_flat)
    e_sorted = e_flat[order]
    tok_sorted = (order // TOP_K).astype(jnp.int32)
    w_sorted = wts.reshape(-1)[order]
    counts = jnp.bincount(e_flat, length=N_EXPERTS)
    start = jnp.cumsum(counts) - counts
    padded = ((counts + EXPERT_BLOCK - 1) // EXPERT_BLOCK) * EXPERT_BLOCK
    pad_end = jnp.cumsum(padded)
    pad_start = pad_end - padded
    dest = pad_start[e_sorted] + (jnp.arange(A) - start[e_sorted])
    P = A + N_EXPERTS * EXPERT_BLOCK
    n_blocks = P // EXPERT_BLOCK
    row_tok = jnp.full((P,), T, jnp.int32).at[dest].set(tok_sorted)
    row_w = jnp.zeros((P,), jnp.float32).at[dest].set(w_sorted)
    block_expert = jnp.minimum(jnp.searchsorted(pad_end, jnp.arange(n_blocks) * EXPERT_BLOCK, side='right'), N_EXPERTS - 1)
    xpad = jnp.concatenate([xt, jnp.zeros((1, D), xt.dtype)], axis=0)

    def expert_block(out, blk):
        tok, wr, e = blk
        rows = xpad[tok]
        y = (jax.nn.silu(rows @ w_gate[e]) * (rows @ w_up[e])) @ w_down[e]
        return out.at[tok].add((y * wr[:, None]).astype(out.dtype)), None

    routed, _ = lax.scan(expert_block, jnp.zeros((T + 1, D), xt.dtype),
                         (row_tok.reshape(n_blocks, EXPERT_BLOCK), row_w.reshape(n_blocks, EXPERT_BLOCK), block_expert))
    shared = (jax.nn.silu(xt @ ws_gate) * (xt @ ws_up)) @ ws_down
    return (routed[:T] + shared).reshape(B_, L, D)

def setup_inputs(seed: int = 0) -> dict:
    key = jax.random.key(seed)
    ks = jax.random.split(key, 26)

    def nrm(k, shape, scale):
        return scale * jax.random.normal(k, shape, jnp.float32)

    Dm = D_MODEL
    return {
        'x': nrm(ks[0], (BATCH, SEQ, Dm), 1.0),
        'c': nrm(ks[1], (BATCH, Dm), 1.0),
        'ctx': nrm(ks[2], (BATCH, CTX_LEN, Dm), 1.0),
        'c_ctx': nrm(ks[3], (Dm,), 1.0),
        'w_mod': nrm(ks[4], (DEPTH, Dm, 6 * Dm), 0.5 * Dm ** -0.5),
        'b_mod': nrm(ks[5], (DEPTH, 6 * Dm), 0.02),
        'w_in': nrm(ks[6], (DEPTH, Dm, PROJ_WIDTH), Dm ** -0.5),
        'q_norm': 1.0 + nrm(ks[7], (DEPTH, HEAD_DIM), 0.05),
        'k_norm': 1.0 + nrm(ks[8], (DEPTH, HEAD_DIM), 0.05),
        'pool_w': nrm(ks[9], (DEPTH, len(POOL_WINDOWS), POOL_GROUP, POOL_GROUP), POOL_GROUP ** -0.5),
        'pool_scale': 1.0 + nrm(ks[10], (DEPTH, POOL_WIDTH), 0.05),
        'w_out': nrm(ks[11], (DEPTH, D_MIX, Dm), BETA * D_MIX ** -0.5),
        'ln1_g': 1.0 + nrm(ks[12], (DEPTH, Dm), 0.05),
        'ln1_b': nrm(ks[13], (DEPTH, Dm), 0.02),
        'w_router': nrm(ks[14], (DEPTH, Dm, N_EXPERTS), Dm ** -0.5),
        'router_bias': nrm(ks[15], (DEPTH, N_EXPERTS), 0.01),
        'w_gate': nrm(ks[16], (DEPTH, N_EXPERTS, Dm, EXPERT_FF), Dm ** -0.5),
        'w_up': nrm(ks[17], (DEPTH, N_EXPERTS, Dm, EXPERT_FF), Dm ** -0.5),
        'w_down': nrm(ks[18], (DEPTH, N_EXPERTS, EXPERT_FF, Dm), BETA * EXPERT_FF ** -0.5),
        'ws_gate': nrm(ks[19], (DEPTH, Dm, SHARED_FF), Dm ** -0.5),
        'ws_up': nrm(ks[20], (DEPTH, Dm, SHARED_FF), Dm ** -0.5),
        'ws_down': nrm(ks[21], (DEPTH, SHARED_FF, Dm), BETA * SHARED_FF ** -0.5),
        'ln2_g': 1.0 + nrm(ks[22], (DEPTH, Dm), 0.05),
        'ln2_b': nrm(ks[23], (DEPTH, Dm), 0.02),
    }

def reference(x, c, ctx, c_ctx, w_mod, b_mod, w_in, q_norm, k_norm, pool_w, pool_scale, w_out,
              ln1_g, ln1_b, w_router, router_bias, w_gate, w_up, w_down, ws_gate, ws_up, ws_down,
              ln2_g, ln2_b):
    B_, S_, _ = x.shape
    rows = S_ // GRID_W
    cos, sin = axial_rope_tables(rows)
    for i in range(DEPTH):
        last = i == DEPTH - 1
        mod_lat = (jax.nn.silu(c) @ w_mod[i] + b_mod[i])[:, None, :]
        mod_ctx = (jax.nn.silu(c_ctx) @ w_mod[i] + b_mod[i])[None, None, :]
        sh1, sc1, g1, sh2, sc2, g2 = jnp.split(mod_lat, 6, axis=-1)
        csh1, csc1, cg1, csh2, csc2, cg2 = jnp.split(mod_ctx, 6, axis=-1)

        u_l, q_l, k_l, v_l = split_projection((x * (1.0 + sc1) + sh1) @ w_in[i])
        u_c, q_c, k_c, v_c = split_projection((ctx * (1.0 + csc1) + csh1) @ w_in[i])
        q_l = apply_rope(head_rms_norm(q_l, q_norm[i]), cos, sin)
        k_l = apply_rope(head_rms_norm(k_l, k_norm[i]), cos, sin)
        k_c = head_rms_norm(k_c, k_norm[i])
        k_all = jnp.concatenate([k_c, k_l], axis=1)
        v_all = jnp.concatenate([v_c, v_l], axis=1)
        attn_l = attend_latent_blocks(q_l, k_all, v_all)
        mix_l = jnp.concatenate([pool_mixer(u_l, pool_w[i], pool_scale[i]), attn_l], axis=-1) @ w_out[i]
        x_mid = layer_norm(ALPHA * x + g1 * mix_l, ln1_g[i], ln1_b[i])
        ffn_l = moe_ffn(x_mid * (1.0 + sc2) + sh2, w_router[i], router_bias[i], w_gate[i], w_up[i],
                        w_down[i], ws_gate[i], ws_up[i], ws_down[i])
        x_new = layer_norm(ALPHA * x_mid + g2 * ffn_l, ln2_g[i], ln2_b[i])

        if not last:
            q_c = head_rms_norm(q_c, q_norm[i])
            attn_c = attend(q_c, k_c, v_c).reshape(B_, ctx.shape[1], ATTN_WIDTH)
            mix_c = jnp.concatenate([pool_mixer(u_c, pool_w[i], pool_scale[i]), attn_c], axis=-1) @ w_out[i]
            ctx_mid = layer_norm(ALPHA * ctx + cg1 * mix_c, ln1_g[i], ln1_b[i])
            ffn_c = moe_ffn(ctx_mid * (1.0 + csc2) + csh2, w_router[i], router_bias[i], w_gate[i], w_up[i],
                            w_down[i], ws_gate[i], ws_up[i], ws_down[i])
            ctx = layer_norm(ALPHA * ctx_mid + cg2 * ffn_c, ln2_g[i], ln2_b[i])
        x = x_new
    return x


_drawn_inputs = setup_inputs


def setup_inputs(seed=0):
    import zlib

    import numpy as np

    out = dict(_drawn_inputs(seed))
    spreads = {}
    factors = {'ctx': 5.687,
     'c_ctx': 3.032,
     'q_norm': 8.0,
     'k_norm': 8.0,
     'pool_scale': 7.515,
     'ln2_b': 2.913}
    for name, (base, spread) in spreads.items():
        noise = np.random.default_rng([zlib.crc32(name.encode()), seed]).standard_normal(out[name].shape)
        drawn = base * np.exp(spread * noise) if base else spread * noise
        out[name] = __import__('jax').numpy.asarray(drawn.astype(out[name].dtype))
    for name, factor in factors.items():
        out[name] = (out[name] * factor).astype(out[name].dtype)
    return out
```

```python
from contextlib import ExitStack

import numpy as np

import concourse.bass as bass
from concourse import mybir

F32 = mybir.dt.float32
U32 = mybir.dt.uint32
I32 = mybir.dt.int32
ALU = mybir.AluOpType
ACT = mybir.ActivationFunctionType
AX = mybir.AxisListType.X

P = 128
D = 1024
SEQ = 512
CTX = 256
NT = SEQ // P
NC = CTX // P
DC = D // P
POOLW = 256
WINDOWS = (2, 4, 8, 16)
HD = 64
NH = 12
NKV = 4
GQ = NH // NKV
QW = NH * HD
KW = NKV * HD
PROJ = POOLW + QW + 2 * KW
KEYS = CTX + SEQ
KT = KEYS // P
GRID_W = 64
THETA = 10000.0
E = 64
TOPK = 8
NG = 8
TG = 4
GE = E // NG
FF = 256
RSCALE = 2.5
ALPHA = 2.0 ** 0.25
LN_EPS = 1e-5
RMS_EPS = 1e-6
PAD = 16
UP = SEQ + 2 * PAD
BIG = 1.0e30
MARK = 3.0e38
OV = SEQ * TOPK // P
MAXOVER = OV - 1
ROUNDS = E // 4 - 2

C_ID, C_IOTA, C_UT, C_IDM, C_SLOT = 0, 128, 640, 768, 772
NCONST = 773
T_COS, T_SIN, T_INV = 0, 256, 512
NTEMP = 1536


def constants():
    a = np.zeros((P, NCONST), np.float32)
    a[:, C_ID:C_ID + P] = np.eye(P)
    a[:, C_IOTA:C_IOTA + SEQ] = np.arange(1, SEQ + 1)
    a[:, C_UT:C_UT + P] = np.triu(np.ones((P, P)), 1)
    a[:, C_IDM:C_IDM + NT] = np.arange(P)[:, None] + P * np.arange(NT)[None] - SEQ
    a[:, C_SLOT] = np.arange(P)
    t = np.zeros((P, NTEMP), np.float32)
    ax = HD // 2
    inv = np.float32(THETA) ** (-np.arange(0, ax, 2, dtype=np.float32) / np.float32(ax))
    pos = np.arange(SEQ)
    ang = np.concatenate([(pos // GRID_W).astype(np.float32)[:, None] * inv,
                          (pos % GRID_W).astype(np.float32)[:, None] * inv], axis=-1)
    cos = np.repeat(np.cos(ang), 2, axis=-1)
    sin = np.repeat(np.sin(ang), 2, axis=-1)
    sin[:, 0::2] *= -1
    t[:, T_COS:T_COS + NT * HD] = cos.reshape(NT, P, HD).transpose(1, 0, 2).reshape(P, -1)
    t[:, T_SIN:T_SIN + NT * HD] = sin.reshape(NT, P, HD).transpose(1, 0, 2).reshape(P, -1)
    for g, w in enumerate(WINDOWS):
        n = np.clip(pos + w - w // 2, 0, SEQ) - np.clip(pos - w // 2, 0, SEQ)
        t[HD * (g % 2):HD * (g % 2) + HD, T_INV + SEQ * (g // 2):T_INV + SEQ * (g // 2) + SEQ] = 1.0 / n
    return a, t


def build(nc, a, consts, tempc, out):
    h_rows = nc.dram_tensor("h_rows", [SEQ, D], F32, kind="Internal").ap()
    acc_rows = nc.dram_tensor("acc_rows", [SEQ + P, D], F32, kind="Internal").ap()

    ctx = ExitStack()
    with ctx:
        def sb(name, cols, dt=F32):
            return ctx.enter_context(nc.sbuf_tensor(name, [P, cols], dt))

        def sem(name):
            return ctx.enter_context(nc.semaphore(name))

        ring = sb("ring", 20480)
        xres = sb("xres", 4096)
        xm = sb("xm", 4096)
        cm = sb("cm", 2048)
        kq = sb("kq", 6144)
        vr = sb("vr", 1536)
        pmix = sb("pmix", 1024)
        bc = sb("bc", 4096)
        lnr = sb("lnr", 2048)
        att = sb("att", 4608)
        con = sb("con", NCONST)
        ones = sb("ones", P)
        tabs = sb("tabs", 1024)
        pw = sb("pw", 256)
        gains = sb("gains", 2 * HD)
        rbias = sb("rbias", E)
        cvec = sb("cvec", 16)
        csig = sb("csig", 16)
        csil = sb("csil", 16)
        modc = sb("modc", 32)
        pscale = sb("pscale", 2)
        stat = sb("stat", 36)
        negmax = sb("negmax", 2)
        rowsum = sb("rowsum", 2)
        recips = sb("recips", 2)
        gsb = sb("gsb", 64 + 32 + 64)
        bnw = sb("bnw", 16)
        rsm = sb("rsm", 12)
        iw = sb("iw", 8)
        tcol = sb("tcol", 2)
        gidx = sb("gidx", 4, U32)
        sidx = sb("sidx", 2, U32)
        fb = sb("fb", 2 * NT)
        ovc = sb("ovc", 4)
        ovcode = sb("ovcode", 2 * OV + 1, I32)

        ident = con[:, C_ID:C_ID + P]
        wmod_a = [ring[:, 2048 * s:2048 * s + 2048] for s in range(4)]
        wmod_b = [ring[:, 4096 * s:4096 * s + 4096] for s in range(2)]
        wout = ring[:, 0:8192].rearrange("p (c n) -> p c n", c=DC)
        win = ring[:, 8192:20480].rearrange("p (c n) -> p c n", c=DC)
        gu_flat = [ring[:, 4096 + 4096 * s:8192 + 4096 * s] for s in range(4)]
        gu_w = [g.rearrange("p (u c f) -> p u c f", u=2, c=DC) for g in gu_flat]
        dn_flat = [ring[:, 2048 * s:2048 * s + 2048] for s in range(2)]
        dn_w = [g.rearrange("p (c n) -> p c n", c=2) for g in dn_flat]
        xrow = xres[:, :].rearrange("p (t d) -> p t d", t=NT)
        st_n, st_a, st_b, st_q, st_r = (xres[:, 768 * i:768 * i + 768] for i in range(5))
        xmT = xm[:, :].rearrange("p (c t) -> p c t", c=DC)
        mixA = xm[:, 1024:4096].rearrange("p (c t) -> p c t", c=6)
        mixP = pmix[:, :].rearrange("p (c t) -> p c t", c=2)
        lnA = xm[:, 0:1024]
        xg = [xm[:, 0:1024], xm[:, 1024:2048]]
        ysb = [xm[:, 2048:3072], xm[:, 3072:4096]]
        cmT = cm[:, :].rearrange("p (c t) -> p c t", c=DC)
        hperm = cm[:, 0:1024]
        r_sc = cm[:, 1024:1280]
        r_sel = cm[:, 1280:1536]
        r_mask = cm[:, 1536:1792]
        posm = cm[:, 1792:2048]
        mrow = kq[0:2, 0:2048]
        brow_a = kq[0:1, 2048:4096]
        kT = kq[:, 0:3072].rearrange("p (h k) -> p h k", h=NKV)
        qT = kq[:, 3072:6144].rearrange("p (h t) -> p h t", h=6)
        hT = kq[:, 0:4096].rearrange("p (c t) -> p c t", c=DC)
        ws_dn_flat = kq[:, 4096:6144]
        ws_dn = ws_dn_flat.rearrange("p (c n) -> p c n", c=2)
        ln2 = kq[:, 0:2048]
        vall = vr[:, :].rearrange("p (k d) -> p k d", k=KT)
        selm = vr[:, 0:512].rearrange("p (t s) -> p t s", t=NT)
        hrow = [vr[:, 512:768], vr[:, 768:1024]]
        hTe = [vr[:, 1024:1280], vr[:, 1280:1536]]
        gw_t = pmix[:, 0:256]
        sg_t = pmix[:, 256:512]
        xT = [lnr[:, 0:1024], lnr[:, 1024:2048]]
        crow = att[:, 0:2048].rearrange("p (t d) -> p t d", t=NC)
        pU = att[:, 0:2 * UP].rearrange("p (c t) -> p c t", c=2)
        pS2 = att[:, 2 * UP:4 * UP].rearrange("p (c t) -> p c t", c=2)
        pS4 = att[:, 4 * UP:6 * UP].rearrange("p (c t) -> p c t", c=2)
        pS8 = att[:, 6 * UP:7 * UP]
        pS16 = att[:, 7 * UP:8 * UP]
        qcur = att[:, 0:768].rearrange("p (h t) -> p h t", h=6)
        prob = [att[:, 768 + 768 * i:1536 + 768 * i] for i in range(2)]
        prT = [att[:, 2304 + 768 * i:3072 + 768 * i].rearrange("p (k q) -> p k q", k=KT) for i in range(2)]
        arow = att[:, 3840:4608]
        ws_gu_flat = att[:, 0:4096]
        ws_gu = ws_gu_flat.rearrange("p (u c f) -> p u c f", u=2, c=DC)
        wrt_flat = tabs[:, 0:512]
        wrt = wrt_flat.rearrange("p (c e) -> p c e", c=DC)
        info = tabs[:, 512:1024].rearrange("p (t n) -> p t n", t=NT)
        g8 = tabs[:, 512:768].rearrange("p (t g m) -> p t g m", t=NT, g=NG)
        gs16 = gsb[:, 0:64].rearrange("p (t g) -> p t g", t=NT)
        gtop = gsb[:, 64:96].rearrange("p (t g) -> p t g", t=NT)
        gmk = gsb[:, 96:160].rearrange("p (t g) -> p t g", t=NT)

        psum = ctx.enter_context(nc.psum_tensor("psum", [P, 8 * 512], F32))
        PS = [psum[:, 512 * b:512 * b + 512] for b in range(8)]
        PS3 = psum[:, :].rearrange("p (b n) -> p b n", b=8)

        ld_const, ld_temp, ld_c, ld_x, ld_ctx, ld_brow = (sem(n) for n in (
            "ld_const", "ld_temp", "ld_c", "ld_x", "ld_ctx", "ld_brow"))
        ld_wa = [sem(f"ld_wa{i}") for i in range(4)]
        ld_wb = [sem(f"ld_wb{i}") for i in range(2)]
        ld_wkv, ld_wqu, ld_small, ld_wout, ld_x2, ld_ln1, ld_ws, ld_ln2, ld_wr = (sem(n) for n in (
            "ld_wkv", "ld_wqu", "ld_small", "ld_wout", "ld_x2", "ld_ln1", "ld_ws", "ld_ln2", "ld_wr"))
        var_in, root_out = sem("var_in"), sem("root_out")
        ld_gu = [sem(f"ld_gu{i}") for i in range(4)]
        ld_dn = [sem(f"ld_dn{i}") for i in range(2)]
        ones_set, pw_zero = sem("ones_set"), sem("pw_zero")
        c_sigmoid, c_silu = sem("c_sigmoid"), sem("c_silu")
        moda_mm, moda_row, moda_tr, moda_col = sem("moda_mm"), sem("moda_row"), sem("moda_tr"), sem("moda_col")
        xtr, xtr_out = sem("xtr"), sem("xtr_out")
        xmod = sem("xmod")
        scaled, gemv, modb_mm, modb_out = sem("scaled"), sem("gemv"), sem("modb_mm"), sem("modb_out")
        tab_done = sem("tab_done")
        kv_mm, kv_sq, kv_v, kv_row, kv_tr, kv_tr_out, kv_free = (sem(n) for n in (
            "kv_mm", "kv_sq", "kv_v", "kv_row", "kv_tr", "kv_tr_out", "kv_free"))
        u_mm, u_out, u_pad, pooled, pool_mm, pool_out = (sem(n) for n in (
            "u_mm", "u_out", "u_pad", "pooled", "pool_mm", "pool_out"))
        q_cur, scored, maxed, exped, ptr, ptr_a, ptr_b, pv_mm, o_row, atr, atr_out = (sem(n) for n in (
            "q_cur", "scored", "maxed", "exped", "ptr", "ptr_a", "ptr_b", "pv_mm", "o_row", "atr", "atr_out"))
        out_mm, mix_read, ln1_done, hp_ready, hp_tr, hT_out, h_stored, log_mm = (sem(n) for n in (
            "out_mm", "mix_read", "ln1_done", "hp_ready", "hp_tr", "hT_out", "h_stored", "log_mm"))
        sc_done, masked, pos_mm, posm_done, cnt_mm, ov_col, ov_tr, ov_done = (sem(n) for n in (
            "sc_done", "masked", "pos_mm", "posm_done", "cnt_mm", "ov_col", "ov_tr", "ov_done"))
        sh_gu, sh_sig, sh_h, sh_tr, sh_hT, sh_dn, sh_ya, sh_yb, sh_pad = (sem(n) for n in (
            "sh_gu", "sh_sig", "sh_h", "sh_tr", "sh_hT", "sh_dn", "sh_ya", "sh_yb", "sh_pad"))
        sh_st = [sem("sh_st0"), sem("sh_st1")]
        sel_done, info_mm, idx_done, xg_zero, x_tr, xT_a, gu_mm, sig_done, h_done, h_tr, h_out, dn_mm, y_a, y_b = (
            sem(n) for n in ("sel_done", "info_mm", "idx_done", "xg_zero", "x_tr", "xT_a", "gu_mm",
                             "sig_done", "h_done", "h_tr", "h_out", "dn_mm", "y_a", "y_b"))
        gathered = [sem("gathered0"), sem("gathered1")]
        scattered = sem("scattered")
        ov_w, ov_sel, ov_info, ov_idx, ov_gat, ov_xtr, ov_xT, ov_gu, ov_sig, ov_h, ov_htr, ov_hT, ov_dn, ov_y, ov_scat = (
            sem("ov_" + n) for n in ("w", "sel", "info", "idx", "gat", "xtr", "xT", "gu", "sig", "h", "htr",
                                     "hT", "dn", "y", "scat"))
        ov_turn, row_moves = sem("ov_turn"), sem("row_moves")
        f_acc = [sem(f"f_acc{i}") for i in range(NT)]
        f_st, f_norm, f_out, f_stored = sem("f_st"), sem("f_norm"), sem("f_out"), sem("f_stored")
        dve_c, pool_c, hid_c, sid_c, ovd_c, att_c, f_in, f_mul, sc2_one = (sem(n) for n in (
            "dve_chain", "pool_chain", "hidden_chain", "sidx_chain", "over_chain", "att_chain", "f_in", "f_mul", "sc2_one"))

        x_v = a["x"].rearrange("o (t p) d -> p (o t) d", p=P)
        ctx_v = a["ctx"].rearrange("o (t p) d -> p (o t) d", p=P)
        wmod_v = a["w_mod"].rearrange("o (p k) n -> p (o k) n", k=DC)
        bmod_v = a["b_mod"]
        win_v = a["w_in"].rearrange("o (c p) n -> p (o c) n", p=P)
        wout_v = a["w_out"].rearrange("o (c p) n -> p (o c) n", p=P)
        wr_v = a["w_router"].rearrange("o (p c) e -> p (o c e)", c=DC)
        gate_v = a["w_gate"].rearrange("o e (p c) f -> (o e) p (c f)", c=DC)
        up_v = a["w_up"].rearrange("o e (p c) f -> (o e) p (c f)", c=DC)
        down_v = a["w_down"].rearrange("o e (p c) n -> (o e) p (c n)", c=2)
        wsg_v = a["ws_gate"].rearrange("o (p c) f -> p (o c f)", c=DC)
        wsu_v = a["ws_up"].rearrange("o (p c) f -> p (o c f)", c=DC)
        wsd_v = a["ws_down"].rearrange("o (p c) n -> p (o c n)", c=2)

        def row_bcast(name, lo, hi):
            return a[name][0:1, lo:hi].to_broadcast([P, hi - lo])

        block = ctx.enter_context(nc.Block())

        def each_expert(eng, step):
            for e in range(4):
                step(e, e)
            with eng.Fori(0, ROUNDS) as i:
                for j in range(4):
                    step(i * 4 + (4 + j), j)
            for e in range(4 + 4 * ROUNDS, E):
                step(e, e % 4)

        def is_int(e):
            return isinstance(e, int)

        @block.sync
        def _(sp):
            sp.dma_start(con[:, :], consts).then_inc(ld_const, 16)
            sp.dma_start(cvec[:, 0:8], a["c"].rearrange("o (p k) -> p (o k)", k=DC)).then_inc(ld_c, 16)
            sp.dma_start(cvec[:, 8:16], a["c_ctx"].rearrange("(p k) -> p k", k=DC)).then_inc(ld_c, 16)
            sp.dma_start(wmod_a[0], wmod_v[:, 0, 0:2 * D]).then_inc(ld_wa[0], 16)
            sp.dma_start(xres[:, :].rearrange("p (t d) -> p t d", t=NT), x_v).then_inc(ld_x, 16)
            for k in range(1, 4):
                sp.dma_start(wmod_a[k], wmod_v[:, k, 0:2 * D]).then_inc(ld_wa[k], 16)
            sp.dma_start(brow_a, bmod_v[0:1, 0:2 * D]).then_inc(ld_brow, 16)
            sp.dma_start(crow, ctx_v).then_inc(ld_ctx, 16)
            sp.dma_start(lnr[:, 0:NTEMP], tempc).then_inc(ld_temp, 16)
            sp.dma_start(gains[:, 0:HD], row_bcast("q_norm", 0, HD)).then_inc(ld_small, 16)
            sp.dma_start(gains[:, HD:2 * HD], row_bcast("k_norm", 0, HD)).then_inc(ld_small, 16)
            sp.dma_start(rbias[:, :], row_bcast("router_bias", 0, E)).then_inc(ld_small, 16)
            for h in range(2):
                sp.dma_start(pscale[:, h:h + 1], a["pool_scale"][0, P * h:P * h + P].rearrange("(p o) -> p o", o=1)).then_inc(ld_small, 16)
            sp.wait_ge(pw_zero, 1)
            for g in range(4):
                r, col = HD * (g % 2), P * (g // 2) + HD * (g % 2)
                sp.dma_start(pw[r:r + HD, col:col + HD], a["pool_w"][0, g]).then_inc(ld_small, 16)
            for k in range(4, DC):
                sp.wait_ge(moda_mm, k - 3)
                sp.dma_start(wmod_a[k % 4], wmod_v[:, k, 0:2 * D]).then_inc(ld_wa[k % 4], 16)
            sp.dma_start(win[:, :, 1024:PROJ], win_v[:, :, 1024:PROJ]).then_inc(ld_wkv, 16)
            for k in range(DC):
                if k == 2:
                    sp.dma_start(win[:, :, 0:1024], win_v[:, :, 0:1024]).then_inc(ld_wqu, 16)
                if k < 2:
                    sp.wait_ge(moda_mm, 2 * k + 6)
                else:
                    sp.wait_ge(gemv, k - 1)
                sp.dma_start(wmod_b[k % 2], wmod_v[:, k, 2 * D:6 * D]).then_inc(ld_wb[k % 2], 16)
            sp.wait_ge(gemv, DC - 1)
            sp.dma_start(wmod_b[0][0:1, :], bmod_v[0:1, 2 * D:6 * D]).then_inc(ld_wb[0], 16)
            sp.wait_ge(gemv, DC + 1)
            sp.dma_start(wout, wout_v).then_inc(ld_wout, 16)
            sp.wait_ge(kv_mm, KT + NT)
            for e in range(3):
                s = (e + 1) % 4
                sp.dma_start(gu_flat[s][:, 0:2048], gate_v[e]).then_inc(ld_gu[s], 16)
                sp.dma_start(gu_flat[s][:, 2048:4096], up_v[e]).then_inc(ld_gu[s], 16)
            sp.wait_ge(kv_tr, KT + NT)
            sp.dma_start(xrow, x_v).then_inc(ld_x2, 16)
            sp.dma_start(wrt_flat, wr_v).then_inc(ld_wr, 16)
            sp.wait_ge(pooled, 1)
            sp.dma_start(lnr[:, 0:D], row_bcast("ln1_g", 0, D)).then_inc(ld_ln1, 16)
            sp.dma_start(lnr[:, D:2 * D], row_bcast("ln1_b", 0, D)).then_inc(ld_ln1, 16)
            sp.wait_ge(atr_out, 2 * NT)
            sp.wait_ge(atr, 2 * NT)
            sp.wait_ge(o_row, NH * NT)
            sp.dma_start(ws_gu_flat[:, 0:2048], wsg_v).then_inc(ld_ws, 16)
            sp.dma_start(ws_gu_flat[:, 2048:4096], wsu_v).then_inc(ld_ws, 16)
            sp.dma_start(ws_dn_flat, wsd_v).then_inc(ld_ws, 16)
            for t in range(NT):
                sp.wait_ge(hp_ready, t + 1)
                sp.dma_start(h_rows[P * t:P * t + P, :], hperm).then_inc(h_stored, 16)
            sp.wait_ge(out_mm, NT)
            for e in range(2):
                sp.dma_start(dn_flat[e], down_v[e]).then_inc(ld_dn[e], 16)
            sp.dma_start(gu_flat[0][:, 0:2048], gate_v[3]).then_inc(ld_gu[0], 16)
            sp.dma_start(gu_flat[0][:, 2048:4096], up_v[3]).then_inc(ld_gu[0], 16)
            for t in range(NT):
                sp.wait_ge(sh_ya, t + 1)
                sp.wait_ge(sh_yb, t + 1)
                sp.dma_start(acc_rows[P * t:P * t + P, :], ysb[t % 2]).then_inc(sh_st[t % 2], 16)
            sp.dma_start(acc_rows[SEQ:SEQ + P, :], ysb[(NT - 1) % 2]).then_inc(sh_pad, 16)
            sp.wait_ge(sh_dn, NT)
            sp.wait_ge(log_mm, NT)
            sp.dma_start(ln2[:, 0:D], row_bcast("ln2_g", 0, D)).then_inc(ld_ln2, 16)
            sp.dma_start(ln2[:, D:2 * D], row_bcast("ln2_b", 0, D)).then_inc(ld_ln2, 16)

            def step(e, m):
                if not (is_int(e) and (e == 0 or e + 3 >= E)):
                    sp.wait_ge(gu_mm, e)
                    s = m % 4
                    sp.dma_start(gu_flat[s][:, 0:2048].rearrange("p (o n) -> p o n", o=1), gate_v[bass.ds(e + 3, 1)].rearrange("o p n -> p o n")).then_inc(ld_gu[s], 16)
                    sp.dma_start(gu_flat[s][:, 2048:4096].rearrange("p (o n) -> p o n", o=1), up_v[bass.ds(e + 3, 1)].rearrange("o p n -> p o n")).then_inc(ld_gu[s], 16)
                if not (is_int(e) and (e == 0 or e + 1 >= E)):
                    sp.wait_ge(dn_mm, e)
                    sp.dma_start(dn_flat[(m + 1) % 2].rearrange("p (o n) -> p o n", o=1), down_v[bass.ds(e + 1, 1)].rearrange("o p n -> p o n")).then_inc(ld_dn[(m + 1) % 2], 16)
            each_expert(sp, step)

            sp.wait_ge(ov_done, 1)
            sp.wait_ge(dn_mm, E)
            n_over = sp.value_load(ovcode[0:1, 2 * OV:2 * OV + 1], min_val=0, max_val=MAXOVER)
            with sp.Fori(0, MAXOVER) as j:
                with sp.If(j < n_over):
                    sp.wait_ge(ov_turn, j + 1)
                    ex = sp.value_load(ovcode[0:1, bass.ds(j, 1)], min_val=0, max_val=E - 1)
                    sp.dma_start(gu_flat[0][:, 0:2048].rearrange("p (o n) -> p o n", o=1), gate_v[bass.ds(ex, 1)].rearrange("o p n -> p o n")).then_inc(ov_w, 16)
                    sp.dma_start(gu_flat[0][:, 2048:4096].rearrange("p (o n) -> p o n", o=1), up_v[bass.ds(ex, 1)].rearrange("o p n -> p o n")).then_inc(ov_w, 16)
                    sp.dma_start(dn_flat[0].rearrange("p (o n) -> p o n", o=1), down_v[bass.ds(ex, 1)].rearrange("o p n -> p o n")).then_inc(ov_w, 16)

            sp.wait_ge(f_st, 1)
            for t in range(NT):
                sp.dma_start(xm[:, D * t:D * t + D], acc_rows[P * t:P * t + P, :]).then_inc(f_acc[t], 16)
            for t in range(NT):
                sp.wait_ge(f_out, t + 1)
                sp.dma_start(out[0, P * t:P * t + P, :], xm[:, D * t:D * t + D]).then_inc(f_stored, 16)
            sp.wait_ge(f_stored, 16 * NT)

        @block.gpsimd
        def _(pool):
            n = [0]

            def link(ins):
                n[0] += 1
                ins.then_inc(pool_c, 1)
                pool.wait_ge(pool_c, n[0])

            nc.gpsimd.memset(ones[:, :], 1.0).then_inc(ones_set, 1)
            nc.gpsimd.memset(pw[:, :], 0.0).then_inc(pw_zero, 1)
            for k in range(DC):
                pool.wait_ge(scaled, k + 1)
                if k == 0:
                    nc.gpsimd.tensor_copy(bc[:, :], wmod_b[0]).then_inc(gemv, 1)
                else:
                    pool.wait_ge(gemv, k)
                    nc.gpsimd.tensor_tensor(bc[:, :], wmod_b[k % 2], bc[:, :], ALU.add).then_inc(gemv, 1)
            pool.wait_ge(ld_wb[0], 16 * (DC // 2 + 1))
            pool.wait_ge(gemv, DC)
            nc.gpsimd.tensor_tensor(bc[0:1, :], bc[0:1, :], wmod_b[0][0:1, :], ALU.add).then_inc(gemv, 1)

            pool.wait_ge(u_out, 2)
            pool.wait_ge(u_pad, 2)
            hi = UP
            link(nc.gpsimd.tensor_tensor(pS2[:, :, 1:hi], pU[:, :, 0:hi - 1], pU[:, :, 1:hi], ALU.add))
            link(nc.gpsimd.tensor_tensor(pS4[:, :, 2:hi - 1], pS2[:, :, 1:hi - 2], pS2[:, :, 3:hi], ALU.add))
            link(nc.gpsimd.tensor_tensor(pS8[:, 4:hi - 3], pS4[:, 1, 2:hi - 5], pS4[:, 1, 6:hi - 1], ALU.add))
            link(nc.gpsimd.tensor_tensor(pS16[:, 8:hi - 8], pS8[:, 4:hi - 12], pS8[:, 12:hi - 4], ALU.add))
            inv = lnr[:, T_INV:T_INV + 2 * SEQ].rearrange("p (c t) -> p c t", c=2)
            lo = PAD
            pool.wait_ge(ld_temp, 16)
            for r, c, s in ((0, 0, pS2[:, 0]), (1, 0, pS4[:, 0]), (0, 1, pS8), (1, 1, pS16)):
                rs = slice(HD * r, HD * r + HD)
                link(nc.gpsimd.tensor_tensor(mixP[rs, c, :], s[rs, lo:lo + SEQ], inv[rs, c, :], ALU.mult))
            nc.gpsimd.tensor_tensor(mixP[:, :, :], mixP[:, :, :], pU[:, :, lo:lo + SEQ], ALU.subtract).then_inc(pooled, 1)

            pool.wait_ge(h_stored, 16 * NT)
            pool.wait_ge(xg_zero, 2)

            def gather(e, m):
                if is_int(e) and e >= E:
                    return
                pool.wait_ge(idx_done, e + 1)
                if not (is_int(e) and e < 2):
                    pool.wait_ge(x_tr, e - 1)
                pool.sem_inc(row_moves, 1)
                nc.gpsimd.indirect_dma_start(out=xg[m % 2], out_offset=None, in_=h_rows,
                                             in_offset=bass.IndirectOffsetOnAxis(ap=gidx[:, m % 4:m % 4 + 1], axis=0),
                                             bounds_check=SEQ - 1, oob_is_err=False).then_inc(gathered[m % 2], 16)

            def scatter(e, m):
                pool.wait_ge(y_a, e + 1)
                pool.wait_ge(y_b, e + 1)
                if not (is_int(e) and e == 0):
                    pool.wait_ge(scattered, 16 * e)
                pool.sem_inc(row_moves, 1)
                nc.gpsimd.indirect_dma_start(out=acc_rows,
                                             out_offset=bass.IndirectOffsetOnAxis(ap=sidx[:, m % 2:m % 2 + 1], axis=0),
                                             in_=ysb[m % 2], in_offset=None, bounds_check=SEQ + P - 1,
                                             compute_op=ALU.add).then_inc(scattered, 16)

            gather(0, 0)
            gather(1, 1)
            for w in (*sh_st, sh_pad):
                pool.wait_ge(w, 16 if w is sh_pad else 8 * NT)

            def step(e, m):
                gather(e + 2, m + 2)
                if not (is_int(e) and e == 0):
                    scatter(e - 1, m - 1 + 4)
            each_expert(pool, step)
            scatter(E - 1, (E - 1) % 4)
            pool.wait_ge(scattered, 16 * E)

            pool.sem_inc(ov_turn, 1)
            pool.wait_ge(ov_done, 1)
            n_over = pool.value_load(ovcode[0:1, 2 * OV:2 * OV + 1], min_val=0, max_val=MAXOVER)
            with pool.Fori(0, MAXOVER) as j:
                with pool.If(j < n_over):
                    pool.wait_ge(ov_idx, j + 1)
                    pool.sem_inc(row_moves, 1)
                    nc.gpsimd.indirect_dma_start(out=xg[0], out_offset=None, in_=h_rows,
                                                 in_offset=bass.IndirectOffsetOnAxis(ap=gidx[:, 0:1], axis=0),
                                                 bounds_check=SEQ - 1, oob_is_err=False).then_inc(ov_gat, 16)
                    pool.wait_ge(ov_y, 2 * j + 2)
                    pool.sem_inc(row_moves, 1)
                    nc.gpsimd.indirect_dma_start(out=acc_rows,
                                                 out_offset=bass.IndirectOffsetOnAxis(ap=sidx[:, 0:1], axis=0),
                                                 in_=ysb[0], in_offset=None, bounds_check=SEQ + P - 1,
                                                 compute_op=ALU.add).then_inc(ov_scat, 16)
                    pool.wait_ge(ov_scat, 16 * j + 16)
                    pool.sem_inc(ov_turn, 1)
            nc.gpsimd.memset(gidx[:, 0:1], 0).then_inc(f_st, 1)

            for t in range(NT):
                pool.wait_ge(f_norm, t + 1)
                pool.wait_ge(ld_ln2, 32)
                nc.gpsimd.tensor_tensor(xm[:, D * t:D * t + D], xm[:, D * t:D * t + D], ln2[:, 0:D], ALU.mult).then_inc(f_mul, 1)

        @block.scalar
        def _(act):
            act.wait_ge(ld_c, 32)
            nc.scalar.activation(csig[:, :], cvec[:, :], ACT.Sigmoid).then_inc(c_sigmoid, 1)
            for g in range(12):
                act.wait_ge(xtr, g + 1)
                ps = PS[4 + g % 4]
                if g < 8:
                    nc.scalar.activation(xmT[:, g, :], ps[:, :], ACT.Copy).then_inc(xtr_out, 1)
                else:
                    nc.scalar.activation(cmT[:, 2 * (g - 8):2 * (g - 8) + 2, :], ps[:, :].rearrange("p (c t) -> p c t", c=2),
                                         ACT.Copy).then_inc(xtr_out, 1)
            def k_out(j):
                act.wait_ge(kv_tr, j + 1)
                nc.scalar.activation(kT[:, :, P * j:P * j + P], PS[4 + j % 2].rearrange("p (h k) -> p h k", h=NKV),
                                     ACT.Copy).then_inc(kv_tr_out, 1)

            def q_out(i):
                act.wait_ge(kv_tr, KT + i + 1)
                for h in range(2):
                    nc.scalar.activation(qT[:, 3 * h:3 * h + 3, P * i:P * i + P],
                                         PS[4 + h][:, 0:384].rearrange("p (h t) -> p h t", h=3), ACT.Copy).then_inc(kv_tr_out, 1)

            roots = [0]

            def root(row):
                roots[0] += 1
                act.wait_ge(var_in, roots[0])
                nc.scalar.activation(row, row, ACT.Sqrt).then_inc(root_out, 1)

            def scale_wmod(k):
                if k == 0:
                    act.wait_ge(c_silu, 1)
                act.wait_ge(ld_wb[k % 2], 16 * (k // 2 + 1))
                nc.scalar.activation(wmod_b[k % 2], wmod_b[k % 2], ACT.Copy,
                                     scale=csil[:, 2 * k:2 * k + 1]).then_inc(scaled, 1)

            for j in range(KT):
                act.wait_ge(kv_mm, j + 1)
                if j:
                    act.wait_ge(kv_row, j)
                nc.scalar.activation(st_q[:, 0:KW], PS[j % 2][:, 0:KW], ACT.Square).then_inc(kv_sq, 1)
                nc.scalar.activation(vall[:, j, :], PS[j % 2][:, KW:2 * KW], ACT.Copy).then_inc(kv_v, 1)
                root(stat[:, 12:12 + NKV])
                if j:
                    k_out(j - 1)
                if j >= 2:
                    scale_wmod(j - 2)
            for c in range(2):
                act.wait_ge(u_mm, c + 1)
                nc.scalar.activation(pU[:, c, PAD:PAD + SEQ], PS[6 + c], ACT.Copy).then_inc(u_out, 1)
                if c == 0:
                    k_out(KT - 1)
            scale_wmod(4)
            for i in range(NT):
                act.wait_ge(kv_mm, KT + i + 1)
                act.wait_ge(kv_row, KT + i)
                b = i % 2
                nc.scalar.activation(st_q[:, 0:512], PS[b], ACT.Square).then_inc(kv_v, 1)
                nc.scalar.activation(st_q[:, 512:768], PS[2 + b][:, 0:256], ACT.Square).then_inc(kv_sq, 1)
                if i:
                    q_out(i - 1)
                root(stat[:, 12:12 + NH])
                if 5 + i < DC:
                    scale_wmod(5 + i)
            for q in range(8):
                act.wait_ge(modb_mm, q + 1)
                nc.scalar.activation(bc[:, 512 * q:512 * q + 512], PS[6 + q % 2], ACT.Copy).then_inc(modb_out, 1)
            act.wait_ge(ld_small, 16 * 9)
            act.wait_ge(pool_mm, 2)
            for c in range(2):
                nc.scalar.activation(mixP[:, c, :], PS[6 + c], ACT.Copy, scale=pscale[:, c:c + 1]).then_inc(pool_out, 1)
            q_out(NT - 1)

            with act.Fori(0, NT) as t:
                for u in range(NH):
                    act.wait_ge(maxed, t * NH + (u + 1))
                    if u >= 2:
                        act.wait_ge(ptr, t * (2 * NH) + 2 * (u - 1))
                        act.wait_ge(o_row, t * NH + (u - 1))
                    w = u % 2
                    nc.scalar.activation(prob[w].rearrange("p (b k) -> p b k", b=2), PS3[:, 2 * w:2 * w + 2, 0:384], ACT.Exp,
                                         bias=negmax[:, w:w + 1], accum_out=rowsum[:, w:w + 1]).then_inc(exped, 1)
                    act.wait_ge(ptr, t * (2 * NH) + (2 * u + 1))
                    if u >= 2:
                        act.wait_ge(pv_mm, t * NH + (u - 1))
                    nc.scalar.activation(prT[w][:, 0:3, :], PS[4][:, 0:384].rearrange("p (k q) -> p k q", k=3),
                                         ACT.Copy).then_inc(ptr_a, 1)
                for h in range(2):
                    act.wait_ge(atr, t * 2 + (h + 1))
                    nc.scalar.activation(mixA[:, 3 * h:3 * h + 3, bass.ds(t * P, P)],
                                         PS[4 + h][:, 0:384].rearrange("p (k q) -> p k q", k=3), ACT.Copy).then_inc(atr_out, 1)

            def hT_copy(t):
                for g in range(2):
                    act.wait_ge(hp_tr, 2 * t + g + 1)
                    nc.scalar.activation(hT[:, 4 * g:4 * g + 4, P * t:P * t + P],
                                         PS[2 + g].rearrange("p (c t) -> p c t", c=4), ACT.Copy).then_inc(hT_out, 1)
            root(bnw[:, 15:16])
            for t in range(NT):
                hT_copy(t)
                if t + 1 < NT:
                    root(bnw[:, 15:16])
            act.wait_ge(log_mm, NT)
            act.wait_ge(kv_row, KT + NT)
            nc.scalar.activation(r_sc, PS[7][:, 0:256], ACT.Sigmoid).then_inc(sc_done, 1)

            def shared_sig(t):
                act.wait_ge(sh_gu, t + 1)
                if t:
                    act.wait_ge(sh_h, t)
                nc.scalar.activation(sg_t, PS[t % 2][:, 0:FF], ACT.Sigmoid).then_inc(sh_sig, 1)

            shared_sig(0)
            for t in range(NT):
                if t + 1 < NT:
                    shared_sig(t + 1)
                act.wait_ge(sh_dn, t + 1)
                if t >= 2:
                    act.wait_ge(sh_st[t % 2], 16 * (t // 2))
                nc.scalar.activation(ysb[t % 2][:, 0:512], PS[4], ACT.Copy).then_inc(sh_ya, 1)

            def xT_copy(e, m):
                if is_int(e) and e >= E:
                    return
                if not (is_int(e) and e < 2):
                    act.wait_ge(gu_mm, e - 1)
                for g in range(2):
                    act.wait_ge(x_tr, e + 1)
                    nc.scalar.activation(xT[m % 2][:, 512 * g:512 * g + 512], PS[2 + g], ACT.Copy).then_inc(xT_a, 1)

            def y_copy(e, m):
                act.wait_ge(dn_mm, e + 1)
                if is_int(e) and e < 2:
                    for w in (*sh_st, sh_pad):
                        act.wait_ge(w, 16 if w is sh_pad else 8 * NT)
                else:
                    act.wait_ge(scattered, 16 * (e - 1))
                nc.scalar.activation(ysb[m % 2][:, 0:512], PS[4], ACT.Copy).then_inc(y_a, 1)

            xT_copy(0, 0)

            def step(e, m):
                xT_copy(e + 1, m + 1)
                act.wait_ge(gu_mm, e + 1)
                if not (is_int(e) and e == 0):
                    act.wait_ge(h_done, e)
                nc.scalar.activation(sg_t, PS[m % 2][:, 0:FF], ACT.Sigmoid).then_inc(sig_done, 1)
                if not (is_int(e) and e == 0):
                    y_copy(e - 1, m + 3)
            each_expert(act, step)
            y_copy(E - 1, (E - 1) % 4)

            act.wait_ge(ov_done, 1)
            act.wait_ge(scattered, 16 * E)
            n_over = act.value_load(ovcode[0:1, 2 * OV:2 * OV + 1], min_val=0, max_val=MAXOVER)
            with act.Fori(0, MAXOVER) as j:
                with act.If(j < n_over):
                    act.wait_ge(ov_turn, j + 1)
                    act.wait_ge(ov_xtr, j + 1)
                    for g in range(2):
                        nc.scalar.activation(xT[0][:, 512 * g:512 * g + 512], PS[2 + g], ACT.Copy).then_inc(ov_xT, 1)
                    act.wait_ge(ov_gu, j + 1)
                    nc.scalar.activation(sg_t, PS[0][:, 0:FF], ACT.Sigmoid).then_inc(ov_sig, 1)
                    act.wait_ge(ov_dn, j + 1)
                    nc.scalar.activation(ysb[0][:, 0:512], PS[4], ACT.Copy).then_inc(ov_y, 1)

            for t in range(NT):
                root(bnw[:, 15:16])
                act.wait_ge(f_in, t + 1)
                nc.scalar.activation(xm[:, D * t:D * t + D], xrow[:, t, :], ACT.Identity,
                                     bias=fb[:, 2 * t + 1:2 * t + 2], scale=fb[:, 2 * t:2 * t + 1]).then_inc(f_norm, 1)

        @block.tensor
        def _(pe):
            mm = nc.tensor.matmul
            tr = nc.tensor.transpose
            csv = csil[:, :].rearrange("p (k w) -> p k w", w=2)
            pe.wait_ge(ones_set, 1)
            pe.wait_ge(ld_const, 16)

            def mod_a(k):
                if k == 0:
                    pe.wait_ge(c_silu, 1)
                pe.wait_ge(ld_wa[k % 4], 16 * (k // 4 + 1))
                for q in range(4):
                    last = mm(PS[q][0:2, :], csv[:, k, :], wmod_a[k % 4][:, 512 * q:512 * q + 512], start=(k == 0), stop=False)
                last.then_inc(moda_mm, 1)

            def x_transposes(g):
                if g >= 4:
                    pe.wait_ge(xtr_out, g - 3)
                for i in range(4):
                    if g < 8:
                        src = xrow[:, i, P * g:P * g + P]
                    else:
                        c = 2 * (g - 8) + i // 2
                        src = crow[:, i % 2, P * c:P * c + P]
                    last = tr(PS[4 + g % 4][:, P * i:P * i + P], src, ident)
                last.then_inc(xtr, 1)

            mod_a(0)
            pe.wait_ge(ld_x, 16)
            for g in range(8):
                x_transposes(g)
            for k in range(1, 4):
                mod_a(k)
            pe.wait_ge(ld_ctx, 16)
            for g in range(8, 12):
                x_transposes(g)
            for k in range(4, DC):
                mod_a(k)
            pe.wait_ge(ld_brow, 16)
            for q in range(4):
                last = mm(PS[q][0:2, :], ones[0:1, 0:2], brow_a[:, 512 * q:512 * q + 512], start=False, stop=True)
            last.then_inc(moda_mm, 1)
            pe.wait_ge(moda_row, 4)
            pe.wait_ge(xtr_out, 12)
            for i in range(16):
                last = tr(PS[4][:, 2 * i:2 * i + 2], mrow[:, P * i:P * i + P], ident[0:2, 0:2])
            last.then_inc(moda_tr, 1)

            def k_transposes(j):
                pe.wait_ge(kv_row, j + 1)
                if j >= 2:
                    pe.wait_ge(kv_tr_out, j - 1)
                if j < 1:
                    pe.wait_ge(moda_col, 2)
                for h in range(NKV):
                    last = tr(PS[4 + j % 2][:, P * h:P * h + P], st_r[:, P * h:P * h + P], ident)
                last.then_inc(kv_tr, 1)

            def q_transposes(i):
                pe.wait_ge(kv_row, KT + i + 1)
                pe.wait_ge(kv_tr_out, KT + 2 * i)
                for h in range(6):
                    last = tr(PS[4 + h // 3][:, P * (h % 3):P * (h % 3) + P], st_r[:, P * h:P * h + P], ident)
                last.then_inc(kv_tr, 1)

            pe.wait_ge(ld_wkv, 16)
            for j in range(KT):
                if j < 2:
                    pe.wait_ge(moda_row, 4)
                else:
                    pe.wait_ge(kv_v, j - 1)
                    pe.wait_ge(kv_row, j - 1)
                for k in range(DC):
                    if j == 0:
                        pe.wait_ge(xmod, k + 1)
                    if j == NC:
                        pe.wait_ge(xmod, DC + k + 1)
                    lhs = cmT[:, k, P * j:P * j + P] if j < NC else xmT[:, k, P * (j - NC):P * (j - NC) + P]
                    last = mm(PS[j % 2], lhs, win[:, k, 1024:PROJ], start=(k == 0), stop=(k == DC - 1))
                last.then_inc(kv_mm, 1)
                if j:
                    k_transposes(j - 1)
            pe.wait_ge(ld_wqu, 16)
            for c in range(2):
                for k in range(DC):
                    last = mm(PS[6 + c], win[:, k, P * c:P * c + P], xmT[:, k, :], start=(k == 0), stop=(k == DC - 1))
                last.then_inc(u_mm, 1)
                if c == 0:
                    k_transposes(KT - 1)
            for i in range(NT):
                if i < 2:
                    pe.wait_ge(kv_v, KT - 1 + i)
                    pe.wait_ge(kv_sq, KT - 1 + i)
                    pe.wait_ge(kv_row, KT - 1 + i)
                else:
                    pe.wait_ge(kv_row, KT + i - 1)
                for k in range(DC):
                    mm(PS[i % 2], xmT[:, k, P * i:P * i + P], win[:, k, 256:768], start=(k == 0), stop=(k == DC - 1))
                for k in range(DC):
                    last = mm(PS[2 + i % 2][:, 0:256], xmT[:, k, P * i:P * i + P], win[:, k, 768:1024], start=(k == 0), stop=(k == DC - 1))
                last.then_inc(kv_mm, 1)
                if i:
                    q_transposes(i - 1)
            pe.wait_ge(gemv, DC + 1)
            pe.wait_ge(u_out, 2)
            for q in range(8):
                if q >= 2:
                    pe.wait_ge(modb_out, q - 1)
                mm(PS[6 + q % 2], ones[:, :], bc[:, 512 * q:512 * q + 512], start=True, stop=True).then_inc(modb_mm, 1)
            pe.wait_ge(modb_out, 8)
            pe.wait_ge(pooled, 1)
            pe.wait_ge(ld_small, 16 * 9)
            for c in range(2):
                mm(PS[6 + c], pw[:, P * c:P * c + P], mixP[:, c, :], start=True, stop=True).then_inc(pool_mm, 1)
            q_transposes(NT - 1)
            pe.wait_ge(pool_out, 2)
            pe.wait_ge(kv_tr_out, KT + 2 * NT)

            with pe.Fori(0, NT) as t:
                pe.wait_ge(q_cur, t + 1)

                def scores(u):
                    if u >= 2:
                        pe.wait_ge(exped, t * NH + (u - 1))
                    r = HD * (u % 2)
                    for b in range(2):
                        last = mm(PS[2 * (u % 2) + b][:, 0:384], qcur[r:r + HD, u // 2, :],
                                  kT[r:r + HD, u // GQ, 384 * b:384 * b + 384], start=True, stop=True)
                    last.then_inc(scored, 1)

                def prob_transposes(u):
                    pe.wait_ge(exped, t * NH + (u + 1))
                    for b in range(2):
                        if u:
                            pe.wait_ge((ptr_a, ptr_b)[b], t * NH + u)
                        for k in range(3):
                            last = tr(PS[4 + b][:, P * k:P * k + P], prob[u % 2][:, P * (3 * b + k):P * (3 * b + k) + P], ident)
                        last.then_inc(ptr, 1)

                def values(u):
                    pe.wait_ge(ptr_a, t * NH + (u + 1))
                    pe.wait_ge(ptr_b, t * NH + (u + 1))
                    if u >= 2:
                        pe.wait_ge(o_row, t * NH + (u - 1))
                    v = HD * (u // GQ)
                    for k in range(KT):
                        last = mm(PS[6 + u % 2][:, 0:HD], prT[u % 2][:, k, :], vall[:, k, v:v + HD], start=(k == 0), stop=(k == KT - 1))
                    last.then_inc(pv_mm, 1)

                scores(0)
                for u in range(NH):
                    if u + 1 < NH:
                        scores(u + 1)
                    if u:
                        values(u - 1)
                    prob_transposes(u)
                values(NH - 1)
                pe.wait_ge(o_row, t * NH + NH)
                for h in range(2):
                    for k in range(3):
                        last = tr(PS[4 + h][:, P * k:P * k + P], arow[:, P * (3 * h + k):P * (3 * h + k) + P], ident)
                    last.then_inc(atr, 1)
                pe.wait_ge(atr_out, t * 2 + 2)

            pe.wait_ge(ld_wout, 16)

            def out_proj(t):
                if t >= 2:
                    pe.wait_ge(mix_read, t - 1)
                b = 4 * (t % 2)
                for q in range(2):
                    for c in range(DC):
                        lhs = mixP[:, c, P * t:P * t + P] if c < 2 else mixA[:, c - 2, P * t:P * t + P]
                        last = mm(PS[b + q], lhs, wout[:, c, 512 * q:512 * q + 512], start=(c == 0), stop=(c == DC - 1))
                last.then_inc(out_mm, 1)

            def h_transposes(t):
                pe.wait_ge(hp_ready, t + 1)
                if t:
                    pe.wait_ge(hT_out, 2 * t)
                for g in range(2):
                    for i in range(4):
                        c = 4 * g + i
                        last = tr(PS[2 + g][:, P * i:P * i + P], hperm[:, P * c:P * c + P], ident)
                    last.then_inc(hp_tr, 1)

            def logits(t):
                pe.wait_ge(hT_out, 2 * t + 2)
                if t == 0:
                    pe.wait_ge(ld_wr, 16)
                for c in range(DC):
                    last = mm(PS[7][:, E * t:E * t + E], hT[:, c, P * t:P * t + P], wrt[:, c, :], start=(c == 0), stop=(c == DC - 1))
                last.then_inc(log_mm, 1)

            out_proj(0)
            for t in range(NT):
                if t + 1 < NT:
                    out_proj(t + 1)
                h_transposes(t)
                logits(t)

            def swiglu_in(bank, lhs, w):
                for c in range(DC):
                    last = mm(PS[bank].rearrange("p (u f) -> p u f", u=2), lhs(c), w[:, :, c, :], start=(c == 0), stop=(c == DC - 1))
                return last

            def swiglu_out(lhs, w):
                for q in range(2):
                    for c in range(2):
                        last = mm(PS[4 + q], lhs[:, P * c:P * c + P], w[:, c, 512 * q:512 * q + 512], start=(c == 0), stop=(c == 1))
                return last

            def positions():
                pe.wait_ge(masked, 1)
                for t in range(NT):
                    for s in range(t + 1):
                        last = mm(PS[7][:, E * t:E * t + E], con[:, C_UT:C_UT + P] if s == t else ones[:, :],
                                  r_mask[:, E * s:E * s + E], start=(s == 0), stop=(s == t))
                for s in range(NT):
                    last = mm(PS[7][:, 4 * E:5 * E], ones[:, :], r_mask[:, E * s:E * s + E], start=(s == 0), stop=(s == NT - 1))
                last.then_inc(pos_mm, 1)

            pe.wait_ge(ld_ws, 48)
            pe.wait_ge(mix_read, NT)

            def shared_in(t):
                if t >= 2:
                    pe.wait_ge(sh_h, t - 1)
                swiglu_in(t % 2, lambda c: hT[:, c, P * t:P * t + P], ws_gu).then_inc(sh_gu, 1)

            def shared_out(t):
                pe.wait_ge(sh_h, t + 1)
                if t:
                    pe.wait_ge(sh_hT, t)
                for c in range(2):
                    last = tr(PS[6][:, P * c:P * c + P], hrow[t % 2][:, P * c:P * c + P], ident)
                last.then_inc(sh_tr, 1)
                pe.wait_ge(sh_hT, t + 1)
                if t:
                    pe.wait_ge(sh_ya, t)
                    pe.wait_ge(sh_yb, t)
                swiglu_out(hTe[t % 2], ws_dn).then_inc(sh_dn, 1)

            shared_in(0)
            for t in range(NT):
                if t + 1 < NT:
                    shared_in(t + 1)
                if t == 0:
                    positions()
                shared_out(t)
            pe.wait_ge(ov_col, 1)
            pe.wait_ge(posm_done, 1)
            tr(PS[7][0:1, 0:P], ovc[:, 0:1], ident)
            tr(PS[7][0:1, P:2 * P], ovc[:, 1:2], ident).then_inc(ov_tr, 1)
            pe.wait_ge(ov_done, 1)

            def list_info(e, m):
                if is_int(e) and e >= E:
                    return
                pe.wait_ge(sel_done, e + 1)
                if not (is_int(e) and e == 0):
                    pe.wait_ge(idx_done, e)
                for t in range(NT):
                    last = mm(PS[7][:, 0:2], selm[:, t, :], info[:, t, bass.ds(e * 2, 2)], start=(t == 0), stop=(t == NT - 1))
                last.then_inc(info_mm, 1)

            def row_transposes(e, m):
                if is_int(e) and e >= E:
                    return
                if is_int(e):
                    pe.wait_ge(gathered[m % 2], 16 * (e // 2 + 1))
                else:
                    pe.wait_ge(gathered[m % 2], gath_count(e, m))
                if not (is_int(e) and e == 0):
                    pe.wait_ge(xT_a, e * 2)
                for c in range(DC):
                    last = tr(PS[2 + c // 4][:, P * (c % 4):P * (c % 4) + P], xg[m % 2][:, P * c:P * c + P], ident)
                last.then_inc(x_tr, 1)

            def gath_count(e, m):
                return e * 8 + (16 if m % 2 == 0 else 8)

            def slot_count(e, m, per):
                return (e - m % 4) * (per // 4) + per

            def hidden_transposes(e, m):
                pe.wait_ge(h_done, e + 1)
                if not (is_int(e) and e == 0):
                    pe.wait_ge(h_out, e)
                for c in range(2):
                    last = tr(PS[6][:, P * c:P * c + P], hrow[m % 2][:, P * c:P * c + P], ident)
                last.then_inc(h_tr, 1)

            def down(e, m):
                pe.wait_ge(h_out, e + 1)
                if not (is_int(e) and e == 0):
                    pe.wait_ge(y_a, e)
                    pe.wait_ge(y_b, e)
                pe.wait_ge(ld_dn[m % 2], (e * 8 + (16 if m % 2 == 0 else 8)))
                swiglu_out(hTe[m % 2], dn_w[m % 2]).then_inc(dn_mm, 1)

            list_info(0, 0)
            list_info(1, 1)
            row_transposes(0, 0)

            def step(e, m):
                row_transposes(e + 1, m + 1)
                list_info(e + 2, m + 2)
                if not (is_int(e) and e == 0):
                    hidden_transposes(e - 1, m + 3)
                pe.wait_ge(xT_a, e * 2 + 2)
                pe.wait_ge(ld_gu[(m + 1) % 4], slot_count(e, m, 32))
                if not (is_int(e) and e < 2):
                    pe.wait_ge(h_done, e - 1)
                swiglu_in(m % 2, lambda c: xT[m % 2][:, P * c:P * c + P], gu_w[(m + 1) % 4]).then_inc(gu_mm, 1)
                if not (is_int(e) and e == 0):
                    down(e - 1, m + 3)
            each_expert(pe, step)
            hidden_transposes(E - 1, (E - 1) % 4)
            down(E - 1, (E - 1) % 4)

            pe.wait_ge(y_a, E)
            pe.wait_ge(y_b, E)
            pe.wait_ge(scattered, 16 * E)
            n_over = pe.value_load(ovcode[0:1, 2 * OV:2 * OV + 1], min_val=0, max_val=MAXOVER)
            with pe.Fori(0, MAXOVER) as j:
                with pe.If(j < n_over):
                    pe.wait_ge(ov_turn, j + 1)
                    ex = pe.value_load(ovcode[0:1, bass.ds(j, 1)], min_val=0, max_val=E - 1)
                    pe.wait_ge(ov_sel, j + 1)
                    for t in range(NT):
                        last = mm(PS[7][:, 0:2], selm[:, t, :], info[:, t, bass.ds(ex * 2, 2)], start=(t == 0), stop=(t == NT - 1))
                    last.then_inc(ov_info, 1)
                    pe.wait_ge(ov_gat, 16 * j + 16)
                    for c in range(DC):
                        last = tr(PS[2 + c // 4][:, P * (c % 4):P * (c % 4) + P], xg[0][:, P * c:P * c + P], ident)
                    last.then_inc(ov_xtr, 1)
                    pe.wait_ge(ov_xT, 2 * j + 2)
                    pe.wait_ge(ov_w, 48 * j + 48)
                    swiglu_in(0, lambda c: xT[0][:, P * c:P * c + P], gu_w[0]).then_inc(ov_gu, 1)
                    pe.wait_ge(ov_h, j + 1)
                    for c in range(2):
                        last = tr(PS[6][:, P * c:P * c + P], hrow[0][:, P * c:P * c + P], ident)
                    last.then_inc(ov_htr, 1)
                    pe.wait_ge(ov_hT, j + 1)
                    swiglu_out(hTe[0], dn_w[0]).then_inc(ov_dn, 1)
                    pe.wait_ge(ov_y, 2 * j + 2)

        @block.vector
        def _(dve):
            V = nc.vector
            n = [0]

            def link(ins):
                n[0] += 1
                ins.then_inc(dve_c, 1)
                dve.wait_ge(dve_c, n[0])

            csv = csil[:, :].rearrange("p (k w) -> p w k", w=2)
            dve.wait_ge(c_sigmoid, 1)
            V.tensor_tensor(csv, cvec[:, :].rearrange("p (w k) -> p w k", w=2), csig[:, :].rearrange("p (w k) -> p w k", w=2),
                            ALU.mult).then_inc(c_silu, 1)
            dve.wait_ge(ld_temp, 16)
            dve.wait_ge(ld_small, 16 * 9)
            cosv = lnr[:, T_COS:T_COS + 256].rearrange("p (t i w) -> p t i w", t=NT, w=2)
            sinv = lnr[:, T_SIN:T_SIN + 256].rearrange("p (t i w) -> p t i w", t=NT, w=2)
            for s in range(2):
                g = gains[:, HD * s:HD * s + HD].rearrange("p (o i w) -> p o i w", o=1, w=2)
                sc = HD ** -0.5 if s == 0 else 1.0
                for o in range(2):
                    tv = tabs[:, 512 * s + 256 * o:512 * s + 256 * o + 256].rearrange("p (t i w) -> p t i w", t=NT, w=2)
                    src = sinv if o else cosv
                    for w in range(2):
                        gw = g[:, :, :, (w + o) % 2].to_broadcast([P, NT, HD // 2])
                        V.scalar_tensor_tensor(tv[:, :, :, w], src[:, :, :, w], sc, gw, ALU.mult, ALU.mult).then_inc(tab_done, 1)
            dve.wait_ge(moda_mm, DC + 1)
            for q in range(4):
                V.tensor_copy(mrow[:, 512 * q:512 * q + 512], PS[q][0:2, :]).then_inc(moda_row, 1)
            dve.wait_ge(moda_tr, 1)
            V.tensor_copy(modc[:, 0:16], PS[4][:, 0:16]).then_inc(moda_col, 1)
            V.tensor_scalar(modc[:, 16:32], PS[4][:, 16:32], 1.0, None, ALU.add).then_inc(moda_col, 1)
            dve.wait_ge(moda_col, 2)
            mc = modc[:, :].rearrange("p (s k w) -> p s k w", s=2, w=2)
            for k in range(DC):
                V.tensor_scalar(cmT[:, k, :], cmT[:, k, :], mc[:, 1, k, 1:2], mc[:, 0, k, 1:2], ALU.mult, ALU.add).then_inc(xmod, 1)
            for k in range(DC):
                V.tensor_scalar(xmT[:, k, :], xmT[:, k, :], mc[:, 1, k, 0:1], mc[:, 0, k, 0:1], ALU.mult, ALU.add).then_inc(xmod, 1)
            dve.wait_ge(tab_done, 8)

            norms = [0]

            def rstd(heads):
                ss, ms, rs = stat[:, 0:heads], stat[:, 12:12 + heads], stat[:, 24:24 + heads]
                link(V.tensor_reduce(ss, st_q[:, 0:HD * heads].rearrange("p (h d) -> p h d", d=HD), AX, ALU.add))
                V.tensor_scalar(ms, ss, 1.0 / HD, RMS_EPS, ALU.mult, ALU.add).then_inc(var_in, 1)
                norms[0] += 1
                dve.wait_ge(root_out, norms[0])
                link(V.reciprocal(rs, ms))
                return rs

            def rotate(heads, s, t):
                nv = st_n[:, 0:HD * heads].rearrange("p (h i w) -> p h i w", h=heads, w=2)
                bv = st_b[:, 0:HD * heads].rearrange("p (h i w) -> p h i w", h=heads, w=2)
                C = tabs[:, 512 * s + HD * t:512 * s + HD * t + HD]
                S = tabs[:, 512 * s + 256 + HD * t:512 * s + 256 + HD * t + HD].rearrange("p (o i w) -> p o i w", o=1, w=2)
                V.tensor_tensor(st_a[:, 0:HD * heads].rearrange("p (h d) -> p h d", h=heads), st_n[:, 0:HD * heads].rearrange("p (h d) -> p h d", h=heads),
                                C.rearrange("p (o d) -> p o d", o=1).to_broadcast([P, heads, HD]), ALU.mult).then_inc(dve_c, 1)
                for w in range(2):
                    V.tensor_tensor(bv[:, :, :, w], nv[:, :, :, 1 - w], S[:, :, :, w].to_broadcast([P, heads, HD // 2]),
                                    ALU.mult).then_inc(dve_c, 1)
                n[0] += 3
                dve.wait_ge(dve_c, n[0])

            for j in range(KT):
                dve.wait_ge(kv_sq, j + 1)
                rs = rstd(NKV)
                dup = st_r[:, 0:512].rearrange("p (h r d) -> p h r d", h=NKV, r=2)
                link(V.tensor_tensor(st_n[:, 0:KW].rearrange("p (h d) -> p h d", h=NKV), PS[j % 2][:, 0:KW].rearrange("p (h d) -> p h d", h=NKV),
                                     rs.rearrange("p (h o) -> p h o", o=1).to_broadcast([P, NKV, HD]), ALU.mult))
                if j:
                    dve.wait_ge(kv_tr, j)
                if j < NC:
                    for r in range(2):
                        last = V.tensor_tensor(dup[:, :, r, :], st_n[:, 0:KW].rearrange("p (h d) -> p h d", h=NKV),
                                               gains[:, HD:2 * HD].rearrange("p (o d) -> p o d", o=1).to_broadcast([P, NKV, HD]), ALU.mult)
                        if r == 0:
                            last.then_inc(dve_c, 1)
                            n[0] += 1
                    last.then_inc(kv_row, 1)
                else:
                    rotate(NKV, 1, j - NC)
                    for r in range(2):
                        last = V.tensor_tensor(dup[:, :, r, :], st_a[:, 0:KW].rearrange("p (h d) -> p h d", h=NKV),
                                               st_b[:, 0:KW].rearrange("p (h d) -> p h d", h=NKV), ALU.add)
                        if r == 0:
                            last.then_inc(dve_c, 1)
                            n[0] += 1
                    last.then_inc(kv_row, 1)
                dve.wait_ge(kv_row, j + 1)
                dve.wait_ge(dve_c, n[0])
            dve.wait_ge(xtr_out, 12)
            V.memset(pU[:, :, 0:PAD], 0.0).then_inc(u_pad, 1)
            V.memset(pU[:, :, PAD + SEQ:UP], 0.0).then_inc(u_pad, 1)
            for i in range(NT):
                dve.wait_ge(kv_sq, KT + i + 1)
                dve.wait_ge(kv_v, KT + i + 1)
                rb = rstd(NH).rearrange("p (h o) -> p h o", o=1)
                link(V.tensor_tensor(st_n[:, 0:512].rearrange("p (h d) -> p h d", h=8), PS[i % 2].rearrange("p (h d) -> p h d", h=8),
                                     rb[:, 0:8, :].to_broadcast([P, 8, HD]), ALU.mult))
                link(V.tensor_tensor(st_n[:, 512:768].rearrange("p (h d) -> p h d", h=4), PS[2 + i % 2][:, 0:256].rearrange("p (h d) -> p h d", h=4),
                                     rb[:, 8:12, :].to_broadcast([P, 4, HD]), ALU.mult))
                rotate(NH, 0, i)
                dve.wait_ge(kv_tr, KT + i)
                V.tensor_tensor(st_r, st_a, st_b, ALU.add).then_inc(kv_row, 1)
                dve.wait_ge(kv_row, KT + i + 1)

            dve.wait_ge(kv_tr_out, KT + 2 * NT)
            dve.wait_ge(pooled, 1)
            with dve.Fori(0, NT) as t:
                V.tensor_copy(qcur, qT[:, :, bass.ds(t * P, P)]).then_inc(q_cur, 1)

                def row_max(u):
                    dve.wait_ge(scored, t * NH + (u + 1))
                    if u >= 2:
                        dve.wait_ge(exped, t * NH + (u - 1))
                    w = u % 2
                    V.tensor_reduce(negmax[:, w:w + 1], PS3[:, 2 * w:2 * w + 2, 0:384], mybir.AxisListType.XY, ALU.max,
                                    negate=True).then_inc(maxed, 1)

                def out_row(u):
                    w = u % 2
                    dve.wait_ge(pv_mm, t * NH + (u + 1))
                    V.reciprocal(recips[:, 0:1], rowsum[:, w:w + 1]).then_inc(att_c, 1)
                    dve.wait_ge(att_c, t * NH + (u + 1))
                    V.tensor_scalar(arow[:, HD * u:HD * u + HD], PS[6 + w][:, 0:HD], recips[:, 0:1], None, ALU.mult).then_inc(o_row, 1)

                def half_b(u):
                    dve.wait_ge(ptr, t * (2 * NH) + (2 * u + 2))
                    if u >= 2:
                        dve.wait_ge(pv_mm, t * NH + (u - 1))
                    V.tensor_copy(prT[u % 2][:, 3:6, :], PS[5][:, 0:384].rearrange("p (k q) -> p k q", k=3)).then_inc(ptr_b, 1)

                row_max(0)
                for u in range(NH):
                    if u + 1 < NH:
                        row_max(u + 1)
                    if u:
                        out_row(u - 1)
                    half_b(u)
                out_row(NH - 1)

            dve.wait_ge(modb_out, 8)
            g1, sh2, sc2, g2 = (bc[:, D * i:D * i + D] for i in range(4))
            link(V.tensor_scalar(sc2, sc2, 1.0, None, ALU.add))
            dve.wait_ge(ld_x2, 16)
            dve.wait_ge(ld_ln1, 32)

            def norm_stats(row):
                for h in range(2):
                    V.bn_stats(bnw[:, 6 * h:6 * h + 6], row[:, 512 * h:512 * h + 512]).then_inc(dve_c, 1)
                n[0] += 2
                dve.wait_ge(dve_c, n[0])
                link(V.bn_aggr(bnw[:, 12:14], bnw[:, 0:12].rearrange("p (c s) -> p c s", c=2)))
                V.tensor_scalar(bnw[:, 15:16], bnw[:, 13:14], LN_EPS, None, ALU.add).then_inc(var_in, 1)
                norms[0] += 1
                dve.wait_ge(root_out, norms[0])
                link(V.reciprocal(bnw[:, 14:15], bnw[:, 15:16]))

            for t in range(NT):
                xr = xrow[:, t, :]
                b = 4 * (t % 2)
                dve.wait_ge(out_mm, t + 1)
                if t:
                    dve.wait_ge(hp_ready, t)
                V.tensor_tensor(lnA.rearrange("p (b n) -> p b n", b=2), PS3[:, b:b + 2, :], g1.rearrange("p (b n) -> p b n", b=2),
                                ALU.mult).then_inc(mix_read, 1)
                dve.wait_ge(mix_read, t + 1)
                link(V.scalar_tensor_tensor(xr, xr, ALPHA, lnA, ALU.mult, ALU.add))
                norm_stats(xr)
                link(V.tensor_scalar(xr, xr, bnw[:, 12:13], bnw[:, 14:15], ALU.subtract, ALU.mult))
                link(V.tensor_tensor(xr, xr, lnr[:, 0:D], ALU.mult))
                link(V.tensor_tensor(xr, xr, lnr[:, D:2 * D], ALU.add))
                link(V.tensor_tensor(lnA, xr, sc2, ALU.mult))
                if t:
                    dve.wait_ge(hp_tr, 2 * t)
                    dve.wait_ge(h_stored, 16 * t)
                V.tensor_tensor(hperm.rearrange("p (c q) -> p q c", c=DC), lnA.rearrange("p (q c) -> p q c", c=DC),
                                sh2.rearrange("p (q c) -> p q c", c=DC), ALU.add).then_inc(hp_ready, 1)
            dve.wait_ge(hp_ready, NT)
            V.memset(xg[0], 0.0).then_inc(xg_zero, 1)
            V.memset(xg[1], 0.0).then_inc(xg_zero, 1)

            sel3 = r_sel.rearrange("p (t g m) -> p t g m", t=NT, g=NG)
            dve.wait_ge(sc_done, 1)
            dve.wait_ge(ld_small, 16 * 9)
            link(V.tensor_tensor(r_sel.rearrange("p (t e) -> p t e", t=NT), r_sc.rearrange("p (t e) -> p t e", t=NT),
                                 rbias[:, :].rearrange("p (o e) -> p o e", o=1).to_broadcast([P, NT, E]), ALU.add))
            for t in range(NT):
                for g in range(NG):
                    last = V.max(g8[:, t, g, :], sel3[:, t, g, :])
            link(last)
            link(V.memset(gs16[:, :, NG:2 * NG], -BIG))
            link(V.tensor_tensor(gs16[:, :, 0:NG], g8[:, :, :, 0], g8[:, :, :, 1], ALU.add))
            for t in range(NT):
                last = V.max(gtop[:, t, :], gs16[:, t, :])
            link(last)
            link(V.memset(gtop[:, :, TG:8], -BIG))
            for t in range(NT):
                last = V.match_replace(gmk[:, t, :], gtop[:, t, :], gs16[:, t, :], MARK)
            link(last)
            link(V.tensor_scalar(gs16[:, :, 0:NG], gmk[:, :, 0:NG], MARK / 3, -BIG, ALU.is_lt, ALU.mult))
            link(V.tensor_tensor(sel3, sel3, gs16[:, :, 0:NG].rearrange("p t (g o) -> p t g o", o=1).to_broadcast([P, NT, NG, GE]), ALU.add))
            for t in range(NT):
                last = V.max(gtop[:, t, :], r_sel[:, E * t:E * t + E])
            link(last)
            for t in range(NT):
                last = V.match_replace(r_mask[:, E * t:E * t + E], gtop[:, t, :], r_sel[:, E * t:E * t + E], MARK)
            link(last)
            V.tensor_scalar(r_mask, r_mask, MARK / 3, None, ALU.is_ge).then_inc(masked, 1)
            dve.wait_ge(masked, 1)
            inf = info.rearrange("p t (e w) -> p t e w", w=2)
            link(V.tensor_tensor(r_sel, r_sc, r_mask, ALU.mult))
            link(V.tensor_reduce(rsm[:, 0:4], r_sel.rearrange("p (t e) -> p t e", t=NT), AX, ALU.add))
            link(V.reciprocal(rsm[:, 4:8], rsm[:, 0:4]))
            link(V.tensor_scalar(rsm[:, 8:12], rsm[:, 4:8], RSCALE, None, ALU.mult))
            link(V.tensor_tensor(inf[:, :, :, 1], r_sel.rearrange("p (t e) -> p t e", t=NT),
                                 rsm[:, 8:12].rearrange("p (t o) -> p t o", o=1).to_broadcast([P, NT, E]), ALU.mult))
            link(V.tensor_copy(inf[:, :, :, 0], con[:, C_IDM:C_IDM + NT].rearrange("p (t o) -> p t o", o=1).to_broadcast([P, NT, E])))

            def times_up(row, ps):
                return V.tensor_tensor(row.rearrange("p (c q) -> p q c", c=2), gw_t.rearrange("p (q c) -> p q c", c=2),
                                       ps[:, FF:2 * FF].rearrange("p (q c) -> p q c", c=2), ALU.mult)

            def shared_hidden(t):
                dve.wait_ge(sh_gu, t + 1)
                dve.wait_ge(sh_sig, t + 1)
                link(V.tensor_tensor(gw_t, PS[t % 2][:, 0:FF], sg_t, ALU.mult))
                times_up(hrow[t % 2], PS[t % 2]).then_inc(sh_h, 1)

            def shared_hT(t):
                dve.wait_ge(sh_tr, t + 1)
                V.tensor_copy(hTe[t % 2], PS[6][:, 0:FF]).then_inc(sh_hT, 1)

            def shared_y(t):
                dve.wait_ge(sh_dn, t + 1)
                if t >= 2:
                    dve.wait_ge(sh_st[t % 2], 16 * (t // 2))
                V.tensor_copy(ysb[t % 2][:, 512:1024], PS[5]).then_inc(sh_yb, 1)

            shared_hidden(0)
            shared_hidden(1)
            dve.wait_ge(pos_mm, 1)
            V.scalar_tensor_tensor(posm, PS[7][:, 0:NT * E], 1.0, r_mask, ALU.add, ALU.mult).then_inc(posm_done, 1)
            cnt = PS[7][:, NT * E:NT * E + E]
            nb, cum, cmp, cmn = gsb[:, 0:E], r_sel[:, 0:E], r_sel[:, E:2 * E], r_sel[:, 2 * E:3 * E]
            link(V.tensor_scalar(nb, cnt, P + 0.5, None, ALU.is_gt))
            link(V.scalar_tensor_tensor(nb, cnt, 2 * P + 0.5, nb, ALU.is_gt, ALU.add))
            link(V.scalar_tensor_tensor(nb, cnt, 3 * P + 0.5, nb, ALU.is_gt, ALU.add))
            link(V.tensor_tensor_scan(cum, nb, nb, 0.0, ALU.add, ALU.max))
            link(V.tensor_scalar(cmp, cum, con[:, C_SLOT:C_SLOT + 1], None, ALU.is_le))
            link(V.tensor_reduce(ovc[:, 0:1], cmp, AX, ALU.add))
            link(V.tensor_tensor(cmn, cmp, nb, ALU.mult))
            link(V.tensor_reduce(ovc[:, 2:3], cmn, AX, ALU.add))
            link(V.tensor_copy(ovcode[0:1, 2 * OV:2 * OV + 1], cum[0:1, E - 1:E]))
            link(V.tensor_scalar(ovc[:, 3:4], ovc[:, 2:3], -1.0, 1.0, ALU.mult, ALU.add))
            V.tensor_tensor(ovc[:, 1:2], ovc[:, 3:4], con[:, C_SLOT:C_SLOT + 1], ALU.add).then_inc(ov_col, 1)

            for t in range(NT):
                shared_hT(t)
                shared_y(t)
                if t + 2 < NT:
                    shared_hidden(t + 2)
            dve.wait_ge(ov_tr, 1)
            V.tensor_copy(ovcode[0:1, 0:2 * OV].rearrange("o (a b) -> o a b", a=2),
                          PS[7][0:1, 0:2 * P].rearrange("o (a b) -> o a b", a=2)[:, :, 0:OV]).then_inc(ov_done, 1)
            V.tensor_scalar(xres[:, :], xres[:, :], ALPHA, None, ALU.mult).then_inc(dve_c, 1)
            n[0] += 1

            def select(e, m):
                if is_int(e) and e >= E:
                    return
                if not (is_int(e) and e == 0):
                    dve.wait_ge(info_mm, e)
                for t in range(NT):
                    last = V.tensor_scalar(selm[:, t, :], con[:, C_IOTA:C_IOTA + P], posm[:, bass.ds(e + t * E, 1)], None, ALU.is_equal)
                last.then_inc(sel_done, 1)

            def indices(e, m):
                if is_int(e) and e >= E:
                    return
                m = m % 4
                dve.wait_ge(info_mm, e + 1)
                V.tensor_copy(iw[:, 2 * m:2 * m + 2], PS[7][:, 0:2])
                V.tensor_scalar(gidx[:, m:m + 1], PS[7][:, 0:1], float(SEQ), None, ALU.add).then_inc(idx_done, 1)

            def hidden(e, m):
                dve.wait_ge(gu_mm, e + 1)
                dve.wait_ge(sig_done, e + 1)
                V.scalar_tensor_tensor(gw_t, PS[m % 2][:, 0:FF], iw[:, 2 * m + 1:2 * m + 2], sg_t, ALU.mult, ALU.mult).then_inc(hid_c, 1)
                dve.wait_ge(hid_c, e + 1)
                times_up(hrow[m % 2], PS[m % 2]).then_inc(h_done, 1)

            def hidden_T(e, m):
                dve.wait_ge(h_tr, e + 1)
                V.tensor_copy(hTe[m % 2], PS[6][:, 0:FF]).then_inc(h_out, 1)

            def rows_out(e, m):
                m = m % 4
                if is_int(e) and e < 2:
                    for w in (*sh_st, sh_pad):
                        dve.wait_ge(w, 16 if w is sh_pad else 8 * NT)
                else:
                    dve.wait_ge(scattered, e * 16 - 16)
                V.tensor_scalar(tcol[:, m % 2:m % 2 + 1], iw[:, 2 * m:2 * m + 1], 0.0, con[:, C_SLOT:C_SLOT + 1], ALU.is_ge, ALU.mult).then_inc(sid_c, 1)
                dve.wait_ge(sid_c, e + 1)
                V.scalar_tensor_tensor(sidx[:, m % 2:m % 2 + 1], iw[:, 2 * m:2 * m + 1], float(SEQ), tcol[:, m % 2:m % 2 + 1], ALU.add, ALU.add)
                dve.wait_ge(dn_mm, e + 1)
                V.tensor_copy(ysb[m % 2][:, 512:1024], PS[5]).then_inc(y_b, 1)

            for e in range(2):
                select(e, e)
                indices(e, e)

            def step(e, m):
                select(e + 2, m + 2)
                if not (is_int(e) and e == 0):
                    hidden_T(e - 1, m + 3)
                indices(e + 2, m + 2)
                hidden(e, m)
                if not (is_int(e) and e == 0):
                    rows_out(e - 1, m + 3)
            each_expert(dve, step)
            hidden_T(E - 1, (E - 1) % 4)
            rows_out(E - 1, (E - 1) % 4)

            dve.wait_ge(scattered, 16 * E)
            dve.wait_ge(ov_done, 1)
            n_over = dve.value_load(ovcode[0:1, 2 * OV:2 * OV + 1], min_val=0, max_val=MAXOVER)
            with dve.Fori(0, MAXOVER) as j:
                with dve.If(j < n_over):
                    dve.wait_ge(ov_turn, j + 1)
                    ex = dve.value_load(ovcode[0:1, bass.ds(j, 1)], min_val=0, max_val=E - 1)
                    part = dve.value_load(ovcode[0:1, bass.ds(j + OV, 1)], min_val=1, max_val=SEQ // P - 1)
                    for t in range(NT):
                        last = V.tensor_scalar(selm[:, t, :], con[:, bass.ds(part * P + C_IOTA, P)], posm[:, bass.ds(ex + t * E, 1)], None, ALU.is_equal)
                    last.then_inc(ov_sel, 1)
                    dve.wait_ge(ov_info, j + 1)
                    V.tensor_copy(iw[:, 0:2], PS[7][:, 0:2]).then_inc(ovd_c, 1)
                    V.tensor_scalar(gidx[:, 0:1], PS[7][:, 0:1], float(SEQ), None, ALU.add)
                    dve.wait_ge(ovd_c, j * 3 + 1)
                    V.tensor_scalar(tcol[:, 0:1], iw[:, 0:1], 0.0, con[:, C_SLOT:C_SLOT + 1], ALU.is_ge, ALU.mult).then_inc(ovd_c, 1)
                    dve.wait_ge(ovd_c, j * 3 + 2)
                    V.scalar_tensor_tensor(sidx[:, 0:1], iw[:, 0:1], float(SEQ), tcol[:, 0:1], ALU.add, ALU.add).then_inc(ov_idx, 1)
                    dve.wait_ge(ov_gu, j + 1)
                    dve.wait_ge(ov_sig, j + 1)
                    V.scalar_tensor_tensor(gw_t, PS[0][:, 0:FF], iw[:, 1:2], sg_t, ALU.mult, ALU.mult).then_inc(ovd_c, 1)
                    dve.wait_ge(ovd_c, j * 3 + 3)
                    times_up(hrow[0], PS[0]).then_inc(ov_h, 1)
                    dve.wait_ge(ov_htr, j + 1)
                    V.tensor_copy(hTe[0], PS[6][:, 0:FF]).then_inc(ov_hT, 1)
                    dve.wait_ge(ov_dn, j + 1)
                    V.tensor_copy(ysb[0][:, 512:1024], PS[5]).then_inc(ov_y, 1)

            def final_in(t):
                z = xm[:, D * t:D * t + D]
                dve.wait_ge(f_acc[t], 16)
                link(V.tensor_tensor(z, z, g2, ALU.mult))
                link(V.tensor_tensor(xrow[:, t, :], xrow[:, t, :], z, ALU.add))
                norm_stats(xrow[:, t, :])
                link(V.tensor_copy(fb[:, 2 * t:2 * t + 1], bnw[:, 14:15]))
                V.scalar_tensor_tensor(fb[:, 2 * t + 1:2 * t + 2], bnw[:, 12:13], -1.0, bnw[:, 14:15], ALU.mult, ALU.mult).then_inc(f_in, 1)

            def final_out(t):
                dve.wait_ge(f_mul, t + 1)
                V.tensor_tensor(xm[:, D * t:D * t + D], xm[:, D * t:D * t + D], ln2[:, D:2 * D], ALU.add).then_inc(f_out, 1)

            dve.wait_ge(ld_ln2, 32)
            for t in range(NT):
                final_in(t)
                if t:
                    final_out(t - 1)
            final_out(NT - 1)


_INS = ['x', 'c', 'ctx', 'c_ctx', 'w_mod', 'b_mod', 'w_in', 'q_norm', 'k_norm', 'pool_w', 'pool_scale', 'w_out',
        'ln1_g', 'ln1_b', 'w_router', 'router_bias', 'w_gate', 'w_up', 'w_down', 'ws_gate', 'ws_up', 'ws_down',
        'ln2_g', 'ln2_b']


def kernel(**inputs):
    import concourse.bacc as _bacc
    from concourse.bass_utils import run_bass_kernel_spmd as _run

    nc = _bacc.Bacc("TRN2", target_bir_lowering=False, num_devices=1)
    arrays, args = {}, {}
    fixed, temp = constants()
    for name, v in [(k, np.ascontiguousarray(inputs[k])) for k in _INS] + [("consts", fixed), ("tempc", temp)]:
        arrays[f"in_{name}_dram"] = v
        args[name] = nc.dram_tensor(f"in_{name}_dram", v.shape, mybir.dt.from_np(v.dtype), kind="ExternalInput").ap()
    out = nc.dram_tensor("out_0_dram", (1, SEQ, D), F32, kind="ExternalOutput").ap()
    build(nc, args, args["consts"], args["tempc"], out)
    r = _run(nc, [arrays], core_ids=[0])
    return r.results[0]["out_0_dram"]
```

```python
from contextlib import ExitStack

import numpy as np

import concourse.bass as bass
from concourse import mybir

F32 = mybir.dt.float32
U32 = mybir.dt.uint32
I32 = mybir.dt.int32
ALU = mybir.AluOpType
ACT = mybir.ActivationFunctionType
AX = mybir.AxisListType.X

P = 128
D = 1024
SEQ = 512
CTX = 256
NT = SEQ // P
NC = CTX // P
DC = D // P
POOLW = 256
WINDOWS = (2, 4, 8, 16)
HD = 64
NH = 12
NKV = 4
GQ = NH // NKV
QW = NH * HD
KW = NKV * HD
PROJ = POOLW + QW + 2 * KW
KEYS = CTX + SEQ
KT = KEYS // P
GRID_W = 64
THETA = 10000.0
E = 64
TOPK = 8
NG = 8
TG = 4
GE = E // NG
FF = 256
RSCALE = 2.5
ALPHA = 2.0 ** 0.25
LN_EPS = 1e-5
RMS_EPS = 1e-6
MODB = (2, 3, 6, 7)
PAD = 16
UP = SEQ + 2 * PAD
BIG = 1.0e30
MARK = 3.0e38
OV = SEQ * TOPK // P
MAXOVER = OV - 1
FEWOVER = 6
ROUNDS = E // 4 - 2

C_ID, C_IOTA, C_UT, C_IDM, C_SLOT = 0, 128, 640, 768, 772
NCONST = 773
T_COS, T_SIN, T_INV = 0, 256, 512
NTEMP = 1536


def constants():
    a = np.zeros((P, NCONST), np.float32)
    a[:, C_ID:C_ID + P] = np.eye(P)
    a[:, C_IOTA:C_IOTA + SEQ] = np.arange(1, SEQ + 1)
    a[:, C_UT:C_UT + P] = np.triu(np.ones((P, P)), 1)
    a[:, C_IDM:C_IDM + NT] = np.arange(P)[:, None] + P * np.arange(NT)[None] - SEQ
    a[:, C_SLOT] = np.arange(P)
    t = np.zeros((P, NTEMP), np.float32)
    ax = HD // 2
    inv = np.float32(THETA) ** (-np.arange(0, ax, 2, dtype=np.float32) / np.float32(ax))
    pos = np.arange(SEQ)
    ang = np.concatenate([(pos // GRID_W).astype(np.float32)[:, None] * inv,
                          (pos % GRID_W).astype(np.float32)[:, None] * inv], axis=-1)
    cos = np.repeat(np.cos(ang), 2, axis=-1)
    sin = np.repeat(np.sin(ang), 2, axis=-1)
    sin[:, 0::2] *= -1
    t[:, T_COS:T_COS + NT * HD] = cos.reshape(NT, P, HD).transpose(1, 0, 2).reshape(P, -1)
    t[:, T_SIN:T_SIN + NT * HD] = sin.reshape(NT, P, HD).transpose(1, 0, 2).reshape(P, -1)
    for g, w in enumerate(WINDOWS):
        n = np.clip(pos + w - w // 2, 0, SEQ) - np.clip(pos - w // 2, 0, SEQ)
        t[HD * (g % 2):HD * (g % 2) + HD, T_INV + SEQ * (g // 2):T_INV + SEQ * (g // 2) + SEQ] = 1.0 / n
    return a, t


class Tile:

    def __init__(self, i, off):
        self.i, self.off = i, off

    def __call__(self, per, c):
        return self.i * per + (self.off * per + c)

    @property
    def cols(self):
        return bass.ds(self(P, 0), P)

    @property
    def before(self):
        return Tile(self.i, self.off - 1)


def build(nc, a, consts, tempc, out):
    h_rows = nc.dram_tensor("h_rows", [SEQ, D], F32, kind="Internal").ap()
    acc_rows = nc.dram_tensor("acc_rows", [SEQ + P, D], F32, kind="Internal").ap()

    ctx = ExitStack()
    with ctx:
        def sb(name, cols, dt=F32):
            return ctx.enter_context(nc.sbuf_tensor(name, [P, cols], dt))

        def sem(name):
            return ctx.enter_context(nc.semaphore(name))

        ring = sb("ring", 20480)
        xres = sb("xres", 4096)
        xm = sb("xm", 4096)
        cm = sb("cm", 2048)
        kq = sb("kq", 6144)
        vr = sb("vr", 1536)
        pmix = sb("pmix", 1024)
        bc = sb("bc", 4096)
        lnr = sb("lnr", 2048)
        att = sb("att", 4352)
        con = sb("con", NCONST)
        ones = sb("ones", P)
        tabs = sb("tabs", 1024)
        pw = sb("pw", 256)
        gains = sb("gains", 2 * HD)
        rbias = sb("rbias", E)
        cvec = sb("cvec", 16)
        csig = sb("csig", 16)
        csil = sb("csil", 16)
        modc = sb("modc", 32)
        pscale = sb("pscale", 2)
        stat = sb("stat", 36)
        negmax = sb("negmax", 2)
        rowsum = sb("rowsum", 2)
        recips = sb("recips", 2)
        gsb = sb("gsb", 64 + 32 + 64)
        bnw = sb("bnw", 16)
        rsm = sb("rsm", 12)
        iw = sb("iw", 8)
        tcol = sb("tcol", 2)
        gidx = sb("gidx", 4, U32)
        sidx = sb("sidx", 2, U32)
        fb = sb("fb", 2 * NT)
        ovc = sb("ovc", 4)
        ovcode = sb("ovcode", 2 * OV + 1, I32)

        ident = con[:, C_ID:C_ID + P]
        wmod_a = [ring[:, 2048 * s:2048 * s + 2048] for s in range(4)]
        wmod_b = [ring[:, 4096 * s:4096 * s + 4096] for s in range(2)]
        wout = ring[:, 0:8192].rearrange("p (c n) -> p c n", c=DC)
        win = ring[:, 8192:20480].rearrange("p (c n) -> p c n", c=DC)
        gu_flat = [ring[:, 4096 + 4096 * s:8192 + 4096 * s] for s in range(4)]
        gu_w = [g.rearrange("p (u c f) -> p u c f", u=2, c=DC) for g in gu_flat]
        dn_flat = [ring[:, 2048 * s:2048 * s + 2048] for s in range(2)]
        dn_w = [g.rearrange("p (c n) -> p c n", c=2) for g in dn_flat]
        xrow = xres[:, :].rearrange("p (t d) -> p t d", t=NT)
        st_n, st_a, st_b, st_q, st_r = (xres[:, 768 * i:768 * i + 768] for i in range(5))
        xmT = xm[:, :].rearrange("p (c t) -> p c t", c=DC)
        mixA = xm[:, 1024:4096].rearrange("p (c t) -> p c t", c=6)
        mixP = pmix[:, :].rearrange("p (c t) -> p c t", c=2)
        lnA = xm[:, 0:1024]
        xg = [xm[:, 0:1024], xm[:, 1024:2048], cm[:, 0:1024], att[:, 0:1024]]
        ysb = [xm[:, 2048:3072], xm[:, 3072:4096]]
        cmT = cm[:, :].rearrange("p (c t) -> p c t", c=DC)
        hperm = cm[:, 0:1024]
        r_sc = cm[:, 1024:1280]
        r_sel = cm[:, 1280:1536]
        r_mask = cm[:, 1536:1792]
        posm = cm[:, 1792:2048]
        mrow = kq[0:2, 0:2048]
        brow_a = kq[0:1, 2048:4096]
        kT = kq[:, 0:3072].rearrange("p (h k) -> p h k", h=NKV)
        qT = kq[:, 3072:6144].rearrange("p (h t) -> p h t", h=6)
        hT = kq[:, 0:4096].rearrange("p (c t) -> p c t", c=DC)
        ws_dn_flat = kq[:, 4096:6144]
        ws_dn = ws_dn_flat.rearrange("p (c n) -> p c n", c=2)
        ln2 = kq[:, 0:2048]
        vall = vr[:, :].rearrange("p (k d) -> p k d", k=KT)
        selm = vr[:, 0:512].rearrange("p (t s) -> p t s", t=NT)
        hrow = [vr[:, 512:768], vr[:, 768:1024]]
        hTe = [vr[:, 1024:1280], vr[:, 1280:1536]]
        gw_t = pmix[:, 0:256]
        sg_t = pmix[:, 256:512]
        xT = [lnr[:, 0:1024], lnr[:, 1024:2048]]
        crow = att[:, 0:2048].rearrange("p (t d) -> p t d", t=NC)
        pU = att[:, 0:2 * UP].rearrange("p (c t) -> p c t", c=2)
        pS2 = att[:, 2 * UP:4 * UP].rearrange("p (c t) -> p c t", c=2)
        pS4 = att[:, 4 * UP:6 * UP].rearrange("p (c t) -> p c t", c=2)
        pS8 = att[:, 6 * UP:7 * UP]
        pS16 = att[:, 7 * UP:8 * UP]
        qcur = cm[:, 0:NH * P].rearrange("p (h t) -> p h t", h=NH)
        prob = [xres[:, 768 * i:768 * i + 768] for i in range(2)]
        prT = [xres[:, 1536 + 768 * i:2304 + 768 * i].rearrange("p (k q) -> p k q", k=KT) for i in range(2)]
        arow = xres[:, 3072:3840]
        ws_gu_flat = att[:, 0:4096]
        ws_gu = ws_gu_flat.rearrange("p (u c f) -> p u c f", u=2, c=DC)
        wrt_flat = tabs[:, 0:512]
        wrt = wrt_flat.rearrange("p (c e) -> p c e", c=DC)
        info = tabs[:, 512:1024].rearrange("p (t n) -> p t n", t=NT)
        g8 = tabs[:, 512:768].rearrange("p (t g m) -> p t g m", t=NT, g=NG)
        gs16 = gsb[:, 0:64].rearrange("p (t g) -> p t g", t=NT)
        gtop = gsb[:, 64:96].rearrange("p (t g) -> p t g", t=NT)
        gmk = gsb[:, 96:160].rearrange("p (t g) -> p t g", t=NT)

        psum = ctx.enter_context(nc.psum_tensor("psum", [P, 8 * 512], F32))
        PS = [psum[:, 512 * b:512 * b + 512] for b in range(8)]
        PS3 = psum[:, :].rearrange("p (b n) -> p b n", b=8)

        ld_const, ld_temp, ld_c, ld_x, ld_ctx, ld_brow = (sem(n) for n in (
            "ld_const", "ld_temp", "ld_c", "ld_x", "ld_ctx", "ld_brow"))
        ld_wa = [sem(f"ld_wa{i}") for i in range(4)]
        ld_wb = [sem(f"ld_wb{i}") for i in range(2)]
        ld_wkv, ld_wqu, ld_small, ld_wout, ld_x2, ld_ln1, ld_ws, ld_ln2, ld_wr = (sem(n) for n in (
            "ld_wkv", "ld_wqu", "ld_small", "ld_wout", "ld_x2", "ld_ln1", "ld_ws", "ld_ln2", "ld_wr"))
        var_in, root_out = sem("var_in"), sem("root_out")
        ld_gu = [sem(f"ld_gu{i}") for i in range(4)]
        ld_dn = [sem(f"ld_dn{i}") for i in range(2)]
        ones_set, pw_zero, bc_zero, ld_bias, alpha_x = (sem(n) for n in ("ones_set", "pw_zero", "bc_zero", "ld_bias", "alpha_x"))
        c_sigmoid, c_silu = sem("c_sigmoid"), sem("c_silu")
        moda_mm, moda_row, moda_tr, moda_col = sem("moda_mm"), sem("moda_row"), sem("moda_tr"), sem("moda_col")
        xtr, xtr_out = sem("xtr"), sem("xtr_out")
        xmod = sem("xmod")
        scaled, gemv, modb_mm, modb_out = sem("scaled"), sem("gemv"), sem("modb_mm"), sem("modb_out")
        tab_done = sem("tab_done")
        kv_mm, kv_sq, kv_v, kv_row, kv_tr, kv_tr_out, kv_free = (sem(n) for n in (
            "kv_mm", "kv_sq", "kv_v", "kv_row", "kv_tr", "kv_tr_out", "kv_free"))
        u_mm, u_out, u_pad, pooled, pool_mm, pool_out = (sem(n) for n in (
            "u_mm", "u_out", "u_pad", "pooled", "pool_mm", "pool_out"))
        q_cur, q_zero, scored, maxed, exped, ptr, ptr_a, ptr_b, pv_mm, o_row, atr, atr_out = (sem(n) for n in (
            "q_cur", "q_zero", "scored", "maxed", "exped", "ptr", "ptr_a", "ptr_b", "pv_mm", "o_row", "atr", "atr_out"))
        out_mm, mix_read, ln1_done, hp_ready, hp_tr, hT_out, h_stored, log_mm = (sem(n) for n in (
            "out_mm", "mix_read", "ln1_done", "hp_ready", "hp_tr", "hT_out", "h_stored", "log_mm"))
        sc_done, masked, pos_mm, posm_done, cnt_mm, ov_col, ov_tr, ov_done = (sem(n) for n in (
            "sc_done", "masked", "pos_mm", "posm_done", "cnt_mm", "ov_col", "ov_tr", "ov_done"))
        sh_gu, sh_sig, sh_h, sh_tr, sh_hT, sh_dn, sh_ya, sh_yb, sh_pad = (sem(n) for n in (
            "sh_gu", "sh_sig", "sh_h", "sh_tr", "sh_hT", "sh_dn", "sh_ya", "sh_yb", "sh_pad"))
        sh_st = [sem("sh_st0"), sem("sh_st1")]
        sel_done, info_mm, idx_done, xg_zero, x_tr, xT_a, gu_mm, sig_done, h_done, h_tr, h_out, dn_mm, y_a, y_b = (
            sem(n) for n in ("sel_done", "info_mm", "idx_done", "xg_zero", "x_tr", "xT_a", "gu_mm",
                             "sig_done", "h_done", "h_tr", "h_out", "dn_mm", "y_a", "y_b"))
        gathered = [sem(f"gathered{i}") for i in range(4)]
        scattered = sem("scattered")
        ov_w, ov_wd, ov_sel, ov_info, ov_idx, ov_gat, ov_xtr, ov_xT, ov_gu, ov_sig, ov_h, ov_htr, ov_hT, ov_dn, ov_y, ov_scat = (
            sem("ov_" + n) for n in ("w", "wd", "sel", "info", "idx", "gat", "xtr", "xT", "gu", "sig", "h", "htr",
                                     "hT", "dn", "y", "scat"))
        ov_turn, row_moves = sem("ov_turn"), sem("row_moves")
        f_acc = [sem(f"f_acc{i}") for i in range(NT)]
        f_st, f_norm, f_out, f_stored = sem("f_st"), sem("f_norm"), sem("f_out"), sem("f_stored")
        dve_c, pool_c, hid_c, sid_c, ovd_c, att_c, f_in, f_mul, sc2_one = (sem(n) for n in (
            "dve_chain", "pool_chain", "hidden_chain", "sidx_chain", "over_chain", "att_chain", "f_in", "f_mul", "sc2_one"))

        x_v = a["x"].rearrange("o (t p) d -> p (o t) d", p=P)
        ctx_v = a["ctx"].rearrange("o (t p) d -> p (o t) d", p=P)
        wmod_v = a["w_mod"].rearrange("o (p k) n -> p (o k) n", k=DC)
        bmod_v = a["b_mod"]
        win_v = a["w_in"].rearrange("o (c p) n -> p (o c) n", p=P)
        wout_v = a["w_out"].rearrange("o (c p) n -> p (o c) n", p=P)
        wr_v = a["w_router"].rearrange("o (p c) e -> p (o c e)", c=DC)
        gate_v = a["w_gate"].rearrange("o e (p c) f -> (o e) p (c f)", c=DC)
        up_v = a["w_up"].rearrange("o e (p c) f -> (o e) p (c f)", c=DC)
        down_v = a["w_down"].rearrange("o e (p c) n -> (o e) p (c n)", c=2)
        wsg_v = a["ws_gate"].rearrange("o (p c) f -> p (o c f)", c=DC)
        wsu_v = a["ws_up"].rearrange("o (p c) f -> p (o c f)", c=DC)
        wsd_v = a["ws_down"].rearrange("o (p c) n -> p (o c n)", c=2)

        def row_bcast(name, lo, hi):
            return a[name][0:1, lo:hi].to_broadcast([P, hi - lo])

        block = ctx.enter_context(nc.Block())

        def each_expert(eng, step):
            for e in range(4):
                step(e, e)
            with eng.Fori(0, ROUNDS) as i:
                for j in range(4):
                    step(i * 4 + (4 + j), j)
            for e in range(4 + 4 * ROUNDS, E):
                step(e, e % 4)

        def each_part(eng, n_over, step):
            with eng.Fori(0, FEWOVER) as j:
                with eng.If(j < n_over):
                    step(j)
            with eng.If(n_over > FEWOVER):
                with eng.Fori(FEWOVER, MAXOVER) as j:
                    with eng.If(j < n_over):
                        step(j)

        def is_int(e):
            return isinstance(e, int)

        def each_tile(eng, step):
            step(Tile(0, 0), True, False)
            with eng.Fori(0, NT - 2) as i:
                step(Tile(i, 1), False, False)
            step(Tile(0, NT - 1), False, True)

        def pair_before(at, u, first):
            if u % 2 == 0 or (first and u == 1):
                return None
            return (at, (u - 3) // 2) if u >= 3 else (at.before, NH // 2 - 1)

        @block.sync
        def _(sp):
            sp.dma_start(con[:, :], consts).then_inc(ld_const, 16)
            sp.dma_start(cvec[:, 0:8], a["c"].rearrange("o (p k) -> p (o k)", k=DC)).then_inc(ld_c, 16)
            sp.dma_start(cvec[:, 8:16], a["c_ctx"].rearrange("(p k) -> p k", k=DC)).then_inc(ld_c, 16)
            sp.dma_start(wmod_a[0], wmod_v[:, 0, 0:2 * D]).then_inc(ld_wa[0], 16)
            sp.dma_start(xres[:, :].rearrange("p (t d) -> p t d", t=NT), x_v).then_inc(ld_x, 16)
            for k in range(1, 4):
                sp.dma_start(wmod_a[k], wmod_v[:, k, 0:2 * D]).then_inc(ld_wa[k], 16)
            sp.dma_start(brow_a, bmod_v[0:1, 0:2 * D]).then_inc(ld_brow, 16)
            sp.dma_start(crow, ctx_v).then_inc(ld_ctx, 16)
            sp.wait_ge(bc_zero, 1)
            sp.dma_start(bc[0:1, :], bmod_v[0:1, 2 * D:6 * D]).then_inc(ld_bias, 16)
            sp.dma_start(lnr[:, 0:NTEMP], tempc).then_inc(ld_temp, 16)
            sp.dma_start(gains[:, 0:HD], row_bcast("q_norm", 0, HD)).then_inc(ld_small, 16)
            sp.dma_start(gains[:, HD:2 * HD], row_bcast("k_norm", 0, HD)).then_inc(ld_small, 16)
            sp.dma_start(rbias[:, :], row_bcast("router_bias", 0, E)).then_inc(ld_small, 16)
            for h in range(2):
                sp.dma_start(pscale[:, h:h + 1], a["pool_scale"][0, P * h:P * h + P].rearrange("(p o) -> p o", o=1)).then_inc(ld_small, 16)
            sp.wait_ge(pw_zero, 1)
            for g in range(4):
                r, col = HD * (g % 2), P * (g // 2) + HD * (g % 2)
                sp.dma_start(pw[r:r + HD, col:col + HD], a["pool_w"][0, g]).then_inc(ld_small, 16)
            for k in range(4, DC):
                sp.wait_ge(moda_mm, k - 3)
                sp.dma_start(wmod_a[k % 4], wmod_v[:, k, 0:2 * D]).then_inc(ld_wa[k % 4], 16)
            sp.dma_start(win[:, :, 1024:PROJ], win_v[:, :, 1024:PROJ]).then_inc(ld_wkv, 16)
            for k in range(DC):
                if k == 2:
                    sp.dma_start(win[:, :, 0:1024], win_v[:, :, 0:1024]).then_inc(ld_wqu, 16)
                if k < 2:
                    sp.wait_ge(moda_mm, 2 * k + 6)
                else:
                    sp.wait_ge(gemv, k - 1)
                sp.dma_start(wmod_b[k % 2], wmod_v[:, k, 2 * D:6 * D]).then_inc(ld_wb[k % 2], 16)
            sp.wait_ge(gemv, DC)
            sp.dma_start(wout, wout_v).then_inc(ld_wout, 16)
            sp.wait_ge(kv_mm, KT + NT)
            sp.wait_ge(u_mm, 2)
            for e in range(3):
                s = (e + 1) % 4
                sp.dma_start(gu_flat[s][:, 0:2048], gate_v[e]).then_inc(ld_gu[s], 16)
                sp.dma_start(gu_flat[s][:, 2048:4096], up_v[e]).then_inc(ld_gu[s], 16)
            sp.wait_ge(kv_tr, KT + NT)
            sp.dma_start(wrt_flat, wr_v).then_inc(ld_wr, 16)
            sp.wait_ge(pooled, 1)
            sp.dma_start(lnr[:, 0:D], row_bcast("ln1_g", 0, D)).then_inc(ld_ln1, 16)
            sp.dma_start(lnr[:, D:2 * D], row_bcast("ln1_b", 0, D)).then_inc(ld_ln1, 16)
            sp.dma_start(ws_gu_flat[:, 0:2048], wsg_v).then_inc(ld_ws, 16)
            sp.dma_start(ws_gu_flat[:, 2048:4096], wsu_v).then_inc(ld_ws, 16)
            sp.wait_ge(atr_out, NH // 2 * NT)
            sp.wait_ge(o_row, NH * NT)
            sp.dma_start(xrow, x_v).then_inc(ld_x2, 16)
            sp.dma_start(ws_dn_flat, wsd_v).then_inc(ld_ws, 16)
            for t in range(NT):
                sp.wait_ge(hp_ready, t + 1)
                sp.dma_start(h_rows[P * t:P * t + P, :], hperm).then_inc(h_stored, 16)
            sp.wait_ge(out_mm, NT)
            for e in range(2):
                sp.dma_start(dn_flat[e], down_v[e]).then_inc(ld_dn[e], 16)
            sp.dma_start(gu_flat[0][:, 0:2048], gate_v[3]).then_inc(ld_gu[0], 16)
            sp.dma_start(gu_flat[0][:, 2048:4096], up_v[3]).then_inc(ld_gu[0], 16)
            for t in range(NT):
                sp.wait_ge(sh_ya, t + 1)
                sp.wait_ge(sh_yb, t + 1)
                sp.dma_start(acc_rows[P * t:P * t + P, :], ysb[t % 2]).then_inc(sh_st[t % 2], 16)
            sp.dma_start(acc_rows[SEQ:SEQ + P, :], ysb[(NT - 1) % 2]).then_inc(sh_pad, 16)
            sp.wait_ge(sh_dn, NT)
            sp.wait_ge(log_mm, NT)
            sp.dma_start(ln2[:, 0:D], row_bcast("ln2_g", 0, D)).then_inc(ld_ln2, 16)
            sp.dma_start(ln2[:, D:2 * D], row_bcast("ln2_b", 0, D)).then_inc(ld_ln2, 16)

            def step(e, m):
                if not (is_int(e) and e + 4 >= E):
                    sp.wait_ge(gu_mm, e + 1)
                    s = (m + 1) % 4
                    sp.dma_start(gu_flat[s][:, 0:2048].rearrange("p (o n) -> p o n", o=1), gate_v[bass.ds(e + 4, 1)].rearrange("o p n -> p o n")).then_inc(ld_gu[s], 16)
                    sp.dma_start(gu_flat[s][:, 2048:4096].rearrange("p (o n) -> p o n", o=1), up_v[bass.ds(e + 4, 1)].rearrange("o p n -> p o n")).then_inc(ld_gu[s], 16)
                if not (is_int(e) and (e == 0 or e + 1 >= E)):
                    sp.wait_ge(dn_mm, e)
                    sp.dma_start(dn_flat[(m + 1) % 2].rearrange("p (o n) -> p o n", o=1), down_v[bass.ds(e + 1, 1)].rearrange("o p n -> p o n")).then_inc(ld_dn[(m + 1) % 2], 16)
            each_expert(sp, step)

            sp.wait_ge(ov_done, 1)
            n_over = sp.value_load(ovcode[0:1, 2 * OV:2 * OV + 1], min_val=0, max_val=MAXOVER)

            def over_gu(ex):
                sp.dma_start(gu_flat[1][:, 0:2048].rearrange("p (o n) -> p o n", o=1), gate_v[bass.ds(ex, 1)].rearrange("o p n -> p o n")).then_inc(ov_w, 16)
                sp.dma_start(gu_flat[1][:, 2048:4096].rearrange("p (o n) -> p o n", o=1), up_v[bass.ds(ex, 1)].rearrange("o p n -> p o n")).then_inc(ov_w, 16)

            def over_dn(ex):
                sp.dma_start(dn_flat[0].rearrange("p (o n) -> p o n", o=1), down_v[bass.ds(ex, 1)].rearrange("o p n -> p o n")).then_inc(ov_wd, 16)

            with sp.If(n_over > 0):
                ex = sp.value_load(ovcode[0:1, 0:1], min_val=0, max_val=E - 1)
                sp.wait_ge(gu_mm, E - 3)
                over_gu(ex)
                sp.wait_ge(dn_mm, E - 1)
                over_dn(ex)

            def part(j):
                with sp.If(j + 1 < n_over):
                    ex = sp.value_load(ovcode[0:1, bass.ds(j + 1, 1)], min_val=0, max_val=E - 1)
                    sp.wait_ge(ov_gu, j + 1)
                    over_gu(ex)
                    sp.wait_ge(ov_dn, j + 1)
                    over_dn(ex)
            each_part(sp, n_over, part)

            sp.wait_ge(f_st, 1)
            for t in range(NT):
                sp.dma_start(xm[:, D * t:D * t + D], acc_rows[P * t:P * t + P, :]).then_inc(f_acc[t], 16)
            for t in range(NT):
                sp.wait_ge(f_out, t + 1)
                sp.dma_start(out[0, P * t:P * t + P, :], xm[:, D * t:D * t + D]).then_inc(f_stored, 16)
            sp.wait_ge(f_stored, 16 * NT)

        @block.gpsimd
        def _(pool):
            n = [0]

            def link(ins):
                n[0] += 1
                ins.then_inc(pool_c, 1)
                pool.wait_ge(pool_c, n[0])

            nc.gpsimd.memset(ones[:, :], 1.0).then_inc(ones_set, 1)
            nc.gpsimd.memset(pw[:, :], 0.0).then_inc(pw_zero, 1)
            nc.gpsimd.memset(bc[:, :], 0.0).then_inc(bc_zero, 1)
            for k in range(DC):
                pool.wait_ge(scaled, k + 1)
                if k == 0:
                    pool.wait_ge(ld_bias, 16)
                else:
                    pool.wait_ge(gemv, k)
                nc.gpsimd.tensor_tensor(bc[:, :], wmod_b[k % 2], bc[:, :], ALU.add).then_inc(gemv, 1)

            pool.wait_ge(u_out, 2)
            pool.wait_ge(u_pad, 2)
            hi = UP
            link(nc.gpsimd.tensor_tensor(pS2[:, :, 1:hi], pU[:, :, 0:hi - 1], pU[:, :, 1:hi], ALU.add))
            link(nc.gpsimd.tensor_tensor(pS4[:, :, 2:hi - 1], pS2[:, :, 1:hi - 2], pS2[:, :, 3:hi], ALU.add))
            link(nc.gpsimd.tensor_tensor(pS8[:, 4:hi - 3], pS4[:, 1, 2:hi - 5], pS4[:, 1, 6:hi - 1], ALU.add))
            link(nc.gpsimd.tensor_tensor(pS16[:, 8:hi - 8], pS8[:, 4:hi - 12], pS8[:, 12:hi - 4], ALU.add))
            inv = lnr[:, T_INV:T_INV + 2 * SEQ].rearrange("p (c t) -> p c t", c=2)
            lo = PAD
            pool.wait_ge(ld_temp, 16)
            for r, c, s in ((0, 0, pS2[:, 0]), (1, 0, pS4[:, 0]), (0, 1, pS8), (1, 1, pS16)):
                rs = slice(HD * r, HD * r + HD)
                link(nc.gpsimd.tensor_tensor(mixP[rs, c, :], s[rs, lo:lo + SEQ], inv[rs, c, :], ALU.mult))
            nc.gpsimd.tensor_tensor(mixP[:, :, :], mixP[:, :, :], pU[:, :, lo:lo + SEQ], ALU.subtract).then_inc(pooled, 1)

            with pool.Fori(0, NT - 1) as t:
                for u in range(NH):
                    r = HD * (u % 2)
                    if u == 0:
                        pool.wait_ge(pooled, 1)
                    pool.wait_ge(q_cur, t * NH + (NH + u))
                    pool.wait_ge(scored, t * NH + (u + 1))
                    nc.gpsimd.tensor_copy(qcur[r:r + HD, u, :], qT[r:r + HD, u // 2, bass.ds(t * P + P, P)]).then_inc(q_cur, 1)

            pool.wait_ge(h_stored, 16 * NT)
            pool.wait_ge(xg_zero, 4)
            pool.wait_ge(hp_ready, NT)

            def gather(e, m):
                if is_int(e) and e >= E:
                    return
                pool.wait_ge(idx_done, e + 1)
                if not (is_int(e) and e < 4):
                    pool.wait_ge(x_tr, e - 3)
                pool.sem_inc(row_moves, 1)
                nc.gpsimd.indirect_dma_start(out=xg[m % 4], out_offset=None, in_=h_rows,
                                             in_offset=bass.IndirectOffsetOnAxis(ap=gidx[:, m % 4:m % 4 + 1], axis=0),
                                             bounds_check=SEQ - 1, oob_is_err=False).then_inc(gathered[m % 4], 16)

            def scatter(e, m):
                pool.wait_ge(y_a, e + 1)
                pool.wait_ge(y_b, e + 1)
                if not (is_int(e) and e == 0):
                    pool.wait_ge(scattered, 16 * e)
                pool.sem_inc(row_moves, 1)
                nc.gpsimd.indirect_dma_start(out=acc_rows,
                                             out_offset=bass.IndirectOffsetOnAxis(ap=sidx[:, m % 2:m % 2 + 1], axis=0),
                                             in_=ysb[m % 2], in_offset=None, bounds_check=SEQ + P - 1,
                                             compute_op=ALU.add).then_inc(scattered, 16)

            for e in range(3):
                gather(e, e)
            nc.gpsimd.tensor_scalar(xres[:, :], xres[:, :], ALPHA, None, ALU.mult).then_inc(alpha_x, 1)
            for w in (*sh_st, sh_pad):
                pool.wait_ge(w, 16 if w is sh_pad else 8 * NT)

            def step(e, m):
                gather(e + 3, m + 3)
                if not (is_int(e) and e == 0):
                    scatter(e - 1, m - 1 + 4)
            each_expert(pool, step)
            scatter(E - 1, (E - 1) % 4)
            pool.wait_ge(ov_done, 1)
            n_over = pool.value_load(ovcode[0:1, 2 * OV:2 * OV + 1], min_val=0, max_val=MAXOVER)

            def over_gather():
                pool.sem_inc(row_moves, 1)
                nc.gpsimd.indirect_dma_start(out=xg[0], out_offset=None, in_=h_rows,
                                             in_offset=bass.IndirectOffsetOnAxis(ap=gidx[:, 0:1], axis=0),
                                             bounds_check=SEQ - 1, oob_is_err=False).then_inc(ov_gat, 16)

            with pool.If(n_over > 0):
                pool.wait_ge(ov_idx, 1)
                over_gather()
            pool.wait_ge(scattered, 16 * E)
            pool.sem_inc(ov_turn, 1)

            def part(j):
                with pool.If(j + 1 < n_over):
                    pool.wait_ge(ov_xtr, j + 1)
                    pool.wait_ge(ov_idx, j + 2)
                    over_gather()
                pool.wait_ge(ov_y, 2 * j + 2)
                pool.sem_inc(row_moves, 1)
                nc.gpsimd.indirect_dma_start(out=acc_rows,
                                             out_offset=bass.IndirectOffsetOnAxis(ap=sidx[:, 0:1], axis=0),
                                             in_=ysb[0], in_offset=None, bounds_check=SEQ + P - 1,
                                             compute_op=ALU.add).then_inc(ov_scat, 16)
                pool.wait_ge(ov_scat, 16 * j + 16)
                pool.sem_inc(ov_turn, 1)
            each_part(pool, n_over, part)
            nc.gpsimd.memset(gidx[:, 0:1], 0).then_inc(f_st, 1)

            for t in range(NT):
                pool.wait_ge(f_norm, t + 1)
                pool.wait_ge(ld_ln2, 32)
                nc.gpsimd.tensor_tensor(xm[:, D * t:D * t + D], xm[:, D * t:D * t + D], ln2[:, 0:D], ALU.mult).then_inc(f_mul, 1)

        @block.scalar
        def _(act):
            act.wait_ge(ld_c, 32)
            nc.scalar.activation(csig[:, :], cvec[:, :], ACT.Sigmoid).then_inc(c_sigmoid, 1)
            for g in range(12):
                act.wait_ge(xtr, g + 1)
                ps = PS[4 + g % 4]
                if g < 8:
                    nc.scalar.activation(xmT[:, g, :], ps[:, :], ACT.Copy).then_inc(xtr_out, 1)
                else:
                    nc.scalar.activation(cmT[:, 2 * (g - 8):2 * (g - 8) + 2, :], ps[:, :].rearrange("p (c t) -> p c t", c=2),
                                         ACT.Copy).then_inc(xtr_out, 1)
            def k_out(j):
                act.wait_ge(kv_tr, j + 1)
                nc.scalar.activation(kT[:, :, P * j:P * j + P], PS[4 + j % 2].rearrange("p (h k) -> p h k", h=NKV),
                                     ACT.Copy).then_inc(kv_tr_out, 1)

            def q_out(i):
                act.wait_ge(kv_tr, KT + i + 1)
                for h in range(2):
                    nc.scalar.activation(qT[:, 3 * h:3 * h + 3, P * i:P * i + P],
                                         PS[4 + h][:, 0:384].rearrange("p (h t) -> p h t", h=3), ACT.Copy).then_inc(kv_tr_out, 1)

            roots = [0]

            def root(row):
                roots[0] += 1
                act.wait_ge(var_in, roots[0])
                nc.scalar.activation(row, row, ACT.Sqrt).then_inc(root_out, 1)

            def scale_wmod(k):
                if k == 0:
                    act.wait_ge(c_silu, 1)
                act.wait_ge(ld_wb[k % 2], 16 * (k // 2 + 1))
                nc.scalar.activation(wmod_b[k % 2], wmod_b[k % 2], ACT.Copy,
                                     scale=csil[:, 2 * k:2 * k + 1]).then_inc(scaled, 1)

            for j in range(KT):
                act.wait_ge(kv_mm, j + 1)
                if j:
                    act.wait_ge(kv_row, j)
                nc.scalar.activation(st_q[:, 0:KW], PS[j % 2][:, 0:KW], ACT.Square).then_inc(kv_sq, 1)
                nc.scalar.activation(vall[:, j, :], PS[j % 2][:, KW:2 * KW], ACT.Copy).then_inc(kv_v, 1)
                root(stat[:, 12:12 + NKV])
                if j:
                    k_out(j - 1)
                if j >= 2:
                    scale_wmod(j - 2)
            k_out(KT - 1)
            scale_wmod(4)
            for i in range(NT):
                act.wait_ge(kv_mm, KT + i + 1)
                act.wait_ge(kv_row, KT + i)
                b = i % 2
                nc.scalar.activation(st_q[:, 0:512], PS[b], ACT.Square).then_inc(kv_v, 1)
                nc.scalar.activation(st_q[:, 512:768], PS[2 + b][:, 0:256], ACT.Square).then_inc(kv_sq, 1)
                if i:
                    q_out(i - 1)
                root(stat[:, 12:12 + NH])
                if 5 + i < DC:
                    scale_wmod(5 + i)
            act.wait_ge(u_mm, 1)
            nc.scalar.activation(pU[:, 0, PAD:PAD + SEQ], PS[6], ACT.Copy).then_inc(u_out, 1)
            q_out(NT - 1)
            act.wait_ge(u_mm, 2)
            nc.scalar.activation(pU[:, 1, PAD:PAD + SEQ], PS[7], ACT.Copy).then_inc(u_out, 1)

            def pair_out(at, pair):
                act.wait_ge(atr, at(NH // 2, pair + 1))
                nc.scalar.activation(mixA[:, pair, at.cols], PS[4][:, 384:512], ACT.Copy).then_inc(atr_out, 1)

            def act_tile(at, first, last):
                for u in range(NH):
                    w = u % 2
                    act.wait_ge(maxed, at(NH, u + 1))
                    if not (first and u < 2):
                        act.wait_ge(ptr, at(2 * NH, 2 * (u - 1)))
                        act.wait_ge(o_row, at(NH, u - 1))
                    nc.scalar.activation(prob[w].rearrange("p (b k) -> p b k", b=2), PS3[:, 2 * w:2 * w + 2, 0:384], ACT.Exp,
                                         bias=negmax[:, w:w + 1], accum_out=rowsum[:, w:w + 1]).then_inc(exped, 1)
                    act.wait_ge(ptr, at(2 * NH, 2 * u + 1))
                    if not (first and u < 2):
                        act.wait_ge(pv_mm, at(NH, u - 1))
                    nc.scalar.activation(prT[w][:, 0:3, :], PS[4][:, 0:384].rearrange("p (k q) -> p k q", k=3),
                                         ACT.Copy).then_inc(ptr_a, 1)
                    if u % 2 and pair_before(at, u, first):
                        pair_out(*pair_before(at, u, first))
                if last:
                    pair_out(at, NH // 2 - 1)
            each_tile(act, act_tile)

            act.wait_ge(ld_small, 16 * 9)
            act.wait_ge(pool_mm, 2)
            for c in range(2):
                nc.scalar.activation(mixP[:, c, :], PS[6 + c], ACT.Copy, scale=pscale[:, c:c + 1]).then_inc(pool_out, 1)
            for q in range(8):
                act.wait_ge(modb_mm, q + 1)
                nc.scalar.activation(bc[:, 512 * q:512 * q + 512], PS[MODB[q % 4]], ACT.Copy).then_inc(modb_out, 1)

            def hT_copy(t):
                for g in range(2):
                    act.wait_ge(hp_tr, 2 * t + g + 1)
                    nc.scalar.activation(hT[:, 4 * g:4 * g + 4, P * t:P * t + P],
                                         PS[2 + g].rearrange("p (c t) -> p c t", c=4), ACT.Copy).then_inc(hT_out, 1)
            root(bnw[:, 15:16])
            for t in range(NT):
                hT_copy(t)
                if t + 1 < NT:
                    root(bnw[:, 15:16])
            act.wait_ge(log_mm, NT)
            act.wait_ge(kv_row, KT + NT)
            nc.scalar.activation(r_sc, PS[7][:, 0:256], ACT.Sigmoid).then_inc(sc_done, 1)

            def shared_sig(t):
                act.wait_ge(sh_gu, t + 1)
                if t:
                    act.wait_ge(sh_h, t)
                nc.scalar.activation(sg_t, PS[t][:, 0:FF], ACT.Sigmoid).then_inc(sh_sig, 1)

            shared_sig(0)
            for t in range(NT):
                if t + 1 < NT:
                    shared_sig(t + 1)
                act.wait_ge(sh_dn, t + 1)
                if t >= 2:
                    act.wait_ge(sh_st[t % 2], 16 * (t // 2))
                nc.scalar.activation(ysb[t % 2][:, 0:512], PS[4], ACT.Copy).then_inc(sh_ya, 1)

            def xT_copy(e, m):
                if is_int(e) and e >= E:
                    return
                if not (is_int(e) and e < 2):
                    act.wait_ge(gu_mm, e - 1)
                for g in range(2):
                    act.wait_ge(x_tr, e + 1)
                    nc.scalar.activation(xT[m % 2][:, 512 * g:512 * g + 512], PS[2 + g], ACT.Copy).then_inc(xT_a, 1)

            def y_copy(e, m):
                act.wait_ge(dn_mm, e + 1)
                if is_int(e) and e < 2:
                    for w in (*sh_st, sh_pad):
                        act.wait_ge(w, 16 if w is sh_pad else 8 * NT)
                else:
                    act.wait_ge(scattered, 16 * (e - 1))
                nc.scalar.activation(ysb[m % 2][:, 0:512], PS[4], ACT.Copy).then_inc(y_a, 1)

            xT_copy(0, 0)

            def step(e, m):
                xT_copy(e + 1, m + 1)
                act.wait_ge(gu_mm, e + 1)
                if not (is_int(e) and e == 0):
                    act.wait_ge(h_done, e)
                nc.scalar.activation(sg_t, PS[m % 2][:, 0:FF], ACT.Sigmoid).then_inc(sig_done, 1)
                if not (is_int(e) and e == 0):
                    y_copy(e - 1, m + 3)
            each_expert(act, step)
            y_copy(E - 1, (E - 1) % 4)

            act.wait_ge(ov_done, 1)
            n_over = act.value_load(ovcode[0:1, 2 * OV:2 * OV + 1], min_val=0, max_val=MAXOVER)

            def part(j):
                act.wait_ge(ov_xtr, j + 1)
                for g in range(2):
                    nc.scalar.activation(xT[0][:, 512 * g:512 * g + 512], PS[2 + g], ACT.Copy).then_inc(ov_xT, 1)
                act.wait_ge(ov_gu, j + 1)
                nc.scalar.activation(sg_t, PS[0][:, 0:FF], ACT.Sigmoid).then_inc(ov_sig, 1)
                act.wait_ge(ov_turn, j + 1)
                act.wait_ge(ov_dn, j + 1)
                nc.scalar.activation(ysb[0][:, 0:512], PS[4], ACT.Copy).then_inc(ov_y, 1)
            each_part(act, n_over, part)

            for t in range(NT):
                root(bnw[:, 15:16])
                act.wait_ge(f_in, t + 1)
                nc.scalar.activation(xm[:, D * t:D * t + D], xrow[:, t, :], ACT.Identity,
                                     bias=fb[:, 2 * t + 1:2 * t + 2], scale=fb[:, 2 * t:2 * t + 1]).then_inc(f_norm, 1)

        @block.tensor
        def _(pe):
            mm = nc.tensor.matmul
            tr = nc.tensor.transpose
            csv = csil[:, :].rearrange("p (k w) -> p k w", w=2)
            pe.wait_ge(ones_set, 1)
            pe.wait_ge(ld_const, 16)

            def mod_a(k):
                if k == 0:
                    pe.wait_ge(c_silu, 1)
                pe.wait_ge(ld_wa[k % 4], 16 * (k // 4 + 1))
                for q in range(4):
                    last = mm(PS[q][0:2, :], csv[:, k, :], wmod_a[k % 4][:, 512 * q:512 * q + 512], start=(k == 0), stop=False)
                last.then_inc(moda_mm, 1)

            def x_transposes(g):
                if g >= 4:
                    pe.wait_ge(xtr_out, g - 3)
                for i in range(4):
                    if g < 8:
                        src = xrow[:, i, P * g:P * g + P]
                    else:
                        c = 2 * (g - 8) + i // 2
                        src = crow[:, i % 2, P * c:P * c + P]
                    last = tr(PS[4 + g % 4][:, P * i:P * i + P], src, ident)
                last.then_inc(xtr, 1)

            mod_a(0)
            pe.wait_ge(ld_x, 16)
            for g in range(8):
                x_transposes(g)
            for k in range(1, 4):
                mod_a(k)
            pe.wait_ge(ld_ctx, 16)
            for g in range(8, 12):
                x_transposes(g)
            for k in range(4, DC):
                mod_a(k)
            pe.wait_ge(ld_brow, 16)
            for q in range(4):
                last = mm(PS[q][0:2, :], ones[0:1, 0:2], brow_a[:, 512 * q:512 * q + 512], start=False, stop=True)
            last.then_inc(moda_mm, 1)
            pe.wait_ge(moda_row, 4)
            pe.wait_ge(xtr_out, 12)
            for i in range(16):
                last = tr(PS[4][:, 2 * i:2 * i + 2], mrow[:, P * i:P * i + P], ident[0:2, 0:2])
            last.then_inc(moda_tr, 1)

            def k_transposes(j):
                pe.wait_ge(kv_row, j + 1)
                if j >= 2:
                    pe.wait_ge(kv_tr_out, j - 1)
                if j < 1:
                    pe.wait_ge(moda_col, 2)
                for h in range(NKV):
                    last = tr(PS[4 + j % 2][:, P * h:P * h + P], st_r[:, P * h:P * h + P], ident)
                last.then_inc(kv_tr, 1)

            def q_transposes(i):
                pe.wait_ge(kv_row, KT + i + 1)
                pe.wait_ge(kv_tr_out, KT + 2 * i)
                for h in range(6):
                    last = tr(PS[4 + h // 3][:, P * (h % 3):P * (h % 3) + P], st_r[:, P * h:P * h + P], ident)
                last.then_inc(kv_tr, 1)

            pe.wait_ge(ld_wkv, 16)
            for j in range(KT):
                if j < 2:
                    pe.wait_ge(moda_row, 4)
                else:
                    pe.wait_ge(kv_v, j - 1)
                    pe.wait_ge(kv_row, j - 1)
                for k in range(DC):
                    if j == 0:
                        pe.wait_ge(xmod, k + 1)
                    if j == NC:
                        pe.wait_ge(xmod, DC + k + 1)
                    lhs = cmT[:, k, P * j:P * j + P] if j < NC else xmT[:, k, P * (j - NC):P * (j - NC) + P]
                    last = mm(PS[j % 2], lhs, win[:, k, 1024:PROJ], start=(k == 0), stop=(k == DC - 1))
                last.then_inc(kv_mm, 1)
                if j:
                    k_transposes(j - 1)
            pe.wait_ge(ld_wqu, 16)
            k_transposes(KT - 1)
            for i in range(NT):
                if i < 2:
                    pe.wait_ge(kv_v, KT - 1 + i)
                    pe.wait_ge(kv_sq, KT - 1 + i)
                    pe.wait_ge(kv_row, KT - 1 + i)
                else:
                    pe.wait_ge(kv_row, KT + i - 1)
                for k in range(DC):
                    mm(PS[i % 2], xmT[:, k, P * i:P * i + P], win[:, k, 256:768], start=(k == 0), stop=(k == DC - 1))
                for k in range(DC):
                    last = mm(PS[2 + i % 2][:, 0:256], xmT[:, k, P * i:P * i + P], win[:, k, 768:1024], start=(k == 0), stop=(k == DC - 1))
                last.then_inc(kv_mm, 1)
                if i:
                    q_transposes(i - 1)
            for c in range(2):
                for k in range(DC):
                    last = mm(PS[6 + c], win[:, k, P * c:P * c + P], xmT[:, k, :], start=(k == 0), stop=(k == DC - 1))
                last.then_inc(u_mm, 1)
                if c == 0:
                    q_transposes(NT - 1)
            pe.wait_ge(kv_tr_out, KT + 2 * NT)
            pe.wait_ge(u_out, 2)

            def scores(at, u, first):
                pe.wait_ge(q_cur, NH if first else at(NH, u + 1))
                if not (first and u < 2):
                    pe.wait_ge(exped, at(NH, u - 1))
                for b in range(2):
                    last = mm(PS[2 * (u % 2) + b][:, 0:384], qcur[:, u, :], kT[:, u // GQ, 384 * b:384 * b + 384],
                              start=True, stop=True)
                last.then_inc(scored, 1)

            def pair_transpose(at, pair):
                pe.wait_ge(o_row, at(NH, 2 * pair + 2))
                tr(PS[4][:, 384:512], arow[:, P * pair:P * pair + P], ident).then_inc(atr, 1)

            def prob_transposes(at, u, first):
                pe.wait_ge(exped, at(NH, u + 1))
                for b in range(2):
                    if not (first and u == 0):
                        pe.wait_ge((ptr_a, ptr_b)[b], at(NH, u))
                    if b == 0:
                        if u % 2 == 0 and not (first and u <= 2):
                            pe.wait_ge(atr_out, at(NH // 2, u // 2 - 1))
                        pair = pair_before(at, u, first)
                        if pair:
                            pair_transpose(*pair)
                    for k in range(3):
                        last = tr(PS[4 + b][:, P * k:P * k + P], prob[u % 2][:, P * (3 * b + k):P * (3 * b + k) + P], ident)
                    last.then_inc(ptr, 1)

            def values(at, u, first):
                pe.wait_ge(ptr_a, at(NH, u + 1))
                pe.wait_ge(ptr_b, at(NH, u + 1))
                if not (first and u < 2):
                    pe.wait_ge(o_row, at(NH, u - 1))
                v = HD * (u // GQ)
                for k in range(KT):
                    last = mm(PS[6 + u % 2][:, 0:HD], prT[u % 2][:, k, :], vall[:, k, v:v + HD], start=(k == 0), stop=(k == KT - 1))
                last.then_inc(pv_mm, 1)

            def pe_tile(at, first, last):
                if first:
                    scores(at, 0, True)
                for u in range(NH):
                    if u + 1 < NH:
                        scores(at, u + 1, first)
                    elif not last:
                        scores(Tile(at.i, at.off + 1), 0, False)
                    if u:
                        values(at, u - 1, first)
                    elif not first:
                        values(at.before, NH - 1, False)
                    prob_transposes(at, u, first)
                if last:
                    values(at, NH - 1, False)
                    pe.wait_ge(atr_out, at(NH // 2, NH // 2 - 1))
                    pair_transpose(at, NH // 2 - 1)
            each_tile(pe, pe_tile)
            pe.wait_ge(atr_out, NH // 2 * NT)

            pe.wait_ge(pooled, 1)
            pe.wait_ge(ld_small, 16 * 9)
            for c in range(2):
                mm(PS[6 + c], pw[:, P * c:P * c + P], mixP[:, c, :], start=True, stop=True).then_inc(pool_mm, 1)
            pe.wait_ge(gemv, DC)
            for q in range(8):
                if q == 2:
                    pe.wait_ge(pool_out, 2)
                if q >= 4:
                    pe.wait_ge(modb_out, q - 3)
                mm(PS[MODB[q % 4]], ones[:, :], bc[:, 512 * q:512 * q + 512], start=True, stop=True).then_inc(modb_mm, 1)
            pe.wait_ge(modb_out, 8)

            pe.wait_ge(ld_wout, 16)

            def out_proj(t):
                if t >= 2:
                    pe.wait_ge(mix_read, t - 1)
                b = 4 * (t % 2)
                for q in range(2):
                    for c in range(DC):
                        lhs = mixP[:, c, P * t:P * t + P] if c < 2 else mixA[:, c - 2, P * t:P * t + P]
                        last = mm(PS[b + q], lhs, wout[:, c, 512 * q:512 * q + 512], start=(c == 0), stop=(c == DC - 1))
                last.then_inc(out_mm, 1)

            def h_transposes(t):
                pe.wait_ge(hp_ready, t + 1)
                if t:
                    pe.wait_ge(hT_out, 2 * t)
                for g in range(2):
                    for i in range(4):
                        c = 4 * g + i
                        last = tr(PS[2 + g][:, P * i:P * i + P], hperm[:, P * c:P * c + P], ident)
                    last.then_inc(hp_tr, 1)

            def logits(t):
                pe.wait_ge(hT_out, 2 * t + 2)
                if t == 0:
                    pe.wait_ge(ld_wr, 16)
                for c in range(DC):
                    last = mm(PS[7][:, E * t:E * t + E], hT[:, c, P * t:P * t + P], wrt[:, c, :], start=(c == 0), stop=(c == DC - 1))
                last.then_inc(log_mm, 1)

            def swiglu_in(bank, lhs, w):
                for c in range(DC):
                    last = mm(PS[bank].rearrange("p (u f) -> p u f", u=2), lhs(c), w[:, :, c, :], start=(c == 0), stop=(c == DC - 1))
                return last

            def swiglu_out(lhs, w):
                for q in range(2):
                    for c in range(2):
                        last = mm(PS[4 + q], lhs[:, P * c:P * c + P], w[:, c, 512 * q:512 * q + 512], start=(c == 0), stop=(c == 1))
                return last

            def positions():
                pe.wait_ge(masked, 1)
                for t in range(NT):
                    for s in range(t + 1):
                        last = mm(PS[7][:, E * t:E * t + E], con[:, C_UT:C_UT + P] if s == t else ones[:, :],
                                  r_mask[:, E * s:E * s + E], start=(s == 0), stop=(s == t))
                for s in range(NT):
                    last = mm(PS[7][:, 4 * E:5 * E], ones[:, :], r_mask[:, E * s:E * s + E], start=(s == 0), stop=(s == NT - 1))
                last.then_inc(pos_mm, 1)

            def shared_in(t):
                swiglu_in(t, lambda c: hT[:, c, P * t:P * t + P], ws_gu).then_inc(sh_gu, 1)

            def shared_out(t):
                pe.wait_ge(sh_h, t + 1)
                if t:
                    pe.wait_ge(sh_hT, t)
                for c in range(2):
                    last = tr(PS[6][:, P * c:P * c + P], hrow[t % 2][:, P * c:P * c + P], ident)
                last.then_inc(sh_tr, 1)
                pe.wait_ge(sh_hT, t + 1)
                if t:
                    pe.wait_ge(sh_ya, t)
                    pe.wait_ge(sh_yb, t)
                swiglu_out(hTe[t % 2], ws_dn).then_inc(sh_dn, 1)

            def over_rows():
                pe.wait_ge(ov_col, 1)
                pe.wait_ge(posm_done, 1)
                tr(PS[7][0:1, 0:P], ovc[:, 0:1], ident)
                tr(PS[7][0:1, P:2 * P], ovc[:, 1:2], ident).then_inc(ov_tr, 1)

            out_proj(0)
            for t in range(NT):
                if t + 1 < NT:
                    out_proj(t + 1)
                else:
                    pe.wait_ge(ld_ws, 48)
                    pe.wait_ge(mix_read, NT - 1)
                    shared_in(0)
                h_transposes(t)
                logits(t)
            shared_in(1)
            pe.wait_ge(hT_out, 2 * NT)
            pe.wait_ge(mix_read, NT)
            for t in range(2, NT):
                shared_in(t)
            positions()

            def list_info(e, m):
                if is_int(e) and e >= E:
                    return
                pe.wait_ge(sel_done, e + 1)
                if not (is_int(e) and e == 0):
                    pe.wait_ge(idx_done, e)
                for t in range(NT):
                    last = mm(PS[7][:, 0:2], selm[:, t, :], info[:, t, bass.ds(e * 2, 2)], start=(t == 0), stop=(t == NT - 1))
                last.then_inc(info_mm, 1)

            def row_transposes(e, m):
                if is_int(e) and e >= E:
                    return
                pe.wait_ge(gathered[m % 4], slot_count(e, m, 16))
                if not (is_int(e) and e == 0):
                    pe.wait_ge(xT_a, e * 2)
                for c in range(DC):
                    last = tr(PS[2 + c // 4][:, P * (c % 4):P * (c % 4) + P], xg[m % 4][:, P * c:P * c + P], ident)
                last.then_inc(x_tr, 1)

            def slot_count(e, m, per):
                return (e - m % 4) * (per // 4) + per

            def hidden_transposes(e, m):
                pe.wait_ge(h_done, e + 1)
                if not (is_int(e) and e == 0):
                    pe.wait_ge(h_out, e)
                for c in range(2):
                    last = tr(PS[6][:, P * c:P * c + P], hrow[m % 2][:, P * c:P * c + P], ident)
                last.then_inc(h_tr, 1)

            def down(e, m):
                pe.wait_ge(h_out, e + 1)
                if not (is_int(e) and e == 0):
                    pe.wait_ge(y_a, e)
                    pe.wait_ge(y_b, e)
                pe.wait_ge(ld_dn[m % 2], (e * 8 + (16 if m % 2 == 0 else 8)))
                swiglu_out(hTe[m % 2], dn_w[m % 2]).then_inc(dn_mm, 1)

            for t in range(NT):
                shared_out(t)
                if t == 0:
                    over_rows()
                    pe.wait_ge(ov_done, 1)
                else:
                    list_info(t - 1, t - 1)
            row_transposes(0, 0)

            def step(e, m):
                row_transposes(e + 1, m + 1)
                if not (is_int(e) and e == 0):
                    hidden_transposes(e - 1, m + 3)
                pe.wait_ge(xT_a, e * 2 + 2)
                pe.wait_ge(ld_gu[(m + 1) % 4], slot_count(e, m, 32))
                if not (is_int(e) and e < 2):
                    pe.wait_ge(h_done, e - 1)
                swiglu_in(m % 2, lambda c: xT[m % 2][:, P * c:P * c + P], gu_w[(m + 1) % 4]).then_inc(gu_mm, 1)
                list_info(e + 3, m + 3)
                if not (is_int(e) and e == 0):
                    down(e - 1, m + 3)
            each_expert(pe, step)
            hidden_transposes(E - 1, (E - 1) % 4)
            down(E - 1, (E - 1) % 4)

            pe.wait_ge(y_a, E)
            pe.wait_ge(y_b, E)
            n_over = pe.value_load(ovcode[0:1, 2 * OV:2 * OV + 1], min_val=0, max_val=MAXOVER)

            def over_info(ex):
                for t in range(NT):
                    last = mm(PS[7][:, 0:2], selm[:, t, :], info[:, t, bass.ds(ex * 2, 2)], start=(t == 0), stop=(t == NT - 1))
                last.then_inc(ov_info, 1)

            with pe.If(n_over > 0):
                ex = pe.value_load(ovcode[0:1, 0:1], min_val=0, max_val=E - 1)
                pe.wait_ge(ov_sel, 1)
                over_info(ex)

            def part(j):
                pe.wait_ge(ov_gat, 16 * j + 16)
                for c in range(DC):
                    last = tr(PS[2 + c // 4][:, P * (c % 4):P * (c % 4) + P], xg[0][:, P * c:P * c + P], ident)
                last.then_inc(ov_xtr, 1)
                with pe.If(j + 1 < n_over):
                    ex = pe.value_load(ovcode[0:1, bass.ds(j + 1, 1)], min_val=0, max_val=E - 1)
                    pe.wait_ge(ov_sel, j + 2)
                    pe.wait_ge(ov_idx, j + 1)
                    over_info(ex)
                pe.wait_ge(ov_xT, 2 * j + 2)
                pe.wait_ge(ov_w, 32 * j + 32)
                swiglu_in(0, lambda c: xT[0][:, P * c:P * c + P], gu_w[1]).then_inc(ov_gu, 1)
                pe.wait_ge(ov_h, j + 1)
                for c in range(2):
                    last = tr(PS[6][:, P * c:P * c + P], hrow[0][:, P * c:P * c + P], ident)
                last.then_inc(ov_htr, 1)
                pe.wait_ge(ov_hT, j + 1)
                pe.wait_ge(ov_wd, 16 * j + 16)
                swiglu_out(hTe[0], dn_w[0]).then_inc(ov_dn, 1)
                pe.wait_ge(ov_y, 2 * j + 2)
            each_part(pe, n_over, part)

        @block.vector
        def _(dve):
            V = nc.vector
            n = [0]

            def link(ins):
                n[0] += 1
                ins.then_inc(dve_c, 1)
                dve.wait_ge(dve_c, n[0])

            csv = csil[:, :].rearrange("p (k w) -> p w k", w=2)
            dve.wait_ge(c_sigmoid, 1)
            V.tensor_tensor(csv, cvec[:, :].rearrange("p (w k) -> p w k", w=2), csig[:, :].rearrange("p (w k) -> p w k", w=2),
                            ALU.mult).then_inc(c_silu, 1)
            dve.wait_ge(ld_temp, 16)
            dve.wait_ge(ld_small, 16 * 9)
            cosv = lnr[:, T_COS:T_COS + 256].rearrange("p (t i w) -> p t i w", t=NT, w=2)
            sinv = lnr[:, T_SIN:T_SIN + 256].rearrange("p (t i w) -> p t i w", t=NT, w=2)
            for s in range(2):
                g = gains[:, HD * s:HD * s + HD].rearrange("p (o i w) -> p o i w", o=1, w=2)
                sc = HD ** -0.5 if s == 0 else 1.0
                for o in range(2):
                    tv = tabs[:, 512 * s + 256 * o:512 * s + 256 * o + 256].rearrange("p (t i w) -> p t i w", t=NT, w=2)
                    src = sinv if o else cosv
                    for w in range(2):
                        gw = g[:, :, :, (w + o) % 2].to_broadcast([P, NT, HD // 2])
                        V.scalar_tensor_tensor(tv[:, :, :, w], src[:, :, :, w], sc, gw, ALU.mult, ALU.mult).then_inc(tab_done, 1)
            dve.wait_ge(moda_mm, DC + 1)
            for q in range(4):
                V.tensor_copy(mrow[:, 512 * q:512 * q + 512], PS[q][0:2, :]).then_inc(moda_row, 1)
            dve.wait_ge(moda_tr, 1)
            V.tensor_copy(modc[:, 0:16], PS[4][:, 0:16]).then_inc(moda_col, 1)
            V.tensor_scalar(modc[:, 16:32], PS[4][:, 16:32], 1.0, None, ALU.add).then_inc(moda_col, 1)
            dve.wait_ge(moda_col, 2)
            mc = modc[:, :].rearrange("p (s k w) -> p s k w", s=2, w=2)
            for k in range(DC):
                V.tensor_scalar(cmT[:, k, :], cmT[:, k, :], mc[:, 1, k, 1:2], mc[:, 0, k, 1:2], ALU.mult, ALU.add).then_inc(xmod, 1)
            for k in range(DC):
                V.tensor_scalar(xmT[:, k, :], xmT[:, k, :], mc[:, 1, k, 0:1], mc[:, 0, k, 0:1], ALU.mult, ALU.add).then_inc(xmod, 1)
            dve.wait_ge(tab_done, 8)

            norms = [0]

            def rstd(heads):
                ss, ms, rs = stat[:, 0:heads], stat[:, 12:12 + heads], stat[:, 24:24 + heads]
                link(V.tensor_reduce(ss, st_q[:, 0:HD * heads].rearrange("p (h d) -> p h d", d=HD), AX, ALU.add))
                V.tensor_scalar(ms, ss, 1.0 / HD, RMS_EPS, ALU.mult, ALU.add).then_inc(var_in, 1)
                norms[0] += 1
                dve.wait_ge(root_out, norms[0])
                link(V.reciprocal(rs, ms))
                return rs

            def rotate(heads, s, t):
                nv = st_n[:, 0:HD * heads].rearrange("p (h i w) -> p h i w", h=heads, w=2)
                bv = st_b[:, 0:HD * heads].rearrange("p (h i w) -> p h i w", h=heads, w=2)
                C = tabs[:, 512 * s + HD * t:512 * s + HD * t + HD]
                S = tabs[:, 512 * s + 256 + HD * t:512 * s + 256 + HD * t + HD].rearrange("p (o i w) -> p o i w", o=1, w=2)
                V.tensor_tensor(st_a[:, 0:HD * heads].rearrange("p (h d) -> p h d", h=heads), st_n[:, 0:HD * heads].rearrange("p (h d) -> p h d", h=heads),
                                C.rearrange("p (o d) -> p o d", o=1).to_broadcast([P, heads, HD]), ALU.mult).then_inc(dve_c, 1)
                for w in range(2):
                    V.tensor_tensor(bv[:, :, :, w], nv[:, :, :, 1 - w], S[:, :, :, w].to_broadcast([P, heads, HD // 2]),
                                    ALU.mult).then_inc(dve_c, 1)
                n[0] += 3
                dve.wait_ge(dve_c, n[0])

            for j in range(KT):
                dve.wait_ge(kv_sq, j + 1)
                rs = rstd(NKV)
                dup = st_r[:, 0:512].rearrange("p (h r d) -> p h r d", h=NKV, r=2)
                link(V.tensor_tensor(st_n[:, 0:KW].rearrange("p (h d) -> p h d", h=NKV), PS[j % 2][:, 0:KW].rearrange("p (h d) -> p h d", h=NKV),
                                     rs.rearrange("p (h o) -> p h o", o=1).to_broadcast([P, NKV, HD]), ALU.mult))
                if j:
                    dve.wait_ge(kv_tr, j)
                if j < NC:
                    for r in range(2):
                        last = V.tensor_tensor(dup[:, :, r, :], st_n[:, 0:KW].rearrange("p (h d) -> p h d", h=NKV),
                                               gains[:, HD:2 * HD].rearrange("p (o d) -> p o d", o=1).to_broadcast([P, NKV, HD]), ALU.mult)
                        if r == 0:
                            last.then_inc(dve_c, 1)
                            n[0] += 1
                    last.then_inc(kv_row, 1)
                else:
                    rotate(NKV, 1, j - NC)
                    for r in range(2):
                        last = V.tensor_tensor(dup[:, :, r, :], st_a[:, 0:KW].rearrange("p (h d) -> p h d", h=NKV),
                                               st_b[:, 0:KW].rearrange("p (h d) -> p h d", h=NKV), ALU.add)
                        if r == 0:
                            last.then_inc(dve_c, 1)
                            n[0] += 1
                    last.then_inc(kv_row, 1)
                dve.wait_ge(kv_row, j + 1)
                dve.wait_ge(dve_c, n[0])
            dve.wait_ge(xtr_out, 12)
            V.memset(pU[:, :, 0:PAD], 0.0).then_inc(u_pad, 1)
            V.memset(pU[:, :, PAD + SEQ:UP], 0.0).then_inc(u_pad, 1)
            dve.wait_ge(kv_mm, NC)
            V.memset(qcur, 0.0).then_inc(q_zero, 1)
            for i in range(NT):
                dve.wait_ge(kv_sq, KT + i + 1)
                dve.wait_ge(kv_v, KT + i + 1)
                rb = rstd(NH).rearrange("p (h o) -> p h o", o=1)
                link(V.tensor_tensor(st_n[:, 0:512].rearrange("p (h d) -> p h d", h=8), PS[i % 2].rearrange("p (h d) -> p h d", h=8),
                                     rb[:, 0:8, :].to_broadcast([P, 8, HD]), ALU.mult))
                link(V.tensor_tensor(st_n[:, 512:768].rearrange("p (h d) -> p h d", h=4), PS[2 + i % 2][:, 0:256].rearrange("p (h d) -> p h d", h=4),
                                     rb[:, 8:12, :].to_broadcast([P, 4, HD]), ALU.mult))
                rotate(NH, 0, i)
                dve.wait_ge(kv_tr, KT + i)
                V.tensor_tensor(st_r, st_a, st_b, ALU.add).then_inc(kv_row, 1)
                dve.wait_ge(kv_row, KT + i + 1)

            dve.wait_ge(kv_tr_out, KT + 2 * NT)
            for r in range(2):
                dve.wait_ge(q_zero, 1)
                V.tensor_copy(qcur[HD * r:HD * r + HD].rearrange("p (h r) t -> p r h t", r=2)[:, r], qT[HD * r:HD * r + HD, :, 0:P]).then_inc(q_cur, NH // 2)

            def row_max(at, u, first):
                dve.wait_ge(scored, at(NH, u + 1))
                if not (first and u < 2):
                    dve.wait_ge(exped, at(NH, u - 1))
                w = u % 2
                V.tensor_reduce(negmax[:, w:w + 1], PS3[:, 2 * w:2 * w + 2, 0:384], mybir.AxisListType.XY, ALU.max,
                                negate=True).then_inc(maxed, 1)

            def out_row(at, u, first):
                w = u % 2
                dve.wait_ge(pv_mm, at(NH, u + 1))
                V.reciprocal(recips[:, w:w + 1], rowsum[:, w:w + 1]).then_inc(att_c, 1)
                dve.wait_ge(att_c, at(NH, u + 1))
                if not first:
                    dve.wait_ge(atr, at(NH // 2, u // 2 + 1 - NH // 2))
                V.tensor_scalar(arow[:, HD * u:HD * u + HD], PS[6 + w][:, 0:HD], recips[:, w:w + 1], None, ALU.mult).then_inc(o_row, 1)

            def half_b(at, u, first):
                dve.wait_ge(ptr, at(2 * NH, 2 * u + 2))
                if not (first and u < 2):
                    dve.wait_ge(pv_mm, at(NH, u - 1))
                V.tensor_copy(prT[u % 2][:, 3:6, :], PS[5][:, 0:384].rearrange("p (k q) -> p k q", k=3)).then_inc(ptr_b, 1)

            def dve_tile(at, first, last):
                if first:
                    row_max(at, 0, True)
                for u in range(NH):
                    if u + 1 < NH:
                        row_max(at, u + 1, first)
                    elif not last:
                        row_max(Tile(at.i, at.off + 1), 0, False)
                    if u:
                        out_row(at, u - 1, first)
                    elif not first:
                        out_row(at.before, NH - 1, False)
                    half_b(at, u, first)
                if last:
                    out_row(at, NH - 1, False)
            each_tile(dve, dve_tile)

            dve.wait_ge(modb_out, 8)
            g1, sh2, sc2, g2 = (bc[:, D * i:D * i + D] for i in range(4))
            link(V.tensor_scalar(sc2, sc2, 1.0, None, ALU.add))
            dve.wait_ge(ld_x2, 16)
            dve.wait_ge(ld_ln1, 32)

            def norm_stats(row):
                for h in range(2):
                    V.bn_stats(bnw[:, 6 * h:6 * h + 6], row[:, 512 * h:512 * h + 512]).then_inc(dve_c, 1)
                n[0] += 2
                dve.wait_ge(dve_c, n[0])
                link(V.bn_aggr(bnw[:, 12:14], bnw[:, 0:12].rearrange("p (c s) -> p c s", c=2)))
                V.tensor_scalar(bnw[:, 15:16], bnw[:, 13:14], LN_EPS, None, ALU.add).then_inc(var_in, 1)
                norms[0] += 1
                dve.wait_ge(root_out, norms[0])
                link(V.reciprocal(bnw[:, 14:15], bnw[:, 15:16]))

            for t in range(NT):
                xr = xrow[:, t, :]
                b = 4 * (t % 2)
                dve.wait_ge(out_mm, t + 1)
                if t:
                    dve.wait_ge(hp_ready, t)
                V.tensor_tensor(lnA.rearrange("p (b n) -> p b n", b=2), PS3[:, b:b + 2, :], g1.rearrange("p (b n) -> p b n", b=2),
                                ALU.mult).then_inc(mix_read, 1)
                dve.wait_ge(mix_read, t + 1)
                link(V.scalar_tensor_tensor(xr, xr, ALPHA, lnA, ALU.mult, ALU.add))
                norm_stats(xr)
                link(V.tensor_scalar(xr, xr, bnw[:, 12:13], bnw[:, 14:15], ALU.subtract, ALU.mult))
                link(V.tensor_tensor(xr, xr, lnr[:, 0:D], ALU.mult))
                link(V.tensor_tensor(xr, xr, lnr[:, D:2 * D], ALU.add))
                link(V.tensor_tensor(lnA, xr, sc2, ALU.mult))
                if t:
                    dve.wait_ge(hp_tr, 2 * t)
                    dve.wait_ge(h_stored, 16 * t)
                V.tensor_tensor(hperm.rearrange("p (c q) -> p q c", c=DC), lnA.rearrange("p (q c) -> p q c", c=DC),
                                sh2.rearrange("p (q c) -> p q c", c=DC), ALU.add).then_inc(hp_ready, 1)
            dve.wait_ge(hp_ready, NT)
            V.memset(xg[0], 0.0).then_inc(xg_zero, 1)
            V.memset(xg[1], 0.0).then_inc(xg_zero, 1)

            sel3 = r_sel.rearrange("p (t g m) -> p t g m", t=NT, g=NG)
            dve.wait_ge(sc_done, 1)
            dve.wait_ge(ld_small, 16 * 9)
            link(V.tensor_tensor(r_sel.rearrange("p (t e) -> p t e", t=NT), r_sc.rearrange("p (t e) -> p t e", t=NT),
                                 rbias[:, :].rearrange("p (o e) -> p o e", o=1).to_broadcast([P, NT, E]), ALU.add))
            for t in range(NT):
                for g in range(NG):
                    last = V.max(g8[:, t, g, :], sel3[:, t, g, :])
            link(last)
            link(V.memset(gs16[:, :, NG:2 * NG], -BIG))
            link(V.tensor_tensor(gs16[:, :, 0:NG], g8[:, :, :, 0], g8[:, :, :, 1], ALU.add))
            for t in range(NT):
                last = V.max(gtop[:, t, :], gs16[:, t, :])
            link(last)
            link(V.memset(gtop[:, :, TG:8], -BIG))
            for t in range(NT):
                last = V.match_replace(gmk[:, t, :], gtop[:, t, :], gs16[:, t, :], MARK)
            link(last)
            link(V.tensor_scalar(gs16[:, :, 0:NG], gmk[:, :, 0:NG], MARK / 3, -BIG, ALU.is_lt, ALU.mult))
            link(V.tensor_tensor(sel3, sel3, gs16[:, :, 0:NG].rearrange("p t (g o) -> p t g o", o=1).to_broadcast([P, NT, NG, GE]), ALU.add))
            for t in range(NT):
                last = V.max(gtop[:, t, :], r_sel[:, E * t:E * t + E])
            link(last)
            for t in range(NT):
                last = V.match_replace(r_mask[:, E * t:E * t + E], gtop[:, t, :], r_sel[:, E * t:E * t + E], MARK)
            link(last)
            V.tensor_scalar(r_mask, r_mask, MARK / 3, None, ALU.is_ge).then_inc(masked, 1)
            dve.wait_ge(masked, 1)
            inf = info.rearrange("p t (e w) -> p t e w", w=2)
            link(V.tensor_tensor(r_sel, r_sc, r_mask, ALU.mult))
            link(V.tensor_reduce(rsm[:, 0:4], r_sel.rearrange("p (t e) -> p t e", t=NT), AX, ALU.add))
            link(V.reciprocal(rsm[:, 4:8], rsm[:, 0:4]))
            link(V.tensor_scalar(rsm[:, 8:12], rsm[:, 4:8], RSCALE, None, ALU.mult))
            link(V.tensor_tensor(inf[:, :, :, 1], r_sel.rearrange("p (t e) -> p t e", t=NT),
                                 rsm[:, 8:12].rearrange("p (t o) -> p t o", o=1).to_broadcast([P, NT, E]), ALU.mult))
            link(V.tensor_copy(inf[:, :, :, 0], con[:, C_IDM:C_IDM + NT].rearrange("p (t o) -> p t o", o=1).to_broadcast([P, NT, E])))

            def times_up(row, ps):
                return V.tensor_tensor(row.rearrange("p (c q) -> p q c", c=2), gw_t.rearrange("p (q c) -> p q c", c=2),
                                       ps[:, FF:2 * FF].rearrange("p (q c) -> p q c", c=2), ALU.mult)

            def shared_hidden(t):
                dve.wait_ge(sh_gu, t + 1)
                dve.wait_ge(sh_sig, t + 1)
                link(V.tensor_tensor(gw_t, PS[t][:, 0:FF], sg_t, ALU.mult))
                times_up(hrow[t % 2], PS[t]).then_inc(sh_h, 1)

            def shared_hT(t):
                dve.wait_ge(sh_tr, t + 1)
                V.tensor_copy(hTe[t % 2], PS[6][:, 0:FF]).then_inc(sh_hT, 1)

            def shared_y(t):
                dve.wait_ge(sh_dn, t + 1)
                if t >= 2:
                    dve.wait_ge(sh_st[t % 2], 16 * (t // 2))
                V.tensor_copy(ysb[t % 2][:, 512:1024], PS[5]).then_inc(sh_yb, 1)

            shared_hidden(0)
            shared_hidden(1)
            dve.wait_ge(pos_mm, 1)
            V.scalar_tensor_tensor(posm, PS[7][:, 0:NT * E], 1.0, r_mask, ALU.add, ALU.mult).then_inc(posm_done, 1)
            cnt = PS[7][:, NT * E:NT * E + E]
            nb, cum, cmp, cmn = gsb[:, 0:E], r_sel[:, 0:E], r_sel[:, E:2 * E], r_sel[:, 2 * E:3 * E]
            link(V.tensor_scalar(nb, cnt, P + 0.5, None, ALU.is_gt))
            link(V.scalar_tensor_tensor(nb, cnt, 2 * P + 0.5, nb, ALU.is_gt, ALU.add))
            link(V.scalar_tensor_tensor(nb, cnt, 3 * P + 0.5, nb, ALU.is_gt, ALU.add))
            link(V.tensor_tensor_scan(cum, nb, nb, 0.0, ALU.add, ALU.max))
            link(V.tensor_scalar(cmp, cum, con[:, C_SLOT:C_SLOT + 1], None, ALU.is_le))
            link(V.tensor_reduce(ovc[:, 0:1], cmp, AX, ALU.add))
            link(V.tensor_tensor(cmn, cmp, nb, ALU.mult))
            link(V.tensor_reduce(ovc[:, 2:3], cmn, AX, ALU.add))
            link(V.tensor_copy(ovcode[0:1, 2 * OV:2 * OV + 1], cum[0:1, E - 1:E]))
            link(V.tensor_scalar(ovc[:, 3:4], ovc[:, 2:3], -1.0, 1.0, ALU.mult, ALU.add))
            V.tensor_tensor(ovc[:, 1:2], ovc[:, 3:4], con[:, C_SLOT:C_SLOT + 1], ALU.add).then_inc(ov_col, 1)

            def select(e, m):
                if is_int(e) and e >= E:
                    return
                if not (is_int(e) and e == 0):
                    dve.wait_ge(info_mm, e)
                for t in range(NT):
                    last = V.tensor_scalar(selm[:, t, :], con[:, C_IOTA:C_IOTA + P], posm[:, bass.ds(e + t * E, 1)], None, ALU.is_equal)
                last.then_inc(sel_done, 1)

            def indices(e, m):
                if is_int(e) and e >= E:
                    return
                m = m % 4
                dve.wait_ge(info_mm, e + 1)
                V.tensor_copy(iw[:, 2 * m:2 * m + 2], PS[7][:, 0:2])
                V.tensor_scalar(gidx[:, m:m + 1], PS[7][:, 0:1], float(SEQ), None, ALU.add).then_inc(idx_done, 1)

            def hidden(e, m):
                dve.wait_ge(gu_mm, e + 1)
                dve.wait_ge(sig_done, e + 1)
                V.scalar_tensor_tensor(gw_t, PS[m % 2][:, 0:FF], iw[:, 2 * m + 1:2 * m + 2], sg_t, ALU.mult, ALU.mult).then_inc(hid_c, 1)
                dve.wait_ge(hid_c, e + 1)
                times_up(hrow[m % 2], PS[m % 2]).then_inc(h_done, 1)

            def hidden_T(e, m):
                dve.wait_ge(h_tr, e + 1)
                V.tensor_copy(hTe[m % 2], PS[6][:, 0:FF]).then_inc(h_out, 1)

            def places(e, m):
                m = m % 4
                if not (is_int(e) and e < 2):
                    dve.wait_ge(scattered, e * 16 - 16)
                V.tensor_scalar(tcol[:, m % 2:m % 2 + 1], iw[:, 2 * m:2 * m + 1], 0.0, con[:, C_SLOT:C_SLOT + 1], ALU.is_ge, ALU.mult).then_inc(sid_c, 1)
                dve.wait_ge(sid_c, e * 2 + 1)
                V.scalar_tensor_tensor(sidx[:, m % 2:m % 2 + 1], iw[:, 2 * m:2 * m + 1], float(SEQ), tcol[:, m % 2:m % 2 + 1], ALU.add, ALU.add).then_inc(sid_c, 1)
                dve.wait_ge(sid_c, e * 2 + 2)

            def rows_out(e, m):
                if is_int(e) and e < 2:
                    for w in (*sh_st, sh_pad):
                        dve.wait_ge(w, 16 if w is sh_pad else 8 * NT)
                dve.wait_ge(dn_mm, e + 1)
                V.tensor_copy(ysb[m % 2][:, 512:1024], PS[5]).then_inc(y_b, 1)

            dve.wait_ge(hp_tr, 2 * NT)
            dve.wait_ge(h_stored, 16 * NT)
            V.memset(xg[2], 0.0).then_inc(xg_zero, 1)
            dve.wait_ge(sh_gu, NT)
            V.memset(xg[3], 0.0).then_inc(xg_zero, 1)

            for t in range(NT):
                shared_hT(t)
                shared_y(t)
                if t + 2 < NT:
                    shared_hidden(t + 2)
                if t == 0:
                    dve.wait_ge(ov_tr, 1)
                    V.tensor_copy(ovcode[0:1, 0:2 * OV].rearrange("o (a b) -> o a b", a=2),
                                  PS[7][0:1, 0:2 * P].rearrange("o (a b) -> o a b", a=2)[:, :, 0:OV]).then_inc(ov_done, 1)
                else:
                    indices(t - 1, t - 1)
                if t < NT - 1:
                    select(t, t)

            def step(e, m):
                if not (is_int(e) and e == 0):
                    hidden_T(e - 1, m + 3)
                select(e + 3, m + 3)
                if not (is_int(e) and e == 0):
                    places(e - 1, m + 3)
                hidden(e, m)
                indices(e + 3, m + 3)
                if not (is_int(e) and e == 0):
                    rows_out(e - 1, m + 3)
            each_expert(dve, step)
            hidden_T(E - 1, (E - 1) % 4)
            places(E - 1, (E - 1) % 4)
            rows_out(E - 1, (E - 1) % 4)

            dve.wait_ge(ov_done, 1)
            n_over = dve.value_load(ovcode[0:1, 2 * OV:2 * OV + 1], min_val=0, max_val=MAXOVER)

            def over_select(k):
                ex = dve.value_load(ovcode[0:1, bass.ds(k, 1)], min_val=0, max_val=E - 1)
                part = dve.value_load(ovcode[0:1, bass.ds(k + OV, 1)], min_val=1, max_val=SEQ // P - 1)
                for t in range(NT):
                    last = V.tensor_scalar(selm[:, t, :], con[:, bass.ds(part * P + C_IOTA, P)], posm[:, bass.ds(ex + t * E, 1)], None, ALU.is_equal)
                last.then_inc(ov_sel, 1)

            def over_indices():
                V.tensor_copy(iw[:, 0:2], PS[7][:, 0:2])
                V.tensor_scalar(gidx[:, 0:1], PS[7][:, 0:1], float(SEQ), None, ALU.add).then_inc(ov_idx, 1)

            over_w = iw[:, 3:4]
            over_i = iw[:, 2:3]
            with dve.If(n_over > 0):
                over_select(0)
                dve.wait_ge(ov_info, 1)
                over_indices()

            def part(j):
                dve.wait_ge(ov_idx, j + 1)
                V.tensor_copy(iw[:, 2:4], iw[:, 0:2]).then_inc(ovd_c, 1)
                with dve.If(j + 1 < n_over):
                    over_select(j + 1)
                    dve.wait_ge(ov_xtr, j + 1)
                    dve.wait_ge(ovd_c, j * 4 + 1)
                    dve.wait_ge(ov_info, j + 2)
                    over_indices()
                dve.wait_ge(ovd_c, j * 4 + 1)
                dve.wait_ge(ov_gu, j + 1)
                dve.wait_ge(ov_sig, j + 1)
                V.scalar_tensor_tensor(gw_t, PS[0][:, 0:FF], over_w, sg_t, ALU.mult, ALU.mult).then_inc(ovd_c, 1)
                dve.wait_ge(ovd_c, j * 4 + 2)
                times_up(hrow[0], PS[0]).then_inc(ov_h, 1)
                dve.wait_ge(ov_htr, j + 1)
                V.tensor_copy(hTe[0], PS[6][:, 0:FF]).then_inc(ov_hT, 1)
                dve.wait_ge(ov_turn, j + 1)
                V.tensor_scalar(tcol[:, 0:1], over_i, 0.0, con[:, C_SLOT:C_SLOT + 1], ALU.is_ge, ALU.mult).then_inc(ovd_c, 1)
                dve.wait_ge(ovd_c, j * 4 + 3)
                V.scalar_tensor_tensor(sidx[:, 0:1], over_i, float(SEQ), tcol[:, 0:1], ALU.add, ALU.add).then_inc(ovd_c, 1)
                dve.wait_ge(ovd_c, j * 4 + 4)
                dve.wait_ge(ov_dn, j + 1)
                V.tensor_copy(ysb[0][:, 512:1024], PS[5]).then_inc(ov_y, 1)
            each_part(dve, n_over, part)

            def final_in(t):
                z = xm[:, D * t:D * t + D]
                dve.wait_ge(f_acc[t], 16)
                link(V.tensor_tensor(z, z, g2, ALU.mult))
                link(V.tensor_tensor(xrow[:, t, :], xrow[:, t, :], z, ALU.add))
                norm_stats(xrow[:, t, :])
                link(V.tensor_copy(fb[:, 2 * t:2 * t + 1], bnw[:, 14:15]))
                V.scalar_tensor_tensor(fb[:, 2 * t + 1:2 * t + 2], bnw[:, 12:13], -1.0, bnw[:, 14:15], ALU.mult, ALU.mult).then_inc(f_in, 1)

            def final_out(t):
                dve.wait_ge(f_mul, t + 1)
                V.tensor_tensor(xm[:, D * t:D * t + D], xm[:, D * t:D * t + D], ln2[:, D:2 * D], ALU.add).then_inc(f_out, 1)

            dve.wait_ge(ld_ln2, 32)
            dve.wait_ge(alpha_x, 1)
            for t in range(NT):
                final_in(t)
                if t:
                    final_out(t - 1)
            final_out(NT - 1)


_INS = ['x', 'c', 'ctx', 'c_ctx', 'w_mod', 'b_mod', 'w_in', 'q_norm', 'k_norm', 'pool_w', 'pool_scale', 'w_out',
        'ln1_g', 'ln1_b', 'w_router', 'router_bias', 'w_gate', 'w_up', 'w_down', 'ws_gate', 'ws_up', 'ws_down',
        'ln2_g', 'ln2_b']


def kernel(**inputs):
    import concourse.bacc as _bacc
    from concourse.bass_utils import run_bass_kernel_spmd as _run

    nc = _bacc.Bacc("TRN2", target_bir_lowering=False, num_devices=1)
    arrays, args = {}, {}
    fixed, temp = constants()
    for name, v in [(k, np.ascontiguousarray(inputs[k])) for k in _INS] + [("consts", fixed), ("tempc", temp)]:
        arrays[f"in_{name}_dram"] = v
        args[name] = nc.dram_tensor(f"in_{name}_dram", v.shape, mybir.dt.from_np(v.dtype), kind="ExternalInput").ap()
    out = nc.dram_tensor("out_0_dram", (1, SEQ, D), F32, kind="ExternalOutput").ap()
    build(nc, args, args["consts"], args["tempc"], out)
    r = _run(nc, [arrays], core_ids=[0])
    return r.results[0]["out_0_dram"]
```

```python
from contextlib import ExitStack

import numpy as np

import concourse.bass as bass
from concourse import mybir

F32 = mybir.dt.float32
BF16 = mybir.dt.bfloat16
U32 = mybir.dt.uint32
I32 = mybir.dt.int32
ALU = mybir.AluOpType
ACT = mybir.ActivationFunctionType
AX = mybir.AxisListType.X

P = 128
D = 1024
SEQ = 512
CTX = 256
NT = SEQ // P
NC = CTX // P
DC = D // P
POOLW = 256
WINDOWS = (2, 4, 8, 16)
HD = 64
NH = 12
NKV = 4
GQ = NH // NKV
QW = NH * HD
KW = NKV * HD
PROJ = POOLW + QW + 2 * KW
KEYS = CTX + SEQ
KT = KEYS // P
GRID_W = 64
THETA = 10000.0
E = 64
TOPK = 8
NG = 8
TG = 4
GE = E // NG
FF = 256
RSCALE = 2.5
ALPHA = 2.0 ** 0.25
LN_EPS = 1e-5
RMS_EPS = 1e-6
SHY = (4, 0)
MODB = (2, 3, 6, 7)
PAD = 16
UP = SEQ + 2 * PAD
BIG = 1.0e30
MARK = 3.0e38
OV = SEQ * TOPK // P
MAXOVER = OV - 1
FEWOVER = 6
ROUNDS = E // 4 - 2

C_ID, C_IOTA, C_UT, C_IDM, C_SLOT = 0, 128, 640, 768, 772
NCONST = 773
T_COS, T_SIN, T_INV = 0, 256, 512
NTEMP = 1536


def constants():
    a = np.zeros((P, NCONST), np.float32)
    a[:, C_ID:C_ID + P] = np.eye(P)
    a[:, C_IOTA:C_IOTA + SEQ] = np.arange(1, SEQ + 1)
    a[:, C_UT:C_UT + P] = np.triu(np.ones((P, P)), 1)
    a[:, C_IDM:C_IDM + NT] = np.arange(P)[:, None] + P * np.arange(NT)[None] - SEQ
    a[:, C_SLOT] = np.arange(P)
    t = np.zeros((P, NTEMP), np.float32)
    ax = HD // 2
    inv = np.float32(THETA) ** (-np.arange(0, ax, 2, dtype=np.float32) / np.float32(ax))
    pos = np.arange(SEQ)
    ang = np.concatenate([(pos // GRID_W).astype(np.float32)[:, None] * inv,
                          (pos % GRID_W).astype(np.float32)[:, None] * inv], axis=-1)
    cos = np.repeat(np.cos(ang), 2, axis=-1)
    sin = np.repeat(np.sin(ang), 2, axis=-1)
    sin[:, 0::2] *= -1
    t[:, T_COS:T_COS + NT * HD] = cos.reshape(NT, P, HD).transpose(1, 0, 2).reshape(P, -1)
    t[:, T_SIN:T_SIN + NT * HD] = sin.reshape(NT, P, HD).transpose(1, 0, 2).reshape(P, -1)
    for g, w in enumerate(WINDOWS):
        n = np.clip(pos + w - w // 2, 0, SEQ) - np.clip(pos - w // 2, 0, SEQ)
        t[HD * (g % 2):HD * (g % 2) + HD, T_INV + SEQ * (g // 2):T_INV + SEQ * (g // 2) + SEQ] = 1.0 / n
    return a, t


class Tile:

    def __init__(self, i, off):
        self.i, self.off = i, off

    def __call__(self, per, c):
        return self.i * per + (self.off * per + c)

    @property
    def cols(self):
        return bass.ds(self(P, 0), P)

    @property
    def before(self):
        return Tile(self.i, self.off - 1)


def build(nc, a, consts, tempc, out):
    h_rows = nc.dram_tensor("h_rows", [SEQ, D], F32, kind="Internal").ap()
    acc_rows = nc.dram_tensor("acc_rows", [SEQ + P, D], F32, kind="Internal").ap()

    ctx = ExitStack()
    with ctx:
        def sb(name, cols, dt=F32):
            return ctx.enter_context(nc.sbuf_tensor(name, [P, cols], dt))

        def sem(name):
            return ctx.enter_context(nc.semaphore(name))

        ring = sb("ring", 20480)
        xres = sb("xres", 4096)
        xm = sb("xm", 4096)
        cm = sb("cm", 2048)
        kq = sb("kq", 6144)
        vr = sb("vr", 1536)
        pmix = sb("pmix", 1024)
        bc = sb("bc", 4096)
        lnr = sb("lnr", 2048)
        att = sb("att", 4352)
        con = sb("con", NCONST)
        ones = sb("ones", P)
        tabs = sb("tabs", 1024)
        pw = sb("pw", 256)
        gains = sb("gains", 2 * HD)
        rbias = sb("rbias", E)
        cvec = sb("cvec", 16)
        csig = sb("csig", 16)
        csil = sb("csil", 16)
        modc = sb("modc", 32)
        pscale = sb("pscale", 2)
        stat = sb("stat", 36)
        negmax = sb("negmax", 2)
        rowsum = sb("rowsum", 2)
        recips = sb("recips", 2)
        gsb = sb("gsb", 64 + 32 + 64)
        bnw = sb("bnw", 16)
        rsm = sb("rsm", 12)
        iw = sb("iw", 8)
        tcol = sb("tcol", 2)
        gidx = sb("gidx", 4, U32)
        sidx = sb("sidx", 2, U32)
        fbn = sb("fbn", 12 * NT)
        fmv = sb("fmv", 2 * NT)
        fvar = sb("fvar", NT)
        fb = sb("fb", 2 * NT)
        ovc = sb("ovc", 4)
        ovcode = sb("ovcode", 2 * OV + 4, I32)

        ident = con[:, C_ID:C_ID + P]
        wmod_a = [ring[:, 2048 * s:2048 * s + 2048] for s in range(4)]
        wmod_b = [ring[:, 4096 * s:4096 * s + 4096] for s in range(2)]
        wout = ring[:, 0:8192].rearrange("p (c n) -> p c n", c=DC)
        win = ring[:, 8192:20480].rearrange("p (c n) -> p c n", c=DC)
        gu_flat = [ring[:, 4096 + 4096 * s:8192 + 4096 * s] for s in range(4)]
        gu_w = [g.rearrange("p (u c f) -> p u c f", u=2, c=DC) for g in gu_flat]
        dn_flat = [ring[:, 2048 * s:2048 * s + 2048] for s in range(2)]
        dn_w = [g.rearrange("p (c n) -> p c n", c=2) for g in dn_flat]
        xrow = xres[:, :].rearrange("p (t d) -> p t d", t=NT)
        st_n, st_a, st_b, st_q, st_r = (xres[:, 768 * i:768 * i + 768] for i in range(5))
        xmT = xm[:, :].rearrange("p (c t) -> p c t", c=DC)
        mixA = xm[:, 1024:4096].rearrange("p (c t) -> p c t", c=6)
        mixP = pmix[:, :].rearrange("p (c t) -> p c t", c=2)
        lnA = xm[:, 0:1024]
        xg = [xm[:, 0:1024], xm[:, 1024:2048], cm[:, 0:1024], att[:, 0:1024]]
        ysb = [xm[:, 2048:3072], xm[:, 3072:4096]]
        cmT = cm[:, :].rearrange("p (c t) -> p c t", c=DC)
        hperm = cm[:, 0:1024]
        r_sc = cm[:, 1024:1280]
        r_sel = cm[:, 1280:1536]
        r_mask = cm[:, 1536:1792]
        posm = cm[:, 1792:2048]
        mrow = kq[0:2, 0:2048]
        brow_a = kq[0:1, 2048:4096]
        kT = kq[:, 0:3072].rearrange("p (h k) -> p h k", h=NKV)
        qT = kq[:, 3072:6144].rearrange("p (h t) -> p h t", h=6)
        hT = kq[:, 0:4096].rearrange("p (c t) -> p c t", c=DC)
        ws_dn_flat = kq[:, 4096:6144]
        ws_dn = ws_dn_flat.rearrange("p (c n) -> p c n", c=2)
        ln2 = kq[:, 0:2048]
        vall = vr[:, :].rearrange("p (k d) -> p k d", k=KT)
        selm = vr[:, 0:256].bitcast(BF16).rearrange("p (t s) -> p t s", t=NT)
        hrow = [vr[:, 512:768], vr[:, 768:1024]]
        hTe = [vr[:, 1024:1280], vr[:, 1280:1536]]
        gw_t = pmix[:, 0:256]
        sg_t = pmix[:, 256:512]
        xT = [lnr[:, 0:1024], lnr[:, 1024:2048]]
        crow = att[:, 0:2048].rearrange("p (t d) -> p t d", t=NC)
        pU = att[:, 0:2 * UP].rearrange("p (c t) -> p c t", c=2)
        pS2 = att[:, 2 * UP:4 * UP].rearrange("p (c t) -> p c t", c=2)
        pS4 = att[:, 4 * UP:6 * UP].rearrange("p (c t) -> p c t", c=2)
        pS8 = att[:, 6 * UP:7 * UP]
        pS16 = att[:, 7 * UP:8 * UP]
        qcur = cm[:, 0:NH * P].rearrange("p (h t) -> p h t", h=NH)
        prob = [xres[:, 768 * i:768 * i + 768] for i in range(2)]
        prT = [xres[:, 1536 + 768 * i:2304 + 768 * i].rearrange("p (k q) -> p k q", k=KT) for i in range(2)]
        arow = xres[:, 3072:3840]
        ws_gu_flat = att[:, 0:4096]
        ws_gu = ws_gu_flat.rearrange("p (u c f) -> p u c f", u=2, c=DC)
        wrt_flat = tabs[:, 0:512]
        wrt = wrt_flat.rearrange("p (c e) -> p c e", c=DC)
        info = tabs[:, 0:2 * 3 * NT * E // 2].bitcast(BF16).rearrange("p (t n) -> p t n", t=NT)
        g8 = tabs[:, 512:768].rearrange("p (t g m) -> p t g m", t=NT, g=NG)
        gs16 = gsb[:, 0:64].rearrange("p (t g) -> p t g", t=NT)
        gtop = gsb[:, 64:96].rearrange("p (t g) -> p t g", t=NT)
        gmk = gsb[:, 96:160].rearrange("p (t g) -> p t g", t=NT)

        psum = ctx.enter_context(nc.psum_tensor("psum", [P, 8 * 512], F32))
        PS = [psum[:, 512 * b:512 * b + 512] for b in range(8)]
        PS3 = psum[:, :].rearrange("p (b n) -> p b n", b=8)

        ld_const, ld_temp, ld_c, ld_x, ld_ctx, ld_brow = (sem(n) for n in (
            "ld_const", "ld_temp", "ld_c", "ld_x", "ld_ctx", "ld_brow"))
        ld_wa = [sem(f"ld_wa{i}") for i in range(4)]
        ld_wb = [sem(f"ld_wb{i}") for i in range(2)]
        ld_wkv, ld_wqu, ld_small, ld_wout, ld_x2, ld_ln1, ld_ws, ld_ln2, ld_wr = (sem(n) for n in (
            "ld_wkv", "ld_wqu", "ld_small", "ld_wout", "ld_x2", "ld_ln1", "ld_ws", "ld_ln2", "ld_wr"))
        var_in, root_out = sem("var_in"), sem("root_out")
        ld_gu = [sem(f"ld_gu{i}") for i in range(4)]
        ld_dn = [sem(f"ld_dn{i}") for i in range(2)]
        ones_set, pw_zero, bc_zero, ld_bias, iw_c = (sem(n) for n in (
            "ones_set", "pw_zero", "bc_zero", "ld_bias", "iw_chain"))
        c_sigmoid, c_silu = sem("c_sigmoid"), sem("c_silu")
        moda_mm, moda_row, moda_tr, moda_col = sem("moda_mm"), sem("moda_row"), sem("moda_tr"), sem("moda_col")
        xtr, xtr_out = sem("xtr"), sem("xtr_out")
        xmod = sem("xmod")
        scaled, gemv, modb_mm, modb_out = sem("scaled"), sem("gemv"), sem("modb_mm"), sem("modb_out")
        tab_done = sem("tab_done")
        kv_mm, kv_sq, kv_v, kv_row, kv_tr, kv_tr_out = (sem(n) for n in (
            "kv_mm", "kv_sq", "kv_v", "kv_row", "kv_tr", "kv_tr_out"))
        u_mm, u_out, u_pad, pooled, pool_mm, pool_out = (sem(n) for n in (
            "u_mm", "u_out", "u_pad", "pooled", "pool_mm", "pool_out"))
        q_cur, q_zero, scored, maxed, exped, ptr, ptr_a, ptr_b, pv_mm, o_row, atr, atr_out = (sem(n) for n in (
            "q_cur", "q_zero", "scored", "maxed", "exped", "ptr", "ptr_a", "ptr_b", "pv_mm", "o_row", "atr", "atr_out"))
        out_mm, mix_read, hp_ready, hp_tr, hT_out, h_stored, log_mm = (sem(n) for n in (
            "out_mm", "mix_read", "hp_ready", "hp_tr", "hT_out", "h_stored", "log_mm"))
        sc_done, masked, pos_mm, posm_done, ov_col, ov_tr, ov_done = (sem(n) for n in (
            "sc_done", "masked", "pos_mm", "posm_done", "ov_col", "ov_tr", "ov_done"))
        sh_gu, sh_sig, sh_h, sh_tr, sh_hT, sh_dn, sh_y_read, sh_y, sh_pad = (sem(n) for n in (
            "sh_gu", "sh_sig", "sh_h", "sh_tr", "sh_hT", "sh_dn", "sh_y_read", "sh_y", "sh_pad"))
        sh_st = [sem("sh_st0"), sem("sh_st1")]
        sel_done, info_mm, idx_done, xg_zero, x_tr, xT_a, gu_mm, sig_done, h_done, h_tr, h_out, dn_mm, y_out = (
            sem(n) for n in ("sel_done", "info_mm", "idx_done", "xg_zero", "x_tr", "xT_a", "gu_mm",
                             "sig_done", "h_done", "h_tr", "h_out", "dn_mm", "y_out"))
        gathered = [sem(f"gathered{i}") for i in range(4)]
        scattered = sem("scattered")
        ov_w, ov_wd = ([sem(f"ov_{n}{i}") for i in range(2)] for n in ("w", "wd"))
        ov_sel, ov_info, ov_idx, ov_gat, ov_xtr, ov_xT, ov_gu, ov_sig, ov_h, ov_htr, ov_hT, ov_dn, ov_y, ov_scat = (
            sem("ov_" + n) for n in ("sel", "info", "idx", "gat", "xtr", "xT", "gu", "sig", "h", "htr",
                                     "hT", "dn", "y", "scat"))
        ov_turn, row_moves = sem("ov_turn"), sem("row_moves")
        f_acc = [sem(f"f_acc{i}") for i in range(NT)]
        f_st, f_norm, f_out, f_stored = sem("f_st"), sem("f_norm"), sem("f_out"), sem("f_stored")
        dve_c, pool_c, hid_c, sid_c, ovd_c, att_c, f_in, f_mul = (sem(n) for n in (
            "dve_chain", "pool_chain", "hidden_chain", "sidx_chain", "over_chain", "att_chain", "f_in", "f_mul"))

        x_v = a["x"].rearrange("o (t p) d -> p (o t) d", p=P)
        ctx_v = a["ctx"].rearrange("o (t p) d -> p (o t) d", p=P)
        wmod_v = a["w_mod"].rearrange("o (p k) n -> p (o k) n", k=DC)
        bmod_v = a["b_mod"]
        win_v = a["w_in"].rearrange("o (c p) n -> p (o c) n", p=P)
        wout_v = a["w_out"].rearrange("o (c p) n -> p (o c) n", p=P)
        wr_v = a["w_router"].rearrange("o (p c) e -> p (o c e)", c=DC)
        gate_v = a["w_gate"].rearrange("o e (p c) f -> (o e) p (c f)", c=DC)
        up_v = a["w_up"].rearrange("o e (p c) f -> (o e) p (c f)", c=DC)
        down_v = a["w_down"].rearrange("o e (p c) n -> (o e) p (c n)", c=2)
        wsg_v = a["ws_gate"].rearrange("o (p c) f -> p (o c f)", c=DC)
        wsu_v = a["ws_up"].rearrange("o (p c) f -> p (o c f)", c=DC)
        wsd_v = a["ws_down"].rearrange("o (p c) n -> p (o c n)", c=2)

        def row_bcast(name, lo, hi):
            return a[name][0:1, lo:hi].to_broadcast([P, hi - lo])

        block = ctx.enter_context(nc.Block())

        def each_expert(eng, step, count=None):
            for e in range(4):
                step(e, e)
            with eng.Fori(0, ROUNDS) as i:
                for j in range(4):
                    step(i * 4 + (4 + j), j)
            if count:
                count()
            for e in range(4 + 4 * ROUNDS, E):
                step(e, e % 4)

        def over_count(eng, n_over):
            eng.wait_ge(ov_done, 1)
            n_over.append(eng.value_load(ovcode[0:1, 2 * OV:2 * OV + 1], min_val=0, max_val=MAXOVER))

        def each_part(eng, n_over, step):
            n_over, = n_over

            def pairs(lo, hi):
                with eng.Fori(lo, hi) as i:
                    for slot in range(2):
                        with eng.If(i * 2 + slot < n_over):
                            step(i * 2 + slot, i, slot)
            pairs(0, FEWOVER // 2)
            with eng.If(n_over > FEWOVER):
                pairs(FEWOVER // 2, (MAXOVER + 1) // 2)

        def is_int(e):
            return isinstance(e, int)

        def each_tile(eng, step):
            step(Tile(0, 0), True, False)
            with eng.Fori(0, NT - 2) as i:
                step(Tile(i, 1), False, False)
            step(Tile(0, NT - 1), False, True)

        def pair_before(at, u, first):
            if u % 2 == 0 or (first and u == 1):
                return None
            return (at, (u - 3) // 2) if u >= 3 else (at.before, NH // 2 - 1)

        @block.sync
        def _(sp):
            sp.dma_start(con[:, :], consts).then_inc(ld_const, 16)
            sp.dma_start(cvec[:, 0:8], a["c"].rearrange("o (p k) -> p (o k)", k=DC)).then_inc(ld_c, 16)
            sp.dma_start(cvec[:, 8:16], a["c_ctx"].rearrange("(p k) -> p k", k=DC)).then_inc(ld_c, 16)
            sp.dma_start(wmod_a[0], wmod_v[:, 0, 0:2 * D]).then_inc(ld_wa[0], 16)
            sp.dma_start(xres[:, :].rearrange("p (t d) -> p t d", t=NT), x_v).then_inc(ld_x, 16)
            for k in range(1, 4):
                sp.dma_start(wmod_a[k], wmod_v[:, k, 0:2 * D]).then_inc(ld_wa[k], 16)
            sp.dma_start(brow_a, bmod_v[0:1, 0:2 * D]).then_inc(ld_brow, 16)
            sp.dma_start(crow, ctx_v).then_inc(ld_ctx, 16)
            sp.wait_ge(bc_zero, 1)
            sp.dma_start(bc[0:1, :], bmod_v[0:1, 2 * D:6 * D]).then_inc(ld_bias, 16)
            sp.dma_start(lnr[:, 0:NTEMP], tempc).then_inc(ld_temp, 16)
            sp.dma_start(gains[:, 0:HD], row_bcast("q_norm", 0, HD)).then_inc(ld_small, 16)
            sp.dma_start(gains[:, HD:2 * HD], row_bcast("k_norm", 0, HD)).then_inc(ld_small, 16)
            sp.dma_start(rbias[:, :], row_bcast("router_bias", 0, E)).then_inc(ld_small, 16)
            for h in range(2):
                sp.dma_start(pscale[:, h:h + 1], a["pool_scale"][0, P * h:P * h + P].rearrange("(p o) -> p o", o=1)).then_inc(ld_small, 16)
            sp.wait_ge(pw_zero, 1)
            for g in range(4):
                r, col = HD * (g % 2), P * (g // 2) + HD * (g % 2)
                sp.dma_start(pw[r:r + HD, col:col + HD], a["pool_w"][0, g]).then_inc(ld_small, 16)
            for k in range(4, DC):
                sp.wait_ge(moda_mm, k - 3)
                sp.dma_start(wmod_a[k % 4], wmod_v[:, k, 0:2 * D]).then_inc(ld_wa[k % 4], 16)
            sp.dma_start(win[:, :, 1024:PROJ], win_v[:, :, 1024:PROJ]).then_inc(ld_wkv, 16)
            sp.dma_start(win[:, :, 0:1024], win_v[:, :, 0:1024]).then_inc(ld_wqu, 16)
            for k in range(DC):
                if k < 2:
                    sp.wait_ge(moda_mm, 2 * k + 6)
                else:
                    sp.wait_ge(gemv, k - 1)
                sp.dma_start(wmod_b[k % 2], wmod_v[:, k, 2 * D:6 * D]).then_inc(ld_wb[k % 2], 16)
            sp.wait_ge(gemv, DC)
            sp.dma_start(wout, wout_v).then_inc(ld_wout, 16)
            sp.wait_ge(kv_mm, KT + NT)
            sp.wait_ge(u_mm, 2)
            for e in range(3):
                s = (e + 1) % 4
                sp.dma_start(gu_flat[s][:, 0:2048], gate_v[e]).then_inc(ld_gu[s], 16)
                sp.dma_start(gu_flat[s][:, 2048:4096], up_v[e]).then_inc(ld_gu[s], 16)
            sp.wait_ge(kv_tr, KT + NT)
            sp.dma_start(wrt_flat, wr_v).then_inc(ld_wr, 16)
            sp.wait_ge(pooled, 1)
            sp.dma_start(lnr[:, 0:D], row_bcast("ln1_g", 0, D)).then_inc(ld_ln1, 16)
            sp.dma_start(lnr[:, D:2 * D], row_bcast("ln1_b", 0, D)).then_inc(ld_ln1, 16)
            sp.dma_start(ws_gu_flat[:, 0:2048], wsg_v).then_inc(ld_ws, 16)
            sp.dma_start(ws_gu_flat[:, 2048:4096], wsu_v).then_inc(ld_ws, 16)
            sp.wait_ge(atr_out, NH // 2 * NT)
            sp.wait_ge(o_row, NH * NT)
            sp.dma_start(xrow, x_v).then_inc(ld_x2, 16)
            sp.dma_start(ws_dn_flat, wsd_v).then_inc(ld_ws, 16)
            for t in range(NT):
                sp.wait_ge(hp_ready, t + 1)
                sp.dma_start(h_rows[P * t:P * t + P, :], hperm).then_inc(h_stored, 16)
            sp.wait_ge(out_mm, NT)
            for e in range(2):
                sp.dma_start(dn_flat[e], down_v[e]).then_inc(ld_dn[e], 16)
            sp.dma_start(gu_flat[0][:, 0:2048], gate_v[3]).then_inc(ld_gu[0], 16)
            sp.dma_start(gu_flat[0][:, 2048:4096], up_v[3]).then_inc(ld_gu[0], 16)
            for t in range(NT):
                sp.wait_ge(sh_y, t + 1)
                sp.dma_start(acc_rows[P * t:P * t + P, :], ysb[t % 2]).then_inc(sh_st[t % 2], 16)
            sp.dma_start(acc_rows[SEQ:SEQ + P, :], ysb[(NT - 1) % 2]).then_inc(sh_pad, 16)
            sp.wait_ge(sh_dn, NT)
            sp.wait_ge(log_mm, NT)
            sp.dma_start(ln2[:, 0:D], row_bcast("ln2_g", 0, D)).then_inc(ld_ln2, 16)
            sp.dma_start(ln2[:, D:2 * D], row_bcast("ln2_b", 0, D)).then_inc(ld_ln2, 16)

            def step(e, m):
                if not (is_int(e) and e + 4 >= E):
                    sp.wait_ge(gu_mm, e + 1)
                    s = (m + 1) % 4
                    sp.dma_start(gu_flat[s][:, 0:2048].rearrange("p (o n) -> p o n", o=1), gate_v[bass.ds(e + 4, 1)].rearrange("o p n -> p o n")).then_inc(ld_gu[s], 16)
                    sp.dma_start(gu_flat[s][:, 2048:4096].rearrange("p (o n) -> p o n", o=1), up_v[bass.ds(e + 4, 1)].rearrange("o p n -> p o n")).then_inc(ld_gu[s], 16)
                if not (is_int(e) and (e == 0 or e + 1 >= E)):
                    sp.wait_ge(dn_mm, e)
                    sp.dma_start(dn_flat[(m + 1) % 2].rearrange("p (o n) -> p o n", o=1), down_v[bass.ds(e + 1, 1)].rearrange("o p n -> p o n")).then_inc(ld_dn[(m + 1) % 2], 16)
            n_over = []
            each_expert(sp, step, lambda: over_count(sp, n_over))


            def over_gu(ex, slot):
                g = gu_flat[1 + slot]
                sp.dma_start(g[:, 0:2048].rearrange("p (o n) -> p o n", o=1), gate_v[bass.ds(ex, 1)].rearrange("o p n -> p o n")).then_inc(ov_w[slot], 16)
                sp.dma_start(g[:, 2048:4096].rearrange("p (o n) -> p o n", o=1), up_v[bass.ds(ex, 1)].rearrange("o p n -> p o n")).then_inc(ov_w[slot], 16)

            def over_dn(ex, slot):
                sp.dma_start(dn_flat[slot].rearrange("p (o n) -> p o n", o=1), down_v[bass.ds(ex, 1)].rearrange("o p n -> p o n")).then_inc(ov_wd[slot], 16)

            for slot in range(2):
                with sp.If(n_over[0] > slot):
                    ex = sp.value_load(ovcode[0:1, slot:slot + 1], min_val=0, max_val=E - 1)
                    sp.wait_ge(gu_mm, E - 3 + slot)
                    if slot:
                        sp.wait_ge(ov_idx, 2)
                    over_gu(ex, slot)
                    sp.wait_ge(dn_mm, E - 1 + slot)
                    over_dn(ex, slot)

            def part(j, i, slot):
                with sp.If(j + 2 < n_over[0]):
                    ex = sp.value_load(ovcode[0:1, bass.ds(j + 2, 1)], min_val=0, max_val=E - 1)
                    sp.wait_ge(ov_gu, j + 1)
                    over_gu(ex, slot)
                    sp.wait_ge(ov_dn, j + 1)
                    over_dn(ex, slot)
            each_part(sp, n_over, part)

            sp.wait_ge(f_st, 1)
            for t in range(NT):
                sp.dma_start(xm[:, D * t:D * t + D], acc_rows[P * t:P * t + P, :]).then_inc(f_acc[t], 16)
            for t in range(NT):
                sp.wait_ge(f_out, t + 1)
                sp.dma_start(out[0, P * t:P * t + P, :], xm[:, D * t:D * t + D]).then_inc(f_stored, 16)
            sp.wait_ge(f_stored, 16 * NT)

        @block.gpsimd
        def _(pool):
            n = [0]

            def link(ins):
                n[0] += 1
                ins.then_inc(pool_c, 1)
                pool.wait_ge(pool_c, n[0])

            nc.gpsimd.memset(ones[:, :], 1.0).then_inc(ones_set, 1)
            nc.gpsimd.memset(pw[:, :], 0.0).then_inc(pw_zero, 1)
            nc.gpsimd.memset(bc[:, :], 0.0).then_inc(bc_zero, 1)
            for k in range(DC):
                pool.wait_ge(scaled, k + 1)
                if k == 0:
                    pool.wait_ge(ld_bias, 16)
                else:
                    pool.wait_ge(gemv, k)
                nc.gpsimd.tensor_tensor(bc[:, :], wmod_b[k % 2], bc[:, :], ALU.add).then_inc(gemv, 1)

            pool.wait_ge(u_out, 2)
            pool.wait_ge(u_pad, 2)
            hi = UP
            link(nc.gpsimd.tensor_tensor(pS2[:, :, 1:hi], pU[:, :, 0:hi - 1], pU[:, :, 1:hi], ALU.add))
            link(nc.gpsimd.tensor_tensor(pS4[:, :, 2:hi - 1], pS2[:, :, 1:hi - 2], pS2[:, :, 3:hi], ALU.add))
            link(nc.gpsimd.tensor_tensor(pS8[:, 4:hi - 3], pS4[:, 1, 2:hi - 5], pS4[:, 1, 6:hi - 1], ALU.add))
            link(nc.gpsimd.tensor_tensor(pS16[:, 8:hi - 8], pS8[:, 4:hi - 12], pS8[:, 12:hi - 4], ALU.add))
            inv = lnr[:, T_INV:T_INV + 2 * SEQ].rearrange("p (c t) -> p c t", c=2)
            lo = PAD
            pool.wait_ge(ld_temp, 16)
            for r, c, s in ((0, 0, pS2[:, 0]), (1, 0, pS4[:, 0]), (0, 1, pS8), (1, 1, pS16)):
                rs = slice(HD * r, HD * r + HD)
                link(nc.gpsimd.tensor_tensor(mixP[rs, c, :], s[rs, lo:lo + SEQ], inv[rs, c, :], ALU.mult))
            nc.gpsimd.tensor_tensor(mixP[:, :, :], mixP[:, :, :], pU[:, :, lo:lo + SEQ], ALU.subtract).then_inc(pooled, 1)

            with pool.Fori(0, NT - 1) as t:
                for u in range(NH):
                    r = HD * (u % 2)
                    if u == 0:
                        pool.wait_ge(pooled, 1)
                    pool.wait_ge(q_cur, t * NH + (NH + u))
                    pool.wait_ge(scored, t * NH + (u + 1))
                    nc.gpsimd.tensor_copy(qcur[r:r + HD, u, :], qT[r:r + HD, u // 2, bass.ds(t * P + P, P)]).then_inc(q_cur, 1)

            pool.wait_ge(hp_ready, NT)
            nc.gpsimd.memset(xg[0], 0.0).then_inc(xg_zero, 1)
            nc.gpsimd.memset(xg[1], 0.0).then_inc(xg_zero, 1)
            pool.wait_ge(h_stored, 16 * NT)
            pool.wait_ge(hp_tr, 2 * NT)
            nc.gpsimd.memset(xg[2], 0.0).then_inc(xg_zero, 1)
            pool.wait_ge(sh_gu, NT)
            nc.gpsimd.memset(xg[3], 0.0).then_inc(xg_zero, 1)
            pool.wait_ge(xg_zero, 4)

            def gather(e, m):
                if is_int(e) and e >= E:
                    return
                pool.wait_ge(idx_done, e + 1)
                if not (is_int(e) and e < 4):
                    pool.wait_ge(x_tr, e - 3)
                pool.sem_inc(row_moves, 1)
                nc.gpsimd.indirect_dma_start(out=xg[m % 4], out_offset=None, in_=h_rows,
                                             in_offset=bass.IndirectOffsetOnAxis(ap=gidx[:, m % 4:m % 4 + 1], axis=0),
                                             bounds_check=SEQ - 1, oob_is_err=False).then_inc(gathered[m % 4], 16)

            def scatter(e, m):
                pool.wait_ge(y_out, e + 1)
                if not (is_int(e) and e == 0):
                    pool.wait_ge(scattered, 16 * e)
                pool.sem_inc(row_moves, 1)
                nc.gpsimd.indirect_dma_start(out=acc_rows,
                                             out_offset=bass.IndirectOffsetOnAxis(ap=sidx[:, m % 2:m % 2 + 1], axis=0),
                                             in_=ysb[m % 2], in_offset=None, bounds_check=SEQ + P - 1,
                                             compute_op=ALU.add).then_inc(scattered, 16)

            for e in range(3):
                gather(e, e)
            for w in (*sh_st, sh_pad):
                pool.wait_ge(w, 16 if w is sh_pad else 8 * NT)

            def over_gather():
                pool.sem_inc(row_moves, 1)
                nc.gpsimd.indirect_dma_start(out=xg[0], out_offset=None, in_=h_rows,
                                             in_offset=bass.IndirectOffsetOnAxis(ap=gidx[:, 0:1], axis=0),
                                             bounds_check=SEQ - 1, oob_is_err=False).then_inc(ov_gat, 16)
            n_over = []

            def step(e, m):
                gather(e + 3, m + 3)
                if is_int(e) and e == E - 2:
                    with pool.If(n_over[0] > 0):
                        pool.wait_ge(ov_idx, 1)
                        pool.wait_ge(x_tr, E - 3)
                        over_gather()
                if not (is_int(e) and e == 0):
                    scatter(e - 1, m - 1 + 4)
            each_expert(pool, step, lambda: over_count(pool, n_over))
            scatter(E - 1, (E - 1) % 4)
            pool.wait_ge(scattered, 16 * E)
            pool.sem_inc(ov_turn, 1)
            pool.sem_inc(ov_y, 1)

            def part(j, i, slot):
                with pool.If(j + 1 < n_over[0]):
                    pool.wait_ge(ov_xtr, j + 1)
                    pool.wait_ge(ov_idx, j + 2)
                    over_gather()
                with pool.If(j > 0):
                    pool.wait_ge(ov_scat, 16 * j)
                    pool.sem_inc(ov_turn, 1)
                pool.wait_ge(ov_y, j + 2)
                pool.sem_inc(row_moves, 1)
                nc.gpsimd.indirect_dma_start(out=acc_rows,
                                             out_offset=bass.IndirectOffsetOnAxis(ap=sidx[:, 0:1], axis=0),
                                             in_=ysb[0], in_offset=None, bounds_check=SEQ + P - 1,
                                             compute_op=ALU.add).then_inc(ov_scat, 16)
            each_part(pool, n_over, part)
            with pool.If(n_over[0] > 0):
                pool.wait_ge(ov_scat, n_over[0] * 16)
                pool.sem_inc(row_moves, 1)
            nc.gpsimd.memset(gidx[:, 0:1], 0).then_inc(f_st, 1)

            for t in range(1, NT, 2):
                pool.wait_ge(f_norm, t + 1)
                pool.wait_ge(ld_ln2, 32)
                nc.gpsimd.tensor_tensor(xm[:, D * t:D * t + D], xm[:, D * t:D * t + D], ln2[:, 0:D], ALU.mult).then_inc(f_mul, 1)

        @block.scalar
        def _(act):
            act.wait_ge(ld_c, 32)
            nc.scalar.activation(csig[:, :], cvec[:, :], ACT.Sigmoid).then_inc(c_sigmoid, 1)
            for g in range(12):
                act.wait_ge(xtr, g + 1)
                ps = PS[4 + g % 4]
                if g < 8:
                    nc.scalar.activation(xmT[:, g, :], ps[:, :], ACT.Copy).then_inc(xtr_out, 1)
                else:
                    nc.scalar.activation(cmT[:, 2 * (g - 8):2 * (g - 8) + 2, :], ps[:, :].rearrange("p (c t) -> p c t", c=2),
                                         ACT.Copy).then_inc(xtr_out, 1)
            act.wait_ge(moda_mm, DC)
            for q in range(2, 4):
                nc.scalar.activation(mrow[:, 512 * q:512 * q + 512], PS[q][0:2, :], ACT.Copy).then_inc(moda_row, 1)
            def k_out(j):
                act.wait_ge(kv_tr, j + 1)
                nc.scalar.activation(kT[:, :, P * j:P * j + P], PS[4 + j % 2].rearrange("p (h k) -> p h k", h=NKV),
                                     ACT.Copy).then_inc(kv_tr_out, 1)

            def q_out(i):
                act.wait_ge(kv_tr, KT + i + 1)
                for h in range(2):
                    nc.scalar.activation(qT[:, 3 * h:3 * h + 3, P * i:P * i + P],
                                         PS[4 + h][:, 0:384].rearrange("p (h t) -> p h t", h=3), ACT.Copy).then_inc(kv_tr_out, 1)

            roots = [0]

            def root(row):
                roots[0] += 1
                act.wait_ge(var_in, roots[0])
                nc.scalar.activation(row, row, ACT.Sqrt).then_inc(root_out, 1)

            def scale_wmod(k):
                if k == 0:
                    act.wait_ge(c_silu, 1)
                act.wait_ge(ld_wb[k % 2], 16 * (k // 2 + 1))
                nc.scalar.activation(wmod_b[k % 2], wmod_b[k % 2], ACT.Copy,
                                     scale=csil[:, 2 * k:2 * k + 1]).then_inc(scaled, 1)

            for j in range(KT):
                act.wait_ge(kv_mm, j + 1)
                if j:
                    act.wait_ge(kv_row, j)
                nc.scalar.activation(st_q[:, 0:KW], PS[j % 2][:, 0:KW], ACT.Square).then_inc(kv_sq, 1)
                nc.scalar.activation(vall[:, j, :], PS[j % 2][:, KW:2 * KW], ACT.Copy).then_inc(kv_v, 1)
                root(stat[:, 12:12 + NKV])
                if j:
                    k_out(j - 1)
                if 3 <= j < 5:
                    scale_wmod(j - 3)
            scale_wmod(2)
            k_out(KT - 1)
            for i in range(NT):
                act.wait_ge(kv_mm, KT + i + 1)
                act.wait_ge(kv_row, KT + i)
                b = i % 2
                nc.scalar.activation(st_q[:, 0:512], PS[b], ACT.Square).then_inc(kv_v, 1)
                nc.scalar.activation(st_q[:, 512:768], PS[2 + b][:, 0:256], ACT.Square).then_inc(kv_sq, 1)
                if i:
                    q_out(i - 1)
                root(stat[:, 12:12 + NH])
                scale_wmod(3 + i)
            act.wait_ge(u_mm, 1)
            nc.scalar.activation(pU[:, 0, PAD:PAD + SEQ], PS[6], ACT.Copy).then_inc(u_out, 1)
            q_out(NT - 1)
            act.wait_ge(u_mm, 2)
            nc.scalar.activation(pU[:, 1, PAD:PAD + SEQ], PS[7], ACT.Copy).then_inc(u_out, 1)

            def pair_out(at, pair):
                act.wait_ge(atr, at(NH // 2, pair + 1))
                nc.scalar.activation(mixA[:, pair, at.cols], PS[4][:, 384:512], ACT.Copy).then_inc(atr_out, 1)

            def act_tile(at, first, last):
                for u in range(NH):
                    w = u % 2
                    act.wait_ge(maxed, at(NH, u + 1))
                    if not (first and u < 2):
                        act.wait_ge(ptr, at(2 * NH, 2 * (u - 1)))
                        act.wait_ge(o_row, at(NH, u - 1))
                    nc.scalar.activation(prob[w].rearrange("p (b k) -> p b k", b=2), PS3[:, 2 * w:2 * w + 2, 0:384], ACT.Exp,
                                         bias=negmax[:, w:w + 1], accum_out=rowsum[:, w:w + 1]).then_inc(exped, 1)
                    act.wait_ge(ptr, at(2 * NH, 2 * u + 1))
                    if not (first and u < 2):
                        act.wait_ge(pv_mm, at(NH, u - 1))
                    nc.scalar.activation(prT[w][:, 0:3, :], PS[4][:, 0:384].rearrange("p (k q) -> p k q", k=3),
                                         ACT.Copy).then_inc(ptr_a, 1)
                    if first and u == 1:
                        scale_wmod(7)
                    if u % 2 and pair_before(at, u, first):
                        pair_out(*pair_before(at, u, first))
                if last:
                    pair_out(at, NH // 2 - 1)
            each_tile(act, act_tile)

            act.wait_ge(ld_small, 16 * 9)
            act.wait_ge(pool_mm, 2)
            for c in range(2):
                nc.scalar.activation(mixP[:, c, :], PS[6 + c], ACT.Copy, scale=pscale[:, c:c + 1]).then_inc(pool_out, 1)
            for q in range(8):
                act.wait_ge(modb_mm, q + 1)
                nc.scalar.activation(bc[:, 512 * q:512 * q + 512], PS[MODB[q % 4]], ACT.Copy).then_inc(modb_out, 1)

            def hT_copy(t):
                for g in range(2):
                    act.wait_ge(hp_tr, 2 * t + g + 1)
                    nc.scalar.activation(hT[:, 4 * g:4 * g + 4, P * t:P * t + P],
                                         PS[2 + g].rearrange("p (c t) -> p c t", c=4), ACT.Copy).then_inc(hT_out, 1)
            root(bnw[:, 15:16])
            for t in range(NT):
                hT_copy(t)
                if t + 1 < NT:
                    root(bnw[:, 15:16])
            act.wait_ge(log_mm, NT)
            act.wait_ge(kv_row, KT + NT)
            nc.scalar.activation(r_sc, PS[7][:, 0:256], ACT.Sigmoid).then_inc(sc_done, 1)

            def shared_sig(t):
                act.wait_ge(sh_gu, t + 1)
                if t:
                    act.wait_ge(sh_h, t)
                nc.scalar.activation(sg_t, PS[t][:, 0:FF], ACT.Sigmoid).then_inc(sh_sig, 1)

            for t in range(NT):
                shared_sig(t)

            def xT_copy(e, m):
                if is_int(e) and e >= E:
                    return
                if not (is_int(e) and e < 2):
                    act.wait_ge(gu_mm, e - 1)
                for g in range(2):
                    act.wait_ge(x_tr, e + 1)
                    nc.scalar.activation(xT[m % 2][:, 512 * g:512 * g + 512], PS[2 + g], ACT.Copy).then_inc(xT_a, 1)

            xT_copy(0, 0)

            def step(e, m):
                xT_copy(e + 1, m + 1)
                act.wait_ge(gu_mm, e + 1)
                if not (is_int(e) and e == 0):
                    act.wait_ge(h_done, e)
                nc.scalar.activation(sg_t, PS[m % 2][:, 0:FF], ACT.Sigmoid).then_inc(sig_done, 1)
            each_expert(act, step)

            n_over = []
            over_count(act, n_over)

            def over_xT(j):
                act.wait_ge(ov_xtr, j + 1)
                for g in range(2):
                    nc.scalar.activation(xT[0][:, 512 * g:512 * g + 512], PS[2 + g], ACT.Copy).then_inc(ov_xT, 1)

            with act.If(n_over[0] > 0):
                over_xT(0)

            def part(j, i, slot):
                act.wait_ge(ov_gu, j + 1)
                nc.scalar.activation(sg_t, PS[0][:, 0:FF], ACT.Sigmoid).then_inc(ov_sig, 1)
                with act.If(j + 1 < n_over[0]):
                    over_xT(j + 1)
            each_part(act, n_over, part)

            for g in range(NT // 2):
                root(fvar[:, 2 * g:2 * g + 2])
                act.wait_ge(f_in, g + 1)
                for t in (2 * g, 2 * g + 1):
                    nc.scalar.activation(xm[:, D * t:D * t + D], xm[:, D * t:D * t + D], ACT.Identity,
                                         bias=fb[:, 2 * t + 1:2 * t + 2], scale=fb[:, 2 * t:2 * t + 1]).then_inc(f_norm, 1)

        @block.tensor
        def _(pe):
            mm = nc.tensor.matmul
            tr = nc.tensor.transpose
            csv = csil[:, :].rearrange("p (k w) -> p k w", w=2)
            pe.wait_ge(ones_set, 1)
            pe.wait_ge(ld_const, 16)

            def mod_a(k):
                if k == 0:
                    pe.wait_ge(c_silu, 1)
                pe.wait_ge(ld_wa[k % 4], 16 * (k // 4 + 1))
                for q in range(4):
                    last = mm(PS[q][0:2, :], csv[:, k, :], wmod_a[k % 4][:, 512 * q:512 * q + 512], start=(k == 0), stop=(k == DC - 1))
                last.then_inc(moda_mm, 1)

            def x_transposes(g):
                if g >= 4:
                    pe.wait_ge(xtr_out, g - 3)
                for i in range(4):
                    if g < 8:
                        src = xrow[:, i, P * g:P * g + P]
                    else:
                        c = 2 * (g - 8) + i // 2
                        src = crow[:, i % 2, P * c:P * c + P]
                    last = tr(PS[4 + g % 4][:, P * i:P * i + P], src, ident)
                last.then_inc(xtr, 1)

            mod_a(0)
            pe.wait_ge(ld_x, 16)
            for g in range(8):
                x_transposes(g)
            for k in range(1, 4):
                mod_a(k)
            pe.wait_ge(ld_ctx, 16)
            for g in range(8, 12):
                x_transposes(g)
            pe.wait_ge(ld_brow, 16)
            for q in range(4):
                mm(PS[q][0:2, :], ones[0:1, 0:2], brow_a[:, 512 * q:512 * q + 512], start=False, stop=False)
            for k in range(4, DC):
                mod_a(k)
            pe.wait_ge(moda_row, 4)
            pe.wait_ge(xtr_out, 12)
            for i in range(16):
                last = tr(PS[4][:, 2 * i:2 * i + 2], mrow[:, P * i:P * i + P], ident[0:2, 0:2])
            last.then_inc(moda_tr, 1)

            def k_transposes(j):
                pe.wait_ge(kv_row, j + 1)
                if j >= 2:
                    pe.wait_ge(kv_tr_out, j - 1)
                if j < 1:
                    pe.wait_ge(moda_col, 2)
                for h in range(NKV):
                    last = tr(PS[4 + j % 2][:, P * h:P * h + P], st_r[:, P * h:P * h + P], ident)
                last.then_inc(kv_tr, 1)

            def q_transposes(i):
                pe.wait_ge(kv_row, KT + i + 1)
                pe.wait_ge(kv_tr_out, KT + 2 * i)
                for h in range(6):
                    last = tr(PS[4 + h // 3][:, P * (h % 3):P * (h % 3) + P], st_r[:, P * h:P * h + P], ident)
                last.then_inc(kv_tr, 1)

            pe.wait_ge(ld_wkv, 16)
            for j in range(KT):
                if j < 2:
                    pe.wait_ge(moda_row, 4)
                else:
                    pe.wait_ge(kv_v, j - 1)
                    pe.wait_ge(kv_row, j - 1)
                for k in range(DC):
                    if j == 0:
                        pe.wait_ge(xmod, k + 1)
                    if j == NC:
                        pe.wait_ge(xmod, DC + k + 1)
                    lhs = cmT[:, k, P * j:P * j + P] if j < NC else xmT[:, k, P * (j - NC):P * (j - NC) + P]
                    last = mm(PS[j % 2], lhs, win[:, k, 1024:PROJ], start=(k == 0), stop=(k == DC - 1))
                last.then_inc(kv_mm, 1)
                if j:
                    k_transposes(j - 1)
            pe.wait_ge(ld_wqu, 16)
            for i in range(NT):
                if i < 2:
                    pe.wait_ge(kv_v, KT - 1 + i)
                    pe.wait_ge(kv_sq, KT - 1 + i)
                    pe.wait_ge(kv_row, KT - 1 + i)
                else:
                    pe.wait_ge(kv_row, KT + i - 1)
                for k in range(DC):
                    mm(PS[i % 2], xmT[:, k, P * i:P * i + P], win[:, k, 256:768], start=(k == 0), stop=(k == DC - 1))
                for k in range(DC):
                    last = mm(PS[2 + i % 2][:, 0:256], xmT[:, k, P * i:P * i + P], win[:, k, 768:1024], start=(k == 0), stop=(k == DC - 1))
                last.then_inc(kv_mm, 1)
                if i:
                    q_transposes(i - 1)
                else:
                    k_transposes(KT - 1)
            for c in range(2):
                for k in range(DC):
                    last = mm(PS[6 + c], win[:, k, P * c:P * c + P], xmT[:, k, :], start=(k == 0), stop=(k == DC - 1))
                last.then_inc(u_mm, 1)
                if c == 0:
                    q_transposes(NT - 1)
            pe.wait_ge(kv_tr_out, KT + 2 * NT)
            pe.wait_ge(u_out, 2)

            def scores(at, u, first):
                pe.wait_ge(q_cur, NH if first else at(NH, u + 1))
                if not (first and u < 2):
                    pe.wait_ge(exped, at(NH, u - 1))
                for b in range(2):
                    last = mm(PS[2 * (u % 2) + b][:, 0:384], qcur[:, u, :], kT[:, u // GQ, 384 * b:384 * b + 384],
                              start=True, stop=True)
                last.then_inc(scored, 1)

            def pair_transpose(at, pair):
                pe.wait_ge(o_row, at(NH, 2 * pair + 2))
                tr(PS[4][:, 384:512], arow[:, P * pair:P * pair + P], ident).then_inc(atr, 1)

            def prob_transposes(at, u, first):
                pe.wait_ge(exped, at(NH, u + 1))
                for b in range(2):
                    if not (first and u == 0):
                        pe.wait_ge((ptr_a, ptr_b)[b], at(NH, u))
                    if b == 0:
                        if u % 2 == 0 and not (first and u <= 2):
                            pe.wait_ge(atr_out, at(NH // 2, u // 2 - 1))
                        pair = pair_before(at, u, first)
                        if pair:
                            pair_transpose(*pair)
                    for k in range(3):
                        last = tr(PS[4 + b][:, P * k:P * k + P], prob[u % 2][:, P * (3 * b + k):P * (3 * b + k) + P], ident)
                    last.then_inc(ptr, 1)

            def values(at, u, first):
                pe.wait_ge(ptr_a, at(NH, u + 1))
                pe.wait_ge(ptr_b, at(NH, u + 1))
                if not (first and u < 2):
                    pe.wait_ge(o_row, at(NH, u - 1))
                v = HD * (u // GQ)
                for k in range(KT):
                    last = mm(PS[6 + u % 2][:, 0:HD], prT[u % 2][:, k, :], vall[:, k, v:v + HD], start=(k == 0), stop=(k == KT - 1))
                last.then_inc(pv_mm, 1)

            def pe_tile(at, first, last):
                if first:
                    scores(at, 0, True)
                for u in range(NH):
                    if u + 1 < NH:
                        scores(at, u + 1, first)
                    elif not last:
                        scores(Tile(at.i, at.off + 1), 0, False)
                    if u:
                        values(at, u - 1, first)
                    elif not first:
                        values(at.before, NH - 1, False)
                    prob_transposes(at, u, first)
                if last:
                    values(at, NH - 1, False)
                    pe.wait_ge(atr_out, at(NH // 2, NH // 2 - 1))
                    pair_transpose(at, NH // 2 - 1)
            each_tile(pe, pe_tile)
            pe.wait_ge(atr_out, NH // 2 * NT)

            pe.wait_ge(pooled, 1)
            pe.wait_ge(ld_small, 16 * 9)
            for c in range(2):
                mm(PS[6 + c], pw[:, P * c:P * c + P], mixP[:, c, :], start=True, stop=True).then_inc(pool_mm, 1)
            pe.wait_ge(gemv, DC)
            for q in range(8):
                if q == 2:
                    pe.wait_ge(pool_out, 2)
                if q >= 4:
                    pe.wait_ge(modb_out, q - 3)
                mm(PS[MODB[q % 4]], ones[:, :], bc[:, 512 * q:512 * q + 512], start=True, stop=True).then_inc(modb_mm, 1)
            pe.wait_ge(modb_out, 8)

            pe.wait_ge(ld_wout, 16)

            def out_proj(t):
                if t >= 2:
                    pe.wait_ge(mix_read, t - 1)
                b = 4 * (t % 2)
                for q in range(2):
                    for c in range(DC):
                        lhs = mixP[:, c, P * t:P * t + P] if c < 2 else mixA[:, c - 2, P * t:P * t + P]
                        last = mm(PS[b + q], lhs, wout[:, c, 512 * q:512 * q + 512], start=(c == 0), stop=(c == DC - 1))
                last.then_inc(out_mm, 1)

            def h_transposes(t):
                pe.wait_ge(hp_ready, t + 1)
                if t:
                    pe.wait_ge(hT_out, 2 * t)
                for g in range(2):
                    for i in range(4):
                        c = 4 * g + i
                        last = tr(PS[2 + g][:, P * i:P * i + P], hperm[:, P * c:P * c + P], ident)
                    last.then_inc(hp_tr, 1)

            def logits(t):
                pe.wait_ge(hT_out, 2 * t + 2)
                if t == 0:
                    pe.wait_ge(ld_wr, 16)
                for c in range(DC):
                    last = mm(PS[7][:, E * t:E * t + E], hT[:, c, P * t:P * t + P], wrt[:, c, :], start=(c == 0), stop=(c == DC - 1))
                last.then_inc(log_mm, 1)

            def swiglu_in(bank, lhs, w):
                for c in range(DC):
                    last = mm(PS[bank].rearrange("p (u f) -> p u f", u=2), lhs(c), w[:, :, c, :], start=(c == 0), stop=(c == DC - 1))
                return last

            def swiglu_out(lhs, w, bank=4):
                for q in range(2):
                    for c in range(2):
                        last = mm(PS[bank + q], lhs[:, P * c:P * c + P], w[:, c, 512 * q:512 * q + 512], start=(c == 0), stop=(c == 1))
                return last

            def positions():
                pe.wait_ge(masked, 1)
                for t in range(NT):
                    for s in range(t + 1):
                        last = mm(PS[7][:, E * t:E * t + E], con[:, C_UT:C_UT + P] if s == t else ones[:, :],
                                  r_mask[:, E * s:E * s + E], start=(s == 0), stop=(s == t))
                for s in range(NT):
                    last = mm(PS[7][:, 4 * E:5 * E], ones[:, :], r_mask[:, E * s:E * s + E], start=(s == 0), stop=(s == NT - 1))
                last.then_inc(pos_mm, 1)

            def shared_in(t):
                swiglu_in(t, lambda c: hT[:, c, P * t:P * t + P], ws_gu).then_inc(sh_gu, 1)

            def shared_turn(t):
                pe.wait_ge(sh_h, t + 1)
                if t:
                    pe.wait_ge(sh_hT, t)
                for c in range(2):
                    last = tr(PS[6][:, P * c:P * c + P], hrow[t % 2][:, P * c:P * c + P], ident)
                last.then_inc(sh_tr, 1)

            def shared_out(t):
                pe.wait_ge(sh_hT, t + 1)
                if t >= 2:
                    pe.wait_ge(sh_y_read, t - 1)
                swiglu_out(hTe[t % 2], ws_dn, SHY[t % 2]).then_inc(sh_dn, 1)

            def over_rows():
                pe.wait_ge(ov_col, 1)
                pe.wait_ge(posm_done, 1)
                tr(PS[7][0:1, 0:P], ovc[:, 0:1], ident)
                tr(PS[7][0:1, P:2 * P], ovc[:, 1:2], ident).then_inc(ov_tr, 1)

            out_proj(0)
            for t in range(NT):
                if t + 1 < NT:
                    out_proj(t + 1)
                else:
                    pe.wait_ge(ld_ws, 48)
                    pe.wait_ge(mix_read, NT - 1)
                    shared_in(0)
                h_transposes(t)
                logits(t)
            shared_in(1)
            pe.wait_ge(hT_out, 2 * NT)
            pe.wait_ge(mix_read, NT)
            shared_in(2)
            positions()
            shared_in(3)
            shared_turn(0)
            over_rows()

            n_over = []

            def over_info(ex):
                for t in range(NT):
                    last = mm(PS[7][:, 0:6], selm[:, t, :], info[:, t, bass.ds(ex * 6, 6)], start=(t == 0), stop=(t == NT - 1))
                last.then_inc(ov_info, 1)

            def list_info(e, m):
                if is_int(e) and e >= E:
                    return
                pe.wait_ge(sel_done, e + 1)
                if not (is_int(e) and e == 0):
                    pe.wait_ge(idx_done, e)
                for t in range(NT):
                    last = mm(PS[7][:, 0:6], selm[:, t, :], info[:, t, bass.ds(e * 6, 6)], start=(t == 0), stop=(t == NT - 1))
                last.then_inc(info_mm, 1)

            def row_transposes(e, m):
                if is_int(e) and e >= E:
                    return
                pe.wait_ge(gathered[m % 4], slot_count(e, m, 16))
                if not (is_int(e) and e == 0):
                    pe.wait_ge(xT_a, e * 2)
                for c in range(DC):
                    last = tr(PS[2 + c // 4][:, P * (c % 4):P * (c % 4) + P], xg[m % 4][:, P * c:P * c + P], ident)
                last.then_inc(x_tr, 1)

            def slot_count(e, m, per):
                return (e - m % 4) * (per // 4) + per

            def hidden_transposes(e, m):
                pe.wait_ge(h_done, e + 1)
                if not (is_int(e) and e == 0):
                    pe.wait_ge(h_out, e)
                for c in range(2):
                    last = tr(PS[6][:, P * c:P * c + P], hrow[m % 2][:, P * c:P * c + P], ident)
                last.then_inc(h_tr, 1)

            def down(e, m):
                pe.wait_ge(h_out, e + 1)
                if not (is_int(e) and e == 0):
                    pe.wait_ge(y_out, e)
                pe.wait_ge(ld_dn[m % 2], (e * 8 + (16 if m % 2 == 0 else 8)))
                swiglu_out(hTe[m % 2], dn_w[m % 2]).then_inc(dn_mm, 1)

            for t in range(NT):
                if t + 1 < NT:
                    shared_turn(t + 1)
                shared_out(t)
                if t == 0:
                    pe.wait_ge(ov_done, 1)
                if t < 3:
                    list_info(t, t)
            pe.wait_ge(sh_y_read, NT)
            row_transposes(0, 0)

            def step(e, m):
                row_transposes(e + 1, m + 1)
                if not (is_int(e) and e == 0):
                    hidden_transposes(e - 1, m + 3)
                pe.wait_ge(xT_a, e * 2 + 2)
                pe.wait_ge(ld_gu[(m + 1) % 4], slot_count(e, m, 32))
                if not (is_int(e) and e < 2):
                    pe.wait_ge(h_done, e - 1)
                swiglu_in(m % 2, lambda c: xT[m % 2][:, P * c:P * c + P], gu_w[(m + 1) % 4]).then_inc(gu_mm, 1)
                list_info(e + 3, m + 3)
                if is_int(e) and e == E - 2:
                    with pe.If(n_over[0] > 0):
                        ex = pe.value_load(ovcode[0:1, 0:1], min_val=0, max_val=E - 1)
                        pe.wait_ge(ov_sel, 1)
                        pe.wait_ge(idx_done, E)
                        over_info(ex)
                if not (is_int(e) and e == 0):
                    down(e - 1, m + 3)
            each_expert(pe, step, lambda: over_count(pe, n_over))
            hidden_transposes(E - 1, (E - 1) % 4)
            down(E - 1, (E - 1) % 4)

            pe.wait_ge(y_out, E)
            def over_x(j):
                pe.wait_ge(ov_gat, j * 16 + 16)
                for c in range(DC):
                    last = tr(PS[2 + c // 4][:, P * (c % 4):P * (c % 4) + P], xg[0][:, P * c:P * c + P], ident)
                last.then_inc(ov_xtr, 1)

            with pe.If(n_over[0] > 0):
                over_x(0)

            def part(j, i, slot):
                with pe.If(j + 1 < n_over[0]):
                    ex = pe.value_load(ovcode[0:1, bass.ds(j + 1, 1)], min_val=0, max_val=E - 1)
                    pe.wait_ge(ov_sel, j + 2)
                    pe.wait_ge(ov_idx, j + 1)
                    over_info(ex)
                pe.wait_ge(ov_xT, 2 * j + 2)
                pe.wait_ge(ov_w[slot], i * 32 + 32)
                swiglu_in(0, lambda c: xT[0][:, P * c:P * c + P], gu_w[1 + slot]).then_inc(ov_gu, 1)
                with pe.If(j + 1 < n_over[0]):
                    over_x(j + 1)
                pe.wait_ge(ov_h, j + 1)
                for c in range(2):
                    last = tr(PS[6][:, P * c:P * c + P], hrow[0][:, P * c:P * c + P], ident)
                last.then_inc(ov_htr, 1)
                pe.wait_ge(ov_hT, j + 1)
                pe.wait_ge(ov_wd[slot], i * 16 + 16)
                pe.wait_ge(ov_y, j + 1)
                swiglu_out(hTe[0], dn_w[slot]).then_inc(ov_dn, 1)
            each_part(pe, n_over, part)

        @block.vector
        def _(dve):
            V = nc.vector
            n = [0]

            def link(ins, count=1):
                n[0] += count
                ins.then_inc(dve_c, 1)
                dve.wait_ge(dve_c, n[0])

            csv = csil[:, :].rearrange("p (k w) -> p w k", w=2)
            dve.wait_ge(c_sigmoid, 1)
            V.tensor_tensor(csv, cvec[:, :].rearrange("p (w k) -> p w k", w=2), csig[:, :].rearrange("p (w k) -> p w k", w=2),
                            ALU.mult).then_inc(c_silu, 1)
            dve.wait_ge(ld_temp, 16)
            dve.wait_ge(ld_small, 16 * 9)
            cosv = lnr[:, T_COS:T_COS + 256].rearrange("p (t i w) -> p t i w", t=NT, w=2)
            sinv = lnr[:, T_SIN:T_SIN + 256].rearrange("p (t i w) -> p t i w", t=NT, w=2)
            for s in range(2):
                g = gains[:, HD * s:HD * s + HD].rearrange("p (o i w) -> p o i w", o=1, w=2)
                sc = HD ** -0.5 if s == 0 else 1.0
                for o in range(2):
                    tv = tabs[:, 512 * s + 256 * o:512 * s + 256 * o + 256].rearrange("p (t i w) -> p t i w", t=NT, w=2)
                    src = sinv if o else cosv
                    for w in range(2):
                        gw = g[:, :, :, (w + o) % 2].to_broadcast([P, NT, HD // 2])
                        V.scalar_tensor_tensor(tv[:, :, :, w], src[:, :, :, w], sc, gw, ALU.mult, ALU.mult).then_inc(tab_done, 1)
            dve.wait_ge(moda_mm, DC)
            for q in range(2):
                V.tensor_copy(mrow[:, 512 * q:512 * q + 512], PS[q][0:2, :]).then_inc(moda_row, 1)
            dve.wait_ge(moda_tr, 1)
            V.tensor_copy(modc[:, 0:16], PS[4][:, 0:16]).then_inc(moda_col, 1)
            V.tensor_scalar(modc[:, 16:32], PS[4][:, 16:32], 1.0, None, ALU.add).then_inc(moda_col, 1)
            dve.wait_ge(moda_col, 2)
            mc = modc[:, :].rearrange("p (s k w) -> p s k w", s=2, w=2)
            for k in range(DC):
                V.tensor_scalar(cmT[:, k, :], cmT[:, k, :], mc[:, 1, k, 1:2], mc[:, 0, k, 1:2], ALU.mult, ALU.add).then_inc(xmod, 1)
            for k in range(DC):
                V.tensor_scalar(xmT[:, k, :], xmT[:, k, :], mc[:, 1, k, 0:1], mc[:, 0, k, 0:1], ALU.mult, ALU.add).then_inc(xmod, 1)
            dve.wait_ge(tab_done, 8)

            norms = [0]

            def rstd(heads):
                ss, ms, rs = stat[:, 0:heads], stat[:, 12:12 + heads], stat[:, 24:24 + heads]
                link(V.tensor_reduce(ss, st_q[:, 0:HD * heads].rearrange("p (h d) -> p h d", d=HD), AX, ALU.add))
                V.tensor_scalar(ms, ss, 1.0 / HD, RMS_EPS, ALU.mult, ALU.add).then_inc(var_in, 1)
                norms[0] += 1
                dve.wait_ge(root_out, norms[0])
                link(V.reciprocal(rs, ms))
                return rs

            def rotate(heads, s, t):
                nv = st_n[:, 0:HD * heads].rearrange("p (h i w) -> p h i w", h=heads, w=2)
                bv = st_b[:, 0:HD * heads].rearrange("p (h i w) -> p h i w", h=heads, w=2)
                C = tabs[:, 512 * s + HD * t:512 * s + HD * t + HD]
                S = tabs[:, 512 * s + 256 + HD * t:512 * s + 256 + HD * t + HD].rearrange("p (o i w) -> p o i w", o=1, w=2)
                V.tensor_tensor(st_a[:, 0:HD * heads].rearrange("p (h d) -> p h d", h=heads), st_n[:, 0:HD * heads].rearrange("p (h d) -> p h d", h=heads),
                                C.rearrange("p (o d) -> p o d", o=1).to_broadcast([P, heads, HD]), ALU.mult).then_inc(dve_c, 1)
                for w in range(2):
                    V.tensor_tensor(bv[:, :, :, w], nv[:, :, :, 1 - w], S[:, :, :, w].to_broadcast([P, heads, HD // 2]),
                                    ALU.mult).then_inc(dve_c, 1)
                n[0] += 3
                dve.wait_ge(dve_c, n[0])

            for j in range(KT):
                dve.wait_ge(kv_sq, j + 1)
                rs = rstd(NKV)
                dup = st_r[:, 0:512].rearrange("p (h r d) -> p h r d", h=NKV, r=2)
                link(V.tensor_tensor(st_n[:, 0:KW].rearrange("p (h d) -> p h d", h=NKV), PS[j % 2][:, 0:KW].rearrange("p (h d) -> p h d", h=NKV),
                                     rs.rearrange("p (h o) -> p h o", o=1).to_broadcast([P, NKV, HD]), ALU.mult))
                if j:
                    dve.wait_ge(kv_tr, j)
                if j < NC:
                    for r in range(2):
                        last = V.tensor_tensor(dup[:, :, r, :], st_n[:, 0:KW].rearrange("p (h d) -> p h d", h=NKV),
                                               gains[:, HD:2 * HD].rearrange("p (o d) -> p o d", o=1).to_broadcast([P, NKV, HD]), ALU.mult)
                        if r == 0:
                            last.then_inc(dve_c, 1)
                            n[0] += 1
                    last.then_inc(kv_row, 1)
                else:
                    rotate(NKV, 1, j - NC)
                    for r in range(2):
                        last = V.tensor_tensor(dup[:, :, r, :], st_a[:, 0:KW].rearrange("p (h d) -> p h d", h=NKV),
                                               st_b[:, 0:KW].rearrange("p (h d) -> p h d", h=NKV), ALU.add)
                        if r == 0:
                            last.then_inc(dve_c, 1)
                            n[0] += 1
                    last.then_inc(kv_row, 1)
                dve.wait_ge(kv_row, j + 1)
                dve.wait_ge(dve_c, n[0])
            dve.wait_ge(xtr_out, 12)
            V.memset(pU[:, :, 0:PAD], 0.0).then_inc(u_pad, 1)
            V.memset(pU[:, :, PAD + SEQ:UP], 0.0).then_inc(u_pad, 1)
            dve.wait_ge(kv_mm, NC)
            V.memset(qcur, 0.0).then_inc(q_zero, 1)
            for i in range(NT):
                dve.wait_ge(kv_sq, KT + i + 1)
                dve.wait_ge(kv_v, KT + i + 1)
                rb = rstd(NH).rearrange("p (h o) -> p h o", o=1)
                link(V.tensor_tensor(st_n[:, 0:512].rearrange("p (h d) -> p h d", h=8), PS[i % 2].rearrange("p (h d) -> p h d", h=8),
                                     rb[:, 0:8, :].to_broadcast([P, 8, HD]), ALU.mult))
                link(V.tensor_tensor(st_n[:, 512:768].rearrange("p (h d) -> p h d", h=4), PS[2 + i % 2][:, 0:256].rearrange("p (h d) -> p h d", h=4),
                                     rb[:, 8:12, :].to_broadcast([P, 4, HD]), ALU.mult))
                rotate(NH, 0, i)
                dve.wait_ge(kv_tr, KT + i)
                V.tensor_tensor(st_r, st_a, st_b, ALU.add).then_inc(kv_row, 1)
                dve.wait_ge(kv_row, KT + i + 1)

            dve.wait_ge(kv_tr_out, KT + 2 * NT)
            for r in range(2):
                dve.wait_ge(q_zero, 1)
                V.tensor_copy(qcur[HD * r:HD * r + HD].rearrange("p (h r) t -> p r h t", r=2)[:, r], qT[HD * r:HD * r + HD, :, 0:P]).then_inc(q_cur, NH // 2)

            def row_max(at, u, first):
                dve.wait_ge(scored, at(NH, u + 1))
                if not (first and u < 2):
                    dve.wait_ge(exped, at(NH, u - 1))
                w = u % 2
                V.tensor_reduce(negmax[:, w:w + 1], PS3[:, 2 * w:2 * w + 2, 0:384], mybir.AxisListType.XY, ALU.max,
                                negate=True).then_inc(maxed, 1)

            def out_row(at, u, first):
                w = u % 2
                dve.wait_ge(pv_mm, at(NH, u + 1))
                V.reciprocal(recips[:, w:w + 1], rowsum[:, w:w + 1]).then_inc(att_c, 1)
                dve.wait_ge(att_c, at(NH, u + 1))
                if not first:
                    dve.wait_ge(atr, at(NH // 2, u // 2 + 1 - NH // 2))
                V.tensor_scalar(arow[:, HD * u:HD * u + HD], PS[6 + w][:, 0:HD], recips[:, w:w + 1], None, ALU.mult).then_inc(o_row, 1)

            def half_b(at, u, first):
                dve.wait_ge(ptr, at(2 * NH, 2 * u + 2))
                if not (first and u < 2):
                    dve.wait_ge(pv_mm, at(NH, u - 1))
                V.tensor_copy(prT[u % 2][:, 3:6, :], PS[5][:, 0:384].rearrange("p (k q) -> p k q", k=3)).then_inc(ptr_b, 1)

            def dve_tile(at, first, last):
                if first:
                    row_max(at, 0, True)
                for u in range(NH):
                    if u + 1 < NH:
                        row_max(at, u + 1, first)
                    elif not last:
                        row_max(Tile(at.i, at.off + 1), 0, False)
                    if u:
                        out_row(at, u - 1, first)
                    elif not first:
                        out_row(at.before, NH - 1, False)
                    half_b(at, u, first)
                if last:
                    out_row(at, NH - 1, False)
            each_tile(dve, dve_tile)

            dve.wait_ge(modb_out, 8)
            g1, sh2, sc2, g2 = (bc[:, D * i:D * i + D] for i in range(4))
            g2v = g2.rearrange("p (b n) -> p b n", b=2)
            link(V.tensor_scalar(sc2, sc2, 1.0, None, ALU.add))
            dve.wait_ge(ld_x2, 16)
            dve.wait_ge(ld_ln1, 32)

            def norm_stats(row):
                for h in range(2):
                    V.bn_stats(bnw[:, 6 * h:6 * h + 6], row[:, 512 * h:512 * h + 512]).then_inc(dve_c, 1)
                n[0] += 2
                dve.wait_ge(dve_c, n[0])
                link(V.bn_aggr(bnw[:, 12:14], bnw[:, 0:12].rearrange("p (c s) -> p c s", c=2)))
                V.tensor_scalar(bnw[:, 15:16], bnw[:, 13:14], LN_EPS, None, ALU.add).then_inc(var_in, 1)
                norms[0] += 1
                dve.wait_ge(root_out, norms[0])
                link(V.reciprocal(bnw[:, 14:15], bnw[:, 15:16]))

            for t in range(NT):
                xr = xrow[:, t, :]
                b = 4 * (t % 2)
                dve.wait_ge(out_mm, t + 1)
                if t:
                    dve.wait_ge(hp_ready, t)
                V.tensor_tensor(lnA.rearrange("p (b n) -> p b n", b=2), PS3[:, b:b + 2, :], g1.rearrange("p (b n) -> p b n", b=2),
                                ALU.mult).then_inc(mix_read, 1)
                dve.wait_ge(mix_read, t + 1)
                link(V.scalar_tensor_tensor(xr, xr, ALPHA, lnA, ALU.mult, ALU.add))
                norm_stats(xr)
                link(V.tensor_scalar(xr, xr, bnw[:, 12:13], bnw[:, 14:15], ALU.subtract, ALU.mult))
                link(V.tensor_tensor(xr, xr, lnr[:, 0:D], ALU.mult))
                link(V.tensor_tensor(xr, xr, lnr[:, D:2 * D], ALU.add))
                link(V.tensor_tensor(lnA, xr, sc2, ALU.mult))
                if t:
                    dve.wait_ge(hp_tr, 2 * t)
                    dve.wait_ge(h_stored, 16 * t)
                V.tensor_tensor(hperm.rearrange("p (c q) -> p q c", c=DC), lnA.rearrange("p (q c) -> p q c", c=DC),
                                sh2.rearrange("p (q c) -> p q c", c=DC), ALU.add).then_inc(hp_ready, 1)
            sel3 = r_sel.rearrange("p (t g m) -> p t g m", t=NT, g=NG)
            dve.wait_ge(sc_done, 1)
            dve.wait_ge(ld_small, 16 * 9)
            link(V.tensor_tensor(r_sel.rearrange("p (t e) -> p t e", t=NT), r_sc.rearrange("p (t e) -> p t e", t=NT),
                                 rbias[:, :].rearrange("p (o e) -> p o e", o=1).to_broadcast([P, NT, E]), ALU.add))
            for t in range(NT):
                for g in range(NG):
                    last = V.max(g8[:, t, g, :], sel3[:, t, g, :])
            link(last)
            link(V.memset(gs16[:, :, NG:2 * NG], -BIG))
            link(V.tensor_tensor(gs16[:, :, 0:NG], g8[:, :, :, 0], g8[:, :, :, 1], ALU.add))
            for t in range(NT):
                last = V.max(gtop[:, t, :], gs16[:, t, :])
            link(last)
            link(V.memset(gtop[:, :, TG:8], -BIG))
            for t in range(NT):
                last = V.match_replace(gmk[:, t, :], gtop[:, t, :], gs16[:, t, :], MARK)
            link(last)
            link(V.tensor_scalar(gs16[:, :, 0:NG], gmk[:, :, 0:NG], MARK / 3, -BIG, ALU.is_lt, ALU.mult))
            link(V.tensor_tensor(sel3, sel3, gs16[:, :, 0:NG].rearrange("p t (g o) -> p t g o", o=1).to_broadcast([P, NT, NG, GE]), ALU.add))
            for t in range(NT):
                last = V.max(gtop[:, t, :], r_sel[:, E * t:E * t + E])
            link(last)
            for t in range(NT):
                last = V.match_replace(r_mask[:, E * t:E * t + E], gtop[:, t, :], r_sel[:, E * t:E * t + E], MARK)
            link(last)
            V.tensor_scalar(r_mask, r_mask, MARK / 3, None, ALU.is_ge).then_inc(masked, 1)
            dve.wait_ge(masked, 1)
            link(V.tensor_tensor(r_sel, r_sc, r_mask, ALU.mult))
            link(V.tensor_reduce(rsm[:, 0:4], r_sel.rearrange("p (t e) -> p t e", t=NT), AX, ALU.add))
            link(V.reciprocal(rsm[:, 4:8], rsm[:, 0:4]))
            link(V.tensor_scalar(rsm[:, 8:12], rsm[:, 4:8], RSCALE, None, ALU.mult))
            link(V.tensor_tensor(r_sel.rearrange("p (t e) -> p t e", t=NT), r_sel.rearrange("p (t e) -> p t e", t=NT),
                                 rsm[:, 8:12].rearrange("p (t o) -> p t o", o=1).to_broadcast([P, NT, E]), ALU.mult))
            inf = info.rearrange("p t (e w c) -> p t e w c", w=2, c=3)
            toks = con[:, C_IDM:C_IDM + NT].rearrange("p (t o) -> p t o", o=1)
            wgt = r_sel.rearrange("p (t e) -> p t e", t=NT)
            tokr = rsm[:, 0:4].rearrange("p (t o) -> p t o", o=1)
            link(V.tensor_copy(inf[:, :, :, 0, 0], toks.to_broadcast([P, NT, E])))
            V.tensor_copy(inf[:, :, :, 1, 0], wgt).then_inc(dve_c, 1)
            V.memset(inf[:, :, :, 0, 2], 0.0).then_inc(dve_c, 1)
            link(V.tensor_tensor(tokr, toks, inf[:, :, 0:1, 0, 0], ALU.subtract), 3)
            V.tensor_copy(inf[:, :, :, 0, 1], tokr.to_broadcast([P, NT, E])).then_inc(dve_c, 1)
            link(V.tensor_tensor(wgt, wgt, inf[:, :, :, 1, 0], ALU.subtract), 2)
            link(V.tensor_copy(inf[:, :, :, 1, 1], wgt))
            link(V.tensor_tensor(wgt, wgt, inf[:, :, :, 1, 1], ALU.subtract))
            link(V.tensor_copy(inf[:, :, :, 1, 2], wgt))

            def times_up(row, ps):
                return V.tensor_tensor(row.rearrange("p (c q) -> p q c", c=2), gw_t.rearrange("p (q c) -> p q c", c=2),
                                       ps[:, FF:2 * FF].rearrange("p (q c) -> p q c", c=2), ALU.mult)

            def shared_hidden(t):
                dve.wait_ge(sh_gu, t + 1)
                dve.wait_ge(sh_sig, t + 1)
                link(V.tensor_tensor(gw_t, PS[t][:, 0:FF], sg_t, ALU.mult))
                times_up(hrow[t % 2], PS[t]).then_inc(sh_h, 1)

            def shared_hT(t):
                dve.wait_ge(sh_tr, t + 1)
                V.tensor_copy(hTe[t % 2], PS[6][:, 0:FF]).then_inc(sh_hT, 1)

            def shared_y(t):
                dve.wait_ge(sh_dn, t + 1)
                if t >= 2:
                    dve.wait_ge(sh_st[t % 2], 16 * (t // 2))
                y2 = ysb[t % 2].rearrange("p (b n) -> p b n", b=2)
                V.tensor_tensor(y2, PS3[:, SHY[t % 2]:SHY[t % 2] + 2, :], g2v, ALU.mult).then_inc(sh_y_read, 1)
                dve.wait_ge(sh_y_read, t + 1)
                V.scalar_tensor_tensor(ysb[t % 2], xrow[:, t, :], ALPHA, ysb[t % 2], ALU.mult, ALU.add).then_inc(sh_y, 1)

            shared_hidden(0)
            shared_hidden(1)
            dve.wait_ge(pos_mm, 1)
            V.scalar_tensor_tensor(posm, PS[7][:, 0:NT * E], 1.0, r_mask, ALU.add, ALU.mult).then_inc(posm_done, 1)
            cnt = PS[7][:, NT * E:NT * E + E]
            nb, cum, cmp, cmn = gsb[:, 0:E], r_sel[:, 0:E], r_sel[:, E:2 * E], r_sel[:, 2 * E:3 * E]
            link(V.tensor_scalar(nb, cnt, P + 0.5, None, ALU.is_gt))
            link(V.scalar_tensor_tensor(nb, cnt, 2 * P + 0.5, nb, ALU.is_gt, ALU.add))
            link(V.scalar_tensor_tensor(nb, cnt, 3 * P + 0.5, nb, ALU.is_gt, ALU.add))
            link(V.tensor_tensor_scan(cum, nb, nb, 0.0, ALU.add, ALU.max))
            link(V.tensor_scalar(cmp, cum, con[:, C_SLOT:C_SLOT + 1], None, ALU.is_le))
            link(V.tensor_reduce(ovc[:, 0:1], cmp, AX, ALU.add))
            link(V.tensor_tensor(cmn, cmp, nb, ALU.mult))
            link(V.tensor_reduce(ovc[:, 2:3], cmn, AX, ALU.add))
            link(V.tensor_copy(ovcode[0:1, 2 * OV:2 * OV + 1], cum[0:1, E - 1:E]))
            link(V.tensor_scalar(ovc[:, 3:4], ovc[:, 2:3], -1.0, 1.0, ALU.mult, ALU.add))
            V.tensor_tensor(ovc[:, 1:2], ovc[:, 3:4], con[:, C_SLOT:C_SLOT + 1], ALU.add).then_inc(ov_col, 1)

            list_sums = PS[7][:, 0:6].rearrange("p (w c) -> p w c", w=2)

            def select(e, m):
                if is_int(e) and e >= E:
                    return
                if not (is_int(e) and e == 0):
                    dve.wait_ge(info_mm, e)
                for t in range(NT):
                    last = V.tensor_scalar(selm[:, t, :], con[:, C_IOTA:C_IOTA + P], posm[:, bass.ds(e + t * E, 1)], None, ALU.is_equal)
                last.then_inc(sel_done, 1)

            def indices(e, m):
                if is_int(e) and e >= E:
                    return
                m = m % 4
                dve.wait_ge(info_mm, e + 1)
                V.tensor_reduce(iw[:, 2 * m:2 * m + 2], list_sums, AX, ALU.add).then_inc(iw_c, 1)
                dve.wait_ge(iw_c, e + 1)
                V.tensor_scalar(gidx[:, m:m + 1], iw[:, 2 * m:2 * m + 1], float(SEQ), None, ALU.add).then_inc(idx_done, 1)

            def hidden(e, m):
                dve.wait_ge(gu_mm, e + 1)
                dve.wait_ge(sig_done, e + 1)
                V.scalar_tensor_tensor(gw_t, PS[m % 2][:, 0:FF], iw[:, 2 * m + 1:2 * m + 2], sg_t, ALU.mult, ALU.mult).then_inc(hid_c, 1)
                dve.wait_ge(hid_c, e + 1)
                times_up(hrow[m % 2], PS[m % 2]).then_inc(h_done, 1)

            def hidden_T(e, m):
                dve.wait_ge(h_tr, e + 1)
                V.tensor_copy(hTe[m % 2], PS[6][:, 0:FF]).then_inc(h_out, 1)

            def places(e, m):
                m = m % 4
                if not (is_int(e) and e < 2):
                    dve.wait_ge(scattered, e * 16 - 16)
                V.tensor_scalar(tcol[:, m % 2:m % 2 + 1], iw[:, 2 * m:2 * m + 1], 0.0, con[:, C_SLOT:C_SLOT + 1], ALU.is_ge, ALU.mult).then_inc(sid_c, 1)
                dve.wait_ge(sid_c, e * 2 + 1)
                V.scalar_tensor_tensor(sidx[:, m % 2:m % 2 + 1], iw[:, 2 * m:2 * m + 1], float(SEQ), tcol[:, m % 2:m % 2 + 1], ALU.add, ALU.add).then_inc(sid_c, 1)
                dve.wait_ge(sid_c, e * 2 + 2)

            def rows_out(e, m):
                if is_int(e) and e < 2:
                    for w in (*sh_st, sh_pad):
                        dve.wait_ge(w, 16 if w is sh_pad else 8 * NT)
                dve.wait_ge(dn_mm, e + 1)
                V.tensor_tensor(ysb[m % 2].rearrange("p (b n) -> p b n", b=2), PS3[:, 4:6, :], g2v, ALU.mult).then_inc(y_out, 1)

            shared_hT(0)
            shared_hidden(2)
            dve.wait_ge(ov_tr, 1)
            V.tensor_copy(ovcode[0:1, 0:2 * OV].rearrange("o (a b) -> o a b", a=2),
                          PS[7][0:1, 0:2 * P].rearrange("o (a b) -> o a b", a=2)[:, :, 0:OV]).then_inc(ov_done, 1)
            select(0, 0)
            for t in range(NT):
                if t + 1 < NT:
                    shared_hT(t + 1)
                if t == 0:
                    shared_hidden(3)
                shared_y(t)
                if t < 3:
                    indices(t, t)
                if t < 2:
                    select(t + 1, t + 1)

            n_over = []

            def over_select(k):
                ex = dve.value_load(ovcode[0:1, bass.ds(k, 1)], min_val=0, max_val=E - 1)
                part = dve.value_load(ovcode[0:1, bass.ds(k + OV, 1)], min_val=1, max_val=SEQ // P - 1)
                for t in range(NT):
                    last = V.tensor_scalar(selm[:, t, :], con[:, bass.ds(part * P + C_IOTA, P)], posm[:, bass.ds(ex + t * E, 1)], None, ALU.is_equal)
                last.then_inc(ov_sel, 1)

            def over_indices(k):
                V.tensor_reduce(iw[:, 0:2], list_sums, AX, ALU.add).then_inc(iw_c, 1)
                dve.wait_ge(iw_c, k + (E + 1))
                V.tensor_scalar(gidx[:, 0:1], iw[:, 0:1], float(SEQ), None, ALU.add).then_inc(ov_idx, 1)

            def step(e, m):
                if not (is_int(e) and e == 0):
                    hidden_T(e - 1, m + 3)
                select(e + 3, m + 3)
                if not (is_int(e) and e == 0):
                    places(e - 1, m + 3)
                if is_int(e) and e == E - 3:
                    with dve.If(n_over[0] > 0):
                        over_select(0)
                if is_int(e) and e == E - 1:
                    with dve.If(n_over[0] > 1):
                        over_select(1)
                hidden(e, m)
                indices(e + 3, m + 3)
                if is_int(e) and e == E - 2:
                    with dve.If(n_over[0] > 0):
                        dve.wait_ge(ov_info, 1)
                        over_indices(0)
                if not (is_int(e) and e == 0):
                    rows_out(e - 1, m + 3)
            each_expert(dve, step, lambda: over_count(dve, n_over))
            hidden_T(E - 1, (E - 1) % 4)
            places(E - 1, (E - 1) % 4)
            rows_out(E - 1, (E - 1) % 4)


            over_w = iw[:, 3:4]
            over_i = iw[:, 2:3]
            def part(j, i, slot):
                dve.wait_ge(ov_idx, j + 1)
                V.tensor_copy(iw[:, 2:4], iw[:, 0:2]).then_inc(ovd_c, 1)
                with dve.If(j + 1 < n_over[0]):
                    dve.wait_ge(ov_xtr, j + 1)
                    dve.wait_ge(ovd_c, j * 4 + 1)
                    dve.wait_ge(ov_info, j + 2)
                    over_indices(j + 1)
                dve.wait_ge(ovd_c, j * 4 + 1)
                dve.wait_ge(ov_gu, j + 1)
                dve.wait_ge(ov_sig, j + 1)
                V.scalar_tensor_tensor(gw_t, PS[0][:, 0:FF], over_w, sg_t, ALU.mult, ALU.mult).then_inc(ovd_c, 1)
                dve.wait_ge(ovd_c, j * 4 + 2)
                times_up(hrow[0], PS[0]).then_inc(ov_h, 1)
                dve.wait_ge(ov_htr, j + 1)
                V.tensor_copy(hTe[0], PS[6][:, 0:FF]).then_inc(ov_hT, 1)
                with dve.If(j + 2 < n_over[0]):
                    over_select(j + 2)
                dve.wait_ge(ov_turn, j + 1)
                V.tensor_scalar(tcol[:, 0:1], over_i, 0.0, con[:, C_SLOT:C_SLOT + 1], ALU.is_ge, ALU.mult).then_inc(ovd_c, 1)
                dve.wait_ge(ovd_c, j * 4 + 3)
                V.scalar_tensor_tensor(sidx[:, 0:1], over_i, float(SEQ), tcol[:, 0:1], ALU.add, ALU.add).then_inc(ovd_c, 1)
                dve.wait_ge(ovd_c, j * 4 + 4)
                dve.wait_ge(ov_dn, j + 1)
                V.tensor_tensor(ysb[0].rearrange("p (b n) -> p b n", b=2), PS3[:, 4:6, :], g2v, ALU.mult).then_inc(ov_y, 1)
            each_part(dve, n_over, part)

            mv3 = fmv[:, :].rearrange("p (t w) -> p t w", t=NT)
            fb3 = fb[:, :].rearrange("p (t w) -> p t w", t=NT)

            def final_stats(g):
                ts = (2 * g, 2 * g + 1)
                for t in ts:
                    dve.wait_ge(f_acc[t], 16)
                    for h in range(2):
                        last = V.bn_stats(fbn[:, 12 * t + 6 * h:12 * t + 6 * h + 6], xm[:, D * t + 512 * h:D * t + 512 * h + 512])
                link(last)
                for t in ts:
                    last = V.bn_aggr(fmv[:, 2 * t:2 * t + 2], fbn[:, 12 * t:12 * t + 12].rearrange("p (c s) -> p c s", c=2))
                link(last)
                V.tensor_scalar(fvar[:, ts[0]:ts[1] + 1], mv3[:, ts[0]:ts[1] + 1, 1], LN_EPS, None, ALU.add).then_inc(var_in, 1)
                norms[0] += 1
                dve.wait_ge(root_out, norms[0])
                link(V.reciprocal(fb3[:, ts[0]:ts[1] + 1, 0], fvar[:, ts[0]:ts[1] + 1]))
                V.scalar_tensor_tensor(fb3[:, ts[0]:ts[1] + 1, 1], mv3[:, ts[0]:ts[1] + 1, 0], -1.0, fb3[:, ts[0]:ts[1] + 1, 0],
                                       ALU.mult, ALU.mult).then_inc(f_in, 1)

            def final_out(t):
                z = xm[:, D * t:D * t + D]
                if t % 2:
                    dve.wait_ge(f_mul, t // 2 + 1)
                else:
                    dve.wait_ge(f_norm, t + 1)
                    link(V.tensor_tensor(z, z, ln2[:, 0:D], ALU.mult))
                V.tensor_tensor(z, z, ln2[:, D:2 * D], ALU.add).then_inc(f_out, 1)

            dve.wait_ge(ld_ln2, 32)
            for g in range(NT // 2):
                final_stats(g)
            for t in range(NT):
                final_out(t)


_INS = ['x', 'c', 'ctx', 'c_ctx', 'w_mod', 'b_mod', 'w_in', 'q_norm', 'k_norm', 'pool_w', 'pool_scale', 'w_out',
        'ln1_g', 'ln1_b', 'w_router', 'router_bias', 'w_gate', 'w_up', 'w_down', 'ws_gate', 'ws_up', 'ws_down',
        'ln2_g', 'ln2_b']


def kernel(**inputs):
    import concourse.bacc as _bacc
    from concourse.bass_utils import run_bass_kernel_spmd as _run

    nc = _bacc.Bacc("TRN2", target_bir_lowering=False, num_devices=1)
    arrays, args = {}, {}
    fixed, temp = constants()
    for name, v in [(k, np.ascontiguousarray(inputs[k])) for k in _INS] + [("consts", fixed), ("tempc", temp)]:
        arrays[f"in_{name}_dram"] = v
        args[name] = nc.dram_tensor(f"in_{name}_dram", v.shape, mybir.dt.from_np(v.dtype), kind="ExternalInput").ap()
    out = nc.dram_tensor("out_0_dram", (1, SEQ, D), F32, kind="ExternalOutput").ap()
    build(nc, args, args["consts"], args["tempc"], out)
    r = _run(nc, [arrays], core_ids=[0])
    return r.results[0]["out_0_dram"]
```
